# Optimizing a Trainium2 kernel written in Bass

```python
import jax, jax.numpy as jnp
from jax import lax
import numpy as np
import math

D_MODEL = 1024
BATCH = 1
SEQ = 512
DEPTH = 1

PLE_DIM = 256
EPS = 1e-6
NEG = -1e30

GDN_HEADS = 4
GDN_DK = 128
GDN_DV = 128
GDN_CONV = 4
GDN_CHUNK = 64

NSA_HEADS = 8
NSA_GROUPS = 2
NSA_HPG = NSA_HEADS // NSA_GROUPS
NSA_DK = 64
NSA_DV = 64
CMP_LEN = 32
CMP_STRIDE = 16
CMP_HIDDEN = 256
SEL_BLOCK = 64
SEL_TOPN = 16
SEL_QCHUNK = 64
WINDOW = 512
WIN_QBLOCK = 128
FORCED_SCORE = 1e9

D_FF = 2816
FFN_CONV = 3

IN_SPLITS = (
    GDN_HEADS * GDN_DK,
    GDN_HEADS * GDN_DK,
    GDN_HEADS * GDN_DV,
    GDN_HEADS * GDN_DV,
    GDN_HEADS,
    GDN_HEADS,
    NSA_HEADS * NSA_DK,
    NSA_GROUPS * NSA_DK,
    NSA_GROUPS * NSA_DV,
    NSA_GROUPS * NSA_DK,
    NSA_GROUPS * NSA_DV,
    NSA_GROUPS * NSA_DK,
    NSA_GROUPS * NSA_DV,
    NSA_HEADS * 3,
    2 * D_MODEL,
)
D_IN = sum(IN_SPLITS)


def rmsnorm(x, w):
    xf = x.astype(jnp.float32)
    y = xf * lax.rsqrt(jnp.mean(xf * xf, axis=-1, keepdims=True) + EPS)
    return (y * w.astype(jnp.float32)).astype(x.dtype)

def l2norm(x):
    return x * lax.rsqrt(jnp.sum(x * x, axis=-1, keepdims=True) + EPS)

def causal_dwconv(x, w):
    width, c = w.shape
    return lax.conv_general_dilated(
        x, w[:, None, :].astype(x.dtype), window_strides=(1,), padding=((width - 1, 0),),
        dimension_numbers=('NWC', 'WIO', 'NWC'), feature_group_count=c)

def alibi_slopes(n):
    return 2.0 ** (-8.0 * jnp.arange(1, n + 1, dtype=jnp.float32) / n)

def masked_softmax(s, valid):
    p = jax.nn.softmax(jnp.where(valid, s, NEG), axis=-1)
    return jnp.where(valid, p, 0.0)

def chunk_gated_delta_rule(q, k, v, beta, g):
    B, S, H, dk = q.shape
    dv = v.shape[-1]
    C = GDN_CHUNK
    n = S // C

    def chunks(t):
        t = t.reshape((B, n, C, H) + t.shape[3:])
        return jnp.moveaxis(t, (1, 3), (0, 2))

    qc, kc, vc, bc = chunks(q), chunks(k), chunks(v), chunks(beta)
    gcum = jnp.cumsum(chunks(g), axis=-1)
    idx = jnp.arange(C)
    strict = idx[:, None] > idx[None, :]
    incl = idx[:, None] >= idx[None, :]
    gdiff = gcum[..., :, None] - gcum[..., None, :]
    dec_strict = jnp.where(strict, jnp.exp(jnp.where(strict, gdiff, 0.0)), 0.0)
    dec_incl = jnp.where(incl, jnp.exp(jnp.where(incl, gdiff, 0.0)), 0.0)
    lower = bc[..., None] * jnp.einsum('nbhid,nbhjd->nbhij', kc, kc) * dec_strict
    gam = jnp.exp(gcum)
    rhs = jnp.concatenate([(bc * gam)[..., None] * kc, bc[..., None] * vc], axis=-1)
    sol = lax.linalg.triangular_solve(lower + jnp.eye(C, dtype=q.dtype), rhs,
                                      left_side=True, lower=True, unit_diagonal=True)
    w_c, u0_c = sol[..., :dk], sol[..., dk:]
    qk = jnp.einsum('nbhid,nbhjd->nbhij', qc, kc) * dec_incl
    q_dec = qc * gam[..., None]
    k_tail = kc * jnp.exp(gcum[..., -1:] - gcum)[..., None]
    g_last = gam[..., -1]

    def step(state, inp):
        w_, u0_, qk_, qd_, kt_, gl_ = inp
        u = u0_ - jnp.einsum('bhcd,bhde->bhce', w_, state)
        o = jnp.einsum('bhcd,bhde->bhce', qd_, state) + jnp.einsum('bhij,bhje->bhie', qk_, u)
        new_state = gl_[..., None, None] * state + jnp.einsum('bhcd,bhce->bhde', kt_, u)
        return new_state, o

    s0 = jnp.zeros((B, H, dk, dv), q.dtype)
    _, o = lax.scan(step, s0, (w_c, u0_c, qk, q_dec, k_tail, g_last))
    return jnp.moveaxis(o, (0, 2), (1, 3)).reshape(B, S, H, dv)

def gdn_mixer(q, k, v, z, b, a, conv_w, a_log, dt_bias, norm_w):
    B, S, _ = q.shape
    H, dk, dv = GDN_HEADS, GDN_DK, GDN_DV
    f32 = jnp.float32
    qkv = jax.nn.silu(causal_dwconv(jnp.concatenate([q, k, v], axis=-1), conv_w))
    q, k, v = jnp.split(qkv, [H * dk, 2 * H * dk], axis=-1)
    q = l2norm(q.reshape(B, S, H, dk).astype(f32)) * (dk ** -0.5)
    k = l2norm(k.reshape(B, S, H, dk).astype(f32))
    v = v.reshape(B, S, H, dv).astype(f32)
    beta = jax.nn.sigmoid(b.astype(f32))
    g = -jnp.exp(a_log.astype(f32)) * jax.nn.softplus(a.astype(f32) + dt_bias.astype(f32))
    o = chunk_gated_delta_rule(q, k, v, beta, g).astype(z.dtype)
    o = rmsnorm(o, norm_w) * jax.nn.silu(z.reshape(B, S, H, dv))
    return o.reshape(B, S, H * dv)

def compress_blocks(x, pos, w1, w2):
    B, S, G, d = x.shape
    r = CMP_LEN // CMP_STRIDE
    xs = x.reshape(B, S // CMP_STRIDE, CMP_STRIDE, G, d)
    nc = S // CMP_STRIDE - r + 1
    blocks = jnp.concatenate([xs[:, i:i + nc] for i in range(r)], axis=2)
    blocks = blocks + pos[:, None, :]
    flat = jnp.moveaxis(blocks, 3, 2).reshape(B, nc, G, CMP_LEN * d)
    return jax.nn.gelu(flat @ w1) @ w2

def nsa_mixer(q, k_cmp, v_cmp, k_slc, v_slc, k_win, v_win, gate,
              cmp_pos_k, cmp_w1_k, cmp_w2_k, cmp_pos_v, cmp_w1_v, cmp_w2_v):
    B, S, _ = q.shape
    H, G, R, dk, dv = NSA_HEADS, NSA_GROUPS, NSA_HPG, NSA_DK, NSA_DV
    f32 = jnp.float32
    slopes = alibi_slopes(H).reshape(G, R)
    t = jnp.arange(S)
    qh = q.reshape(B, S, G, R, dk) * (dk ** -0.5)
    grp = lambda y, d: y.reshape(B, S, G, d)

    kc = compress_blocks(grp(k_cmp, dk), cmp_pos_k, cmp_w1_k, cmp_w2_k)
    vc = compress_blocks(grp(v_cmp, dv), cmp_pos_v, cmp_w1_v, cmp_w2_v)
    nc = kc.shape[1]
    blk_start = jnp.arange(nc) * CMP_STRIDE
    dist_c = t[:, None] - (blk_start + CMP_LEN - 1)[None, :]
    s_c = jnp.einsum('bsgrd,bngd->bgrsn', qh, kc).astype(f32) \
        - slopes[None, :, :, None, None] * dist_c.astype(f32)
    p_c = masked_softmax(s_c, dist_c >= 0)
    o_cmp = jnp.einsum('bgrsn,bngd->bsgrd', p_c.astype(vc.dtype), vc)

    ns = S // SEL_BLOCK
    sel_start = jnp.arange(ns) * SEL_BLOCK
    overlap = jnp.clip(jnp.minimum(blk_start[:, None] + CMP_LEN, sel_start[None, :] + SEL_BLOCK)
                       - jnp.maximum(blk_start[:, None], sel_start[None, :]), 0, None).astype(f32) / CMP_LEN
    imp = jnp.einsum('bgsn,nj->bgsj', p_c.sum(axis=2), overlap)
    cur = t // SEL_BLOCK
    j = jnp.arange(ns)
    forced = (j[None, :] == 0) | (j[None, :] == cur[:, None]) | (j[None, :] == cur[:, None] - 1)
    sel_valid = j[None, :] <= cur[:, None]
    imp = jnp.where(sel_valid, jnp.where(forced, FORCED_SCORE, imp), NEG)
    n_sel = min(SEL_TOPN, ns)
    _, sel_idx = lax.top_k(imp, n_sel)

    ks = k_slc.reshape(B, ns, SEL_BLOCK, G, dk).transpose(0, 3, 1, 2, 4)
    vs = v_slc.reshape(B, ns, SEL_BLOCK, G, dv).transpose(0, 3, 1, 2, 4)
    QC = SEL_QCHUNK
    nq = S // QC
    q_ch = qh.reshape(B, nq, QC, G, R, dk).transpose(1, 0, 3, 4, 2, 5)
    idx_ch = sel_idx.reshape(B, G, nq, QC, n_sel).transpose(2, 0, 1, 3, 4)
    t_ch = t.reshape(nq, QC)
    nk = n_sel * SEL_BLOCK

    def sel_chunk(args):
        qb, ib, tb = args
        flat = ib.reshape(B, G, QC * n_sel)[:, :, :, None, None]
        kg = jnp.take_along_axis(ks, flat, axis=2).reshape(B, G, QC, nk, dk)
        vg = jnp.take_along_axis(vs, flat, axis=2).reshape(B, G, QC, nk, dv)
        pos = (ib[..., None] * SEL_BLOCK + jnp.arange(SEL_BLOCK)).reshape(B, G, QC, nk)
        dist = tb[None, None, :, None] - pos
        s = jnp.einsum('bgrqd,bgqkd->bgrqk', qb, kg).astype(f32) \
            - slopes[None, :, :, None, None] * dist[:, :, None].astype(f32)
        pr = masked_softmax(s, (dist >= 0)[:, :, None])
        return jnp.einsum('bgrqk,bgqkd->bgrqd', pr.astype(vg.dtype), vg)

    o_slc = lax.map(sel_chunk, (q_ch, idx_ch, t_ch))
    o_slc = o_slc.transpose(1, 0, 4, 2, 3, 5).reshape(B, S, G, R, dv)

    QB = WIN_QBLOCK
    nb = S // QB
    nwb = WINDOW // QB

    def band(y, d):
        yb = y.reshape(B, nb, QB, G, d).transpose(1, 0, 3, 2, 4)
        yp = jnp.pad(yb, ((nwb, 0), (0, 0), (0, 0), (0, 0), (0, 0)))
        return jnp.concatenate([yp[i:i + nb] for i in range(nwb + 1)], axis=3)

    kband, vband = band(k_win, dk), band(v_win, dv)
    q_wb = qh.reshape(B, nb, QB, G, R, dk).transpose(1, 0, 3, 4, 2, 5)
    qpos = t.reshape(nb, QB)
    kpos = (jnp.arange(nb)[:, None] - nwb) * QB + jnp.arange((nwb + 1) * QB)[None, :]

    def win_block(args):
        qb, kb, vb, tq, tk = args
        dist = tq[:, None] - tk[None, :]
        valid = (dist >= 0) & (dist < WINDOW) & (tk[None, :] >= 0)
        s = jnp.einsum('bgrqd,bgkd->bgrqk', qb, kb).astype(f32) \
            - slopes[None, :, :, None, None] * dist.astype(f32)
        pr = masked_softmax(s, valid)
        return jnp.einsum('bgrqk,bgkd->bgrqd', pr.astype(vb.dtype), vb)

    o_win = lax.map(win_block, (q_wb, kband, vband, qpos, kpos))
    o_win = o_win.transpose(1, 0, 4, 2, 3, 5).reshape(B, S, G, R, dv)

    gates = jax.nn.sigmoid(gate).reshape(B, S, G, R, 3)
    o = gates[..., 0:1] * o_cmp + gates[..., 1:2] * o_slc + gates[..., 2:3] * o_win
    return o.reshape(B, S, H * dv)

def first_inputs(seed: int = 0) -> dict:
    key = jax.random.key(seed)
    ks = jax.random.split(key, 32)
    L, D = DEPTH, D_MODEL
    f32 = jnp.float32

    def nrm(k, shape, fan_in):
        return jax.random.normal(k, shape, f32) * (fan_in ** -0.5)

    def gain(k, n):
        return 1.0 + 0.05 * jax.random.normal(k, (L, n), f32)

    dt = jnp.exp(jax.random.uniform(ks[6], (L, GDN_HEADS), f32, minval=np.log(1e-3), maxval=np.log(1e-1)))
    return {
        'x': jax.random.normal(ks[0], (BATCH, SEQ, D), f32),
        'p': jax.random.normal(ks[1], (DEPTH, BATCH, SEQ, PLE_DIM), f32),
        'norm_mix_pre': gain(ks[2], D),
        'w_in': nrm(ks[3], (L, D, D_IN), D),
        'conv_qkv': nrm(ks[4], (L, GDN_CONV, 2 * GDN_HEADS * GDN_DK + GDN_HEADS * GDN_DV), GDN_CONV),
        'a_log': jnp.log(jax.random.uniform(ks[5], (L, GDN_HEADS), f32, minval=1.0, maxval=16.0)),
        'dt_bias': dt + jnp.log(-jnp.expm1(-dt)),
        'gdn_norm': gain(ks[7], GDN_DV),
        'cmp_pos_k': 0.1 * jax.random.normal(ks[8], (L, CMP_LEN, NSA_DK), f32),
        'cmp_w1_k': nrm(ks[9], (L, CMP_LEN * NSA_DK, CMP_HIDDEN), CMP_LEN * NSA_DK),
        'cmp_w2_k': nrm(ks[10], (L, CMP_HIDDEN, NSA_DK), CMP_HIDDEN),
        'cmp_pos_v': 0.1 * jax.random.normal(ks[11], (L, CMP_LEN, NSA_DV), f32),
        'cmp_w1_v': nrm(ks[12], (L, CMP_LEN * NSA_DV, CMP_HIDDEN), CMP_LEN * NSA_DV),
        'cmp_w2_v': nrm(ks[13], (L, CMP_HIDDEN, NSA_DV), CMP_HIDDEN),
        'w_a2d': nrm(ks[14], (L, GDN_HEADS * GDN_DV, D), GDN_HEADS * GDN_DV),
        'w_b2d': nrm(ks[15], (L, NSA_HEADS * NSA_DV, D), NSA_HEADS * NSA_DV),
        'w_o': nrm(ks[16], (L, D, D), D),
        'norm_mix_post': gain(ks[17], D),
        'norm_ffn_pre': gain(ks[18], D),
        'w_up': nrm(ks[19], (L, D, 2 * D_FF), D),
        'conv_ffn': nrm(ks[20], (L, FFN_CONV, 2 * D_FF), FFN_CONV),
        'conv_ffn_b': 0.02 * jax.random.normal(ks[21], (L, 2 * D_FF), f32),
        'w_down': nrm(ks[22], (L, D_FF, D), D_FF),
        'norm_ffn_post': gain(ks[23], D),
        'w_ple': nrm(ks[24], (L, PLE_DIM, D), PLE_DIM),
        'w_ple_gate': nrm(ks[25], (L, D, D), D),
        'norm_ple_post': gain(ks[26], D),
    }

def first_block(x, p, norm_mix_pre, w_in, conv_qkv, a_log, dt_bias, gdn_norm,
              cmp_pos_k, cmp_w1_k, cmp_w2_k, cmp_pos_v, cmp_w1_v, cmp_w2_v,
              w_a2d, w_b2d, w_o, norm_mix_post, norm_ffn_pre, w_up, conv_ffn, conv_ffn_b,
              w_down, norm_ffn_post, w_ple, w_ple_gate, norm_ple_post):
    offs = np.cumsum(IN_SPLITS)[:-1].tolist()
    h = x
    for i in range(DEPTH):
        u = rmsnorm(h, norm_mix_pre[i])
        (qa, ka, va, za, ba, aa, qb, kcm, vcm, ksl, vsl, kwi, vwi, gnsa, gmix) = \
            jnp.split(u @ w_in[i], offs, axis=-1)
        ya = gdn_mixer(qa, ka, va, za, ba, aa, conv_qkv[i], a_log[i], dt_bias[i], gdn_norm[i])
        yb = nsa_mixer(qb, kcm, vcm, ksl, vsl, kwi, vwi, gnsa,
                       cmp_pos_k[i], cmp_w1_k[i], cmp_w2_k[i], cmp_pos_v[i], cmp_w1_v[i], cmp_w2_v[i])
        g_a, g_b = jnp.split(jax.nn.sigmoid(gmix), 2, axis=-1)
        mixed = (g_a * (ya @ w_a2d[i]) + g_b * (yb @ w_b2d[i])) @ w_o[i]
        h = h + rmsnorm(mixed, norm_mix_post[i])
        f = rmsnorm(h, norm_ffn_pre[i]) @ w_up[i]
        f = causal_dwconv(f, conv_ffn[i]) + conv_ffn_b[i]
        f_gate, f_val = jnp.split(f, 2, axis=-1)
        f = (jax.nn.gelu(f_gate) * f_val) @ w_down[i]
        h = h + rmsnorm(f, norm_ffn_post[i])
        e = (p[i] @ w_ple[i]) * jax.nn.sigmoid(h @ w_ple_gate[i])
        h = h + rmsnorm(e, norm_ple_post[i])
    return h


ATTN_HEADS = 8
HEAD_DIM = 64
ATTN_WIDTH = ATTN_HEADS * HEAD_DIM
CONV_GROUPS = 8
CONV_CH = D_MODEL - ATTN_WIDTH
MIX_WIDTH = ATTN_WIDTH + CONV_CH
IN_COLS = 3 * ATTN_WIDTH + 2 * CONV_CH
CONV_KERNEL = 31
MOBA_BLOCK = 256
MOBA_TOPK = 3
Q_CHUNK = 128
NUM_BUCKETS = 32
MAX_DISTANCE = 128
D_FF_2 = -(-8 * D_MODEL // (3 * 256)) * 256
RMS_EPS = 1e-6
LN_EPS = 1e-5
NEG_INF = -1e30
ATTN_SCALE = HEAD_DIM ** -0.5


def rms_norm(x, g):
    xf = x.astype(jnp.float32)
    y = xf * lax.rsqrt(jnp.mean(xf * xf, axis=-1, keepdims=True) + RMS_EPS)
    return (y * g.astype(jnp.float32)).astype(x.dtype)

def t5_bucket(dist):
    max_exact = NUM_BUCKETS // 2
    d = jnp.maximum(dist, 1).astype(jnp.float32)
    large = max_exact + (jnp.log(d / max_exact) / math.log(MAX_DISTANCE / max_exact)
                         * (NUM_BUCKETS - max_exact)).astype(jnp.int32)
    large = jnp.minimum(large, NUM_BUCKETS - 1)
    return jnp.where(dist < max_exact, dist, large)

def moba_attention(q, k, v, rel_bias):
    B, H, S, Dh = q.shape
    nb = -(-S // MOBA_BLOCK)
    s_pad = nb * MOBA_BLOCK
    n_sel = max(1, min(MOBA_TOPK, nb - 1))
    nq = S // Q_CHUNK
    pad = ((0, 0), (0, 0), (0, s_pad - S), (0, 0))
    k_blocks = jnp.pad(k, pad).reshape(B, H, nb, MOBA_BLOCK, Dh)
    v_blocks = jnp.pad(v, pad).reshape(B, H, nb, MOBA_BLOCK, Dh)

    k_mean = jnp.mean(k_blocks.astype(jnp.float32), axis=3)
    gate = jnp.einsum('bhsd,bhnd->bhsn', q.astype(jnp.float32), k_mean)
    q_block = jnp.arange(S, dtype=jnp.int32) // MOBA_BLOCK
    fully_past = jnp.arange(nb, dtype=jnp.int32)[None, :] < q_block[:, None]
    gate = jnp.where(fully_past, gate, NEG_INF)
    _, sel = lax.top_k(gate, n_sel)
    sel = sel.astype(jnp.int32)

    bias_ht = rel_bias.T.astype(jnp.float32)
    head_ix = jnp.arange(H)
    offs = jnp.arange(MOBA_BLOCK, dtype=jnp.int32)
    rank_ix = jnp.arange(n_sel, dtype=jnp.int32)

    q_c = q.reshape(B, H, nq, Q_CHUNK, Dh).transpose(0, 2, 1, 3, 4).reshape(B * nq, H, Q_CHUNK, Dh)
    sel_c = sel.reshape(B, H, nq, Q_CHUNK, n_sel).transpose(0, 2, 1, 3, 4).reshape(B * nq, H, Q_CHUNK, n_sel)
    b_ids = jnp.repeat(jnp.arange(B, dtype=jnp.int32), nq)
    c_ids = jnp.tile(jnp.arange(nq, dtype=jnp.int32), B)

    def chunk(args):
        qc, sc, b, c = args
        kb = k_blocks[b]
        vb = v_blocks[b]
        t = c * Q_CHUNK + jnp.arange(Q_CHUNK, dtype=jnp.int32)
        own = (c * Q_CHUNK) // MOBA_BLOCK
        k_sel = kb[head_ix[:, None, None], sc]
        v_sel = vb[head_ix[:, None, None], sc]
        s_sel = jnp.einsum('hqd,hqnkd->hqnk', qc, k_sel).astype(jnp.float32) * ATTN_SCALE
        dist_sel = t[None, :, None, None] - (sc[..., None] * MOBA_BLOCK + offs)
        s_sel = s_sel + bias_ht[head_ix[:, None, None, None], t5_bucket(jnp.maximum(dist_sel, 0))]
        valid = (rank_ix < own)[None, None, :, None]
        s_sel = jnp.where(valid, s_sel, NEG_INF)
        k_own = kb[:, own]
        v_own = vb[:, own]
        s_own = jnp.einsum('hqd,hkd->hqk', qc, k_own).astype(jnp.float32) * ATTN_SCALE
        dist_own = t[:, None] - (own * MOBA_BLOCK + offs)[None, :]
        s_own = s_own + bias_ht[:, t5_bucket(jnp.maximum(dist_own, 0))]
        s_own = jnp.where((dist_own >= 0)[None], s_own, NEG_INF)
        logits = jnp.concatenate([s_sel.reshape(H, Q_CHUNK, n_sel * MOBA_BLOCK), s_own], axis=-1)
        p = jax.nn.softmax(logits, axis=-1).astype(v.dtype)
        p_sel = p[..., :n_sel * MOBA_BLOCK].reshape(H, Q_CHUNK, n_sel, MOBA_BLOCK)
        p_own = p[..., n_sel * MOBA_BLOCK:]
        return (jnp.einsum('hqnk,hqnkd->hqd', p_sel, v_sel)
                + jnp.einsum('hqk,hkd->hqd', p_own, v_own))

    out = lax.map(chunk, (q_c, sel_c, b_ids, c_ids))
    return out.reshape(B, nq, H, Q_CHUNK, Dh).transpose(0, 1, 3, 2, 4).reshape(B, S, H * Dh)

def conformer_conv(a, g, w_dw, b_dw, ln_g, ln_b):
    C = a.shape[-1]
    u = a * jax.nn.sigmoid(g)
    u = lax.conv_general_dilated(u, w_dw[:, None, :], window_strides=(1,),
                                 padding=((CONV_KERNEL - 1, 0),),
                                 dimension_numbers=('NWC', 'WIO', 'NWC'),
                                 feature_group_count=C) + b_dw
    uf = u.astype(jnp.float32)
    mu = jnp.mean(uf, axis=-1, keepdims=True)
    var = jnp.mean(jnp.square(uf - mu), axis=-1, keepdims=True)
    un = (uf - mu) * lax.rsqrt(var + LN_EPS) * ln_g.astype(jnp.float32) + ln_b.astype(jnp.float32)
    return jax.nn.silu(un).astype(a.dtype)

def second_inputs(seed: int = 0) -> dict:
    key = jax.random.key(seed)
    ks = jax.random.split(key, 16)
    f32 = jnp.float32
    nrm = lambda k, shape, scale: jax.random.normal(k, shape, f32) * scale
    return {
        'x': jax.random.normal(ks[0], (BATCH, SEQ, D_MODEL), f32),
        'mix_norm_g': 1.0 + nrm(ks[1], (DEPTH, D_MODEL), 0.02),
        'w_in': nrm(ks[2], (DEPTH, D_MODEL, IN_COLS), D_MODEL ** -0.5),
        'rel_bias': nrm(ks[3], (NUM_BUCKETS, ATTN_HEADS), 0.5),
        'conv_w': nrm(ks[4], (DEPTH, CONV_KERNEL, CONV_CH), CONV_KERNEL ** -0.5),
        'conv_b': nrm(ks[5], (DEPTH, CONV_CH), 0.02),
        'conv_ln_g': 1.0 + nrm(ks[6], (DEPTH, CONV_CH), 0.02),
        'conv_ln_b': nrm(ks[7], (DEPTH, CONV_CH), 0.02),
        'w_out': nrm(ks[8], (DEPTH, MIX_WIDTH, D_MODEL), MIX_WIDTH ** -0.5),
        'ffn_norm_g': 1.0 + nrm(ks[9], (DEPTH, D_MODEL), 0.02),
        'w_gate': nrm(ks[10], (DEPTH, D_MODEL, D_FF_2), D_MODEL ** -0.5),
        'w_up': nrm(ks[11], (DEPTH, D_MODEL, D_FF_2), D_MODEL ** -0.5),
        'w_down': nrm(ks[12], (DEPTH, D_FF_2, D_MODEL), D_FF_2 ** -0.5),
        'final_norm_g': 1.0 + nrm(ks[13], (D_MODEL,), 0.02),
    }

def second_block(x, mix_norm_g, w_in, rel_bias, conv_w, conv_b, conv_ln_g, conv_ln_b,
              w_out, ffn_norm_g, w_gate, w_up, w_down, final_norm_g):
    B, S, _ = x.shape
    splits = [ATTN_WIDTH, 2 * ATTN_WIDTH, 3 * ATTN_WIDTH, 3 * ATTN_WIDTH + CONV_CH]

    def heads(t):
        return t.reshape(B, S, ATTN_HEADS, HEAD_DIM).transpose(0, 2, 1, 3)

    h = x
    for l in range(DEPTH):
        u = rms_norm(h, mix_norm_g[l])
        proj = u @ w_in[l]
        q, k, v, glu_a, glu_g = jnp.split(proj, splits, axis=-1)
        attn_out = moba_attention(heads(q), heads(k), heads(v), rel_bias)
        conv_out = conformer_conv(glu_a, glu_g, conv_w[l], conv_b[l],
                                  conv_ln_g[l], conv_ln_b[l])
        mixed = jnp.concatenate([attn_out, conv_out], axis=-1)
        h = h + mixed @ w_out[l]
        u = rms_norm(h, ffn_norm_g[l])
        h = h + (jax.nn.silu(u @ w_gate[l]) * (u @ w_up[l])) @ w_down[l]
    return rms_norm(h, final_norm_g)


def setup_inputs(seed=0):
    out = dict(first_inputs(seed))
    for name, value in second_inputs(seed + 1).items():
        if name != "x":
            out[name + "_2"] = value
    return out


def reference(
    x, p, norm_mix_pre, w_in, conv_qkv, a_log, dt_bias, gdn_norm, cmp_pos_k, cmp_w1_k, cmp_w2_k,
    cmp_pos_v, cmp_w1_v, cmp_w2_v, w_a2d, w_b2d, w_o, norm_mix_post, norm_ffn_pre, w_up,
    conv_ffn, conv_ffn_b, w_down, norm_ffn_post, w_ple, w_ple_gate, norm_ple_post, mix_norm_g_2,
    w_in_2, rel_bias_2, conv_w_2, conv_b_2, conv_ln_g_2, conv_ln_b_2, w_out_2, ffn_norm_g_2,
    w_gate_2, w_up_2, w_down_2, final_norm_g_2,
):
    x = first_block(
        x, p, norm_mix_pre, w_in, conv_qkv, a_log, dt_bias, gdn_norm, cmp_pos_k, cmp_w1_k,
        cmp_w2_k, cmp_pos_v, cmp_w1_v, cmp_w2_v, w_a2d, w_b2d, w_o, norm_mix_post, norm_ffn_pre,
        w_up, conv_ffn, conv_ffn_b, w_down, norm_ffn_post, w_ple, w_ple_gate, norm_ple_post,
    )
    return second_block(
        x, mix_norm_g_2, w_in_2, rel_bias_2, conv_w_2, conv_b_2, conv_ln_g_2, conv_ln_b_2,
        w_out_2, ffn_norm_g_2, w_gate_2, w_up_2, w_down_2, final_norm_g_2,
    )


_drawn_inputs = setup_inputs


def setup_inputs(seed=0):
    import zlib

    import numpy as np

    out = dict(_drawn_inputs(seed))
    spreads = {}
    factors = {'cmp_pos_k': 8.0,
     'conv_ffn_b': 3.507,
     'mix_norm_g_2': 8.0,
     'conv_b_2': 17.282,
     'conv_ln_g_2': 29.021,
     'conv_ln_b_2': 29.453,
     'ffn_norm_g_2': 6.796,
     'final_norm_g_2': 21.391,
     'rel_bias_2': 2.708}
    for name, (base, spread) in spreads.items():
        noise = np.random.default_rng([zlib.crc32(name.encode()), seed]).standard_normal(out[name].shape)
        drawn = base * np.exp(spread * noise) if base else spread * noise
        out[name] = __import__('jax').numpy.asarray(drawn.astype(out[name].dtype))
    for name, factor in factors.items():
        out[name] = (out[name] * factor).astype(out[name].dtype)
    return out
```

```python
from contextlib import ExitStack

import numpy as np

import concourse.bass as bass
from concourse import mybir

F32 = mybir.dt.float32
F32R = mybir.dt.float32r
BF16 = mybir.dt.bfloat16
ALU = mybir.AluOpType
ACT = mybir.ActivationFunctionType
AX = mybir.AxisListType.X

P = 128
D = 1024
S = 512
DC = D // P
T = S // P
EPS = 1e-6
LN_EPS = 1e-5
NEG = -1e30

GH = 4
C = 64
NH, NG, DK = 8, 2, 64
R = NH // NG
CMP_LEN, CMP_STRIDE, CMP_HID = 32, 16, 256
NC = S // CMP_STRIDE - 1
PLE = 256
FF = 2816
FC = FF // P
CT = 31
CC = 512 // P

BLK = 16
PHASES = [
    ("qkv", 6, 16, 2), ("z", 2, 16, 2),
    ("nq", 2, 16, 2), ("ncmp", 2, 8, 1), ("nk", 1, 16, 2), ("nv", 1, 16, 2),
    ("mix", 16, 12, 2), ("wo", 4, 16, 2), ("up", 22, 16, 2), ("down", 16, 11, 1), ("ple", 8, 10, 2),
    ("qk2", 4, 16, 2), ("glu", 4, 16, 2), ("v2", 2, 16, 2), ("wo2", 4, 16, 2),
    ("up2", 22, 16, 2), ("down2", 16, 11, 1),
]
PIECE0, SEG0, NB, NSEG, NPIECE, NEXT = {}, {}, {}, {}, {}, {}
_piece = _seg = 0
for _k, (_name, _n, _nb, _s) in enumerate(PHASES):
    PIECE0[_name], SEG0[_name], NB[_name], NSEG[_name], NPIECE[_name] = _piece, _seg, _nb, _s, _n
    NEXT[_name] = PHASES[_k + 1][0] if _k + 1 < len(PHASES) else None
    _piece += _n
    _seg += _n * _s
PIECES = _piece
PIECE_NB = [nb for _, n, nb, _ in PHASES for _ in range(n)]
PIECE_SEG = (
    np.cumsum([0] + [s for _, n, _, s in PHASES for _ in range(n)]).tolist())
RING = {"qkv": 12, "z": 4, "nq": 4, "ncmp": 2, "nk": 2, "nv": 2, "mix": 32, "up": 44, "ple": 16,
        "qk2": 8, "glu": 8, "v2": 4, "up2": 44}
RING0, _n = {}, 0
for _name, _, _, _ in PHASES:
    if _name in RING:
        RING0[_name] = _n
        _n += RING[_name]

COLS = {}
_n = 0
for _name, _w in (("mix_pre", 8), ("mix_post", 8), ("ffn_pre", 8), ("ffn_post", 8), ("ple_post", 8),
                  ("mix2", 8), ("ffn2", 8), ("final", 8), ("cqkv", 48), ("gdn", 1), ("cffn", 132),
                  ("cffnb", 44), ("cw2", 124), ("cb2", 4), ("lng", 4), ("lnb", 4), ("alog", 4),
                  ("dtb", 4), ("far", 8), ("posk", 16), ("posv", 16), ("eps", 1), ("lneps", 1)):
    COLS[_name] = _n
    _n += _w
NCOLS = _n
CON = {}
_n = 0
for _name, _w in (("tri", 128), ("after", 128), ("half", 256), ("level", 6 * 128)):
    CON[_name] = _n
    _n += _w
NCON = _n


def build(nc, wstream, xT, pT, cols_d, ident_d, causal_d, consts_d, cneg_d, c01_d, alibi_d, krow_d, crow_d,
          wsm_d, w1k_d, w1v_d, w2_d, bias2_d, out):
    with ExitStack() as ctx:
        def sb(name, shape, dt=F32, scope=ctx):
            return scope.enter_context(nc.sbuf_tensor(name, shape, dt))

        def sem(name):
            return ctx.enter_context(nc.semaphore(name))

        hT = sb("hT", [P, DC, S])
        AH = sb("AH", [P, DC, S], F32R)
        AL = sb("AL", [P, DC, S], F32R)
        RAW = [sb(f"raw{b}", [P, BLK * P]) for b in range(2)]
        WH = [sb(f"whi{b}", [P, BLK * P], F32R) for b in range(2)]
        WL = [sb(f"wlo{b}", [P, BLK * P], F32R) for b in range(2)]
        cols = sb("cols", [P, NCOLS])
        ones = sb("ones", [P, P])
        ident = sb("ident", [P, P])
        RR = sb("RR", [P, S])
        SQ = sb("SQ", [P, 2, S])
        TMP = sb("TMP", [P, 2, S])
        YX = sb("YX", [P, S])

        def col(name, j=0, n=1):
            if isinstance(j, int):
                return cols[:, COLS[name] + j:COLS[name] + j + n]
            return cols[:, bass.ds(j + COLS[name], n)]

        blk1 = ExitStack()
        SG = sb("SG", [P, T, 32], F32, blk1)
        NG_T = sb("NG_T", [P, P], F32, blk1)
        MB = sb("MB", [P, 2, P], BF16, blk1)
        with ExitStack() as x:
            Tm = sb("Tm", [P, T, GH, P], F32, x)
            TT = sb("TT", [P, T, GH, P], F32, x)
        YAH = sb("YAH", [P, 4, S], F32R, blk1)
        YAL = sb("YAL", [P, 4, S], F32R, blk1)
        with ExitStack() as x:
            QKV = sb("QKV", [P, 12, S], F32, x)
            ZS = sb("ZS", [P, 4, S], F32, x)
            Y1 = sb("Y1", [P, T, GH, P], F32, x)
            AT = sb("AT", [P, T, GH, P], F32, x)
            OFF = sb("OFF", [P, T, GH, P], F32, x)
            QK = sb("QK", [P, T, GH, P], F32, x)
            ST = sb("ST", [P, 2, GH, P], F32, x)
            CS = sb("CS", [P, NCON], F32, x)
            WSR = sb("WSR", [P, DC * 32], F32, x)
            WSH = sb("WSH", [P, DC * 32], F32R, x)
            WSL = sb("WSL", [P, DC * 32], F32R, x)
            SM = sb("SM", [P, T, 32], F32, x)
            AA = sb("AA", [P, 4, T, GH], F32, x)
            EA = sb("EA", [P, GH], F32, x)
            G = sb("G", [P, T, GH], F32, x)
            EX = sb("EX", [P, 4, T, GH], F32, x)
            GC = sb("GC", [P, T, GH], F32, x)
            BG = sb("BG", [P, T, GH], F32, x)
            RO = sb("RO", [P, T, GH], F32, x)
        with ExitStack() as x:
            W1v = sb("W1v", [P, 16, CMP_HID], F32, x)
        YBH = sb("YBH", [P, 4, S], F32R, blk1)
        YBL = sb("YBL", [P, 4, S], F32R, blk1)
        with ExitStack() as x:
            QT = sb("QT", [P, NH, S], F32, x)
            KT = sb("KT", [P, 2, NG, S], F32, x)
            V1 = sb("V1", [P, T, 2 * P], F32, x)
            KC = sb("KC", [P, NG, 32], F32, x)
            VB = sb("VB", [P, NG, R * DK], F32, x)
            W2 = sb("W2", [P, 4, DK], F32, x)
            SC = sb("SC", [P, T, NH, 32], F32, x)
            CN = sb("CN", [P, T, 32], F32, x)
            C01 = sb("C01", [P, T, 32], F32, x)
            HID = sb("HID", [P, 4, 2 * NC], F32, x)
            SX = sb("SX", [P, 3, T, NH], F32, x)
            NM = sb("NM", [P, 2, 2], F32, x)
            LS = sb("LS", [P, 2, 2], F32, x)
            RL = sb("RL", [P, 2, 2], F32, x)
            with ExitStack() as y:
                W1 = [sb("W1k", [P, 16, CMP_HID], F32, y), W1v]
                Z = [sb(f"z{n}", [P, 16, 2 * NC], F32, y) for n in "kv"]
            PR = sb("PR", [P, 2, 2, S], F32, x)
            PT = sb("PT", [P, 2, 2, S], F32, x)
            Y = sb("Y", [P, T, NH * DK], F32, x)
        with ExitStack() as x:
            GHI = sb("GHI", [P, DC, S], F32R, x)
            GLO = sb("GLO", [P, DC, S], F32R, x)
        blk1.close()
        with ExitStack() as x:
            HH = sb("HH", [P, FC, S], F32R, x)
            HL = sb("HL", [P, FC, S], F32R, x)
            CG = sb("CG", [P, 2, S], F32, x)
            CV = sb("CV", [P, 2, S], F32, x)
        with ExitStack() as x:
            E = sb("E", [P, DC, S], F32, x)
            PX = sb("PX", [P, 2, S], F32, x)
            PH = sb("PH", [P, 2, S], F32R, x)
            PL = sb("PL", [P, 2, S], F32R, x)
            GP = sb("GP", [P, 2, S], F32, x)
        with ExitStack() as x:
            MB2 = sb("MB2", [P, P], F32, x)
            QT2 = sb("QT2", [P, 4, S], F32, x)
            KT2 = sb("KT2", [P, 4, S], F32, x)
            V2 = sb("V2", [P, T, 512], F32, x)
            BT = sb("BT", [P, NH, 256], F32, x)
            PR2 = sb("PR2", [P, 2, 2, S], F32, x)
            PT2 = sb("PT2", [P, 2, 2, S], F32, x)
            Y2 = sb("Y2", [P, T, 512], F32, x)
            UG = sb("UG", [P, CC, S + CT - 1], F32, x)
            CU = sb("CU", [P, CC, S], F32, x)
            NM2 = sb("NM2", [P, 2, 2], F32, x)
            LS2 = sb("LS2", [P, 2, 2], F32, x)
            RL2 = sb("RL2", [P, 2, 2], F32, x)
        ps = ctx.enter_context(nc.psum_tensor("ps", [P, 8, 512], F32))

        raw_landed = [sem(f"raw{b}_landed") for b in range(2)]
        w_hi_done, w_lo_done = sem("w_hi_done"), sem("w_lo_done")
        seg_done = sem("seg_done")
        bank_free = sem("bank_free")
        N_CON, N_NSA = 4, 6
        x_landed, cols_landed, con_landed = [sem(f"x{q}_landed") for q in range(4)], sem("cols_landed"), sem("con_landed")
        nsa_landed, w1_landed, p_landed, blk2_landed = (sem("nsa_landed"), sem("w1_landed"),
                                                         sem("p_landed"), sem("blk2_landed"))
        set_up, ws_split = sem("set_up"), sem("ws_split")
        sq_ready, sq_used, ms_ready = sem("sq_ready"), sem("sq_used"), sem("ms_ready")
        rt_ready, rr_ready, h_ready, y0_saved = sem("rt_ready"), sem("rr_ready"), sem("h_ready"), sem("y0_saved")
        in_tmp, in_hi, in_lo = sem("in_tmp"), sem("in_hi"), sem("in_lo")
        out_ready, out_stored = sem("out_ready"), [sem(f"out_stored{b}") for b in range(2)]
        post_tmp = sem("post_tmp")
        dve_own, act_own, pool_own = sem("dve_own"), sem("act_own"), sem("pool_own")

        class Own:

            def __init__(self, eng, sem_):
                self.eng, self.sem, self.n = eng, sem_, 0

            def mark(self, ins):
                ins.then_inc(self.sem, 1)
                self.n += 1

            def wait(self, back=0):
                self.eng.wait_ge(self.sem, self.n - back)

            def link(self, ins):
                self.mark(ins)
                self.wait()

        def staged(ph, last):
            return NB[ph] if not last else (NB[NEXT[ph]] if NEXT[ph] else None)

        def pairs(eng, ph, body):
            n = NPIECE[ph] // 2
            if n > 2:
                with eng.Fori(0, n - 1) as i:
                    body(i, False)
            else:
                for i in range(n - 1):
                    body(i, False)
            body(n - 1, True)

        def stage_hi(act, ph, i, b, last):
            if staged(ph, last) is None:
                return
            n = staged(ph, last) * P
            act.wait_ge(raw_landed[b], 16 * (PIECE0[ph] // 2 + 2) + i * 16)
            act.wait_ge(seg_done, SEG0[ph] + NSEG[ph] * (b + 1) + i * (2 * NSEG[ph]))
            nc.scalar.activation(WH[b][:, 0:n], RAW[b][:, 0:n], ACT.Copy).then_inc(w_hi_done, 1)

        def stage_lo(dve, ph, i, b, last):
            if staged(ph, last) is None:
                return
            n = staged(ph, last) * P
            dve.wait_ge(w_hi_done, PIECE0[ph] + b + 3 + i * 2)
            nc.vector.tensor_tensor(WL[b][:, 0:n], RAW[b][:, 0:n], WH[b][:, 0:n].bitcast(F32),
                                    ALU.subtract).then_inc(w_lo_done, 1)

        def weights_ready(pe, ph, i, b):
            pe.wait_ge(w_lo_done, PIECE0[ph] + b + 1 + i * 2)

        def product(out_, b, j0, n, xh, xl, start=True, stop=True):
            for k in range(n):
                w = slice((j0 + k) * P, (j0 + k + 1) * P)
                nc.tensor.matmul(out_, WH[b][:, w], xh[:, k, :], start=start and k == 0, stop=False)
                nc.tensor.matmul(out_, WH[b][:, w], xl[:, k, :], start=False, stop=False)
                last = nc.tensor.matmul(out_, WL[b][:, w], xh[:, k, :], start=False,
                                        stop=stop and k == n - 1)
            return last

        def square(act, k, m, src):
            if 8 * k + m >= 2:
                act.wait_ge(sq_used, 8 * k + m - 1)
            nc.scalar.activation(SQ[:, m % 2, :], src, ACT.Square).then_inc(sq_ready, 1)

        def add_squares(pe, k, m):
            pe.wait_ge(sq_ready, 8 * k + m + 1)
            nc.tensor.matmul(ps[:, 7, :], ones[:, :], SQ[:, m % 2, :], start=m == 0,
                             stop=m == DC - 1).then_inc(sq_used, 1)

        def rms_root(act, k):
            act.wait_ge(ms_ready, k + 1)
            nc.scalar.activation(RR[:, :], RR[:, :], ACT.Sqrt).then_inc(rt_ready, 1)

        def rms_rest(dve, k):
            dve.wait_ge(sq_used, 8 * k + 8)
            nc.vector.tensor_scalar(RR[:, :], ps[:, 7, :], 1.0 / D, EPS, ALU.mult, ALU.add).then_inc(ms_ready, 1)
            dve.wait_ge(rt_ready, k + 1)
            nc.vector.reciprocal(RR[:, :], RR[:, :]).then_inc(rr_ready, 1)
            dve.wait_ge(rr_ready, k + 1)

        def pre_hi(act, j):
            for m in range(DC):
                act.wait_ge(in_tmp, 8 * j + m + 1)
                nc.scalar.activation(AH[:, m, :], TMP[:, m % 2, :], ACT.Copy).then_inc(in_hi, 1)

        def pre_rest(dve, j, name):
            for m in range(DC + 1):
                if m < DC:
                    if m >= 2:
                        dve.wait_ge(in_lo, 8 * j + m - 1)
                    if name:
                        ins = nc.vector.scalar_tensor_tensor(TMP[:, m % 2, :], hT[:, m, :], col(name, m),
                                                             RR[:, :], ALU.mult, ALU.mult)
                    else:
                        ins = nc.vector.tensor_copy(TMP[:, m % 2, :], hT[:, m, :])
                    ins.then_inc(in_tmp, 1)
                if m >= 1:
                    dve.wait_ge(in_hi, 8 * j + m)
                    nc.vector.tensor_tensor(AL[:, m - 1, :], TMP[:, (m - 1) % 2, :], AH[:, m - 1, :].bitcast(F32),
                                            ALU.subtract).then_inc(in_lo, 1)

        def y_bank(m):
            return ps[:, m % 7, :]

        def post_add(dve, j, name, first, y_of):
            for m in range(DC):
                y = first[:, :] if first is not None and m == 0 else y_of(m)
                nc.vector.scalar_tensor_tensor(TMP[:, m % 2, :], y, col(name, m), RR[:, :], ALU.mult,
                                               ALU.mult).then_inc(post_tmp, 1)
                dve.wait_ge(post_tmp, 8 * j + m + 1)
                nc.vector.tensor_tensor(hT[:, m, :], hT[:, m, :], TMP[:, m % 2, :], ALU.add).then_inc(h_ready, 1)
        small_done, sm_saved, l2_sq, l2_sum, l2_root, l2_rec, l2_done = (sem(n) for n in (
            "small_done", "sm_saved", "l2_sq", "l2_sum", "l2_root", "l2_rec", "l2_done"))
        g_ready, gsum_done, gsum_read, rows_done, at_ready = (sem(n) for n in (
            "g_ready", "gsum_done", "gsum_read", "rows_done", "at_ready"))
        tt_ready, t_ready, off_ready, y_ps, y_sb, d_ps, dt_ps = (sem(n) for n in (
            "tt_ready", "t_ready", "off_ready", "y_ps", "y_sb", "d_ps", "dt_ps"))
        kv_ps, kv_sb, wu_ps, wu_sb, state_ready, ws_ps, u_ready = (sem(n) for n in (
            "kv_ps", "kv_sb", "wu_ps", "wu_sb", "state_ready", "ws_ps", "u_ready"))
        ds_ps, o_sb, o_ps, on_ready, ot_ps, yt_ready, yt_hi, yt_lo = (sem(n) for n in (
            "ds_ps", "o_sb", "o_ps", "on_ready", "ot_ps", "yt_ready", "yt_hi", "yt_lo"))
        conv_base, conv_step, silu_done, dec_pre, dec_exp, sig_ready, soft = (sem(n) for n in (
            "conv_base", "conv_step", "silu_done", "dec_pre", "dec_exp", "sig_ready", "soft"))
        qd_ready, row_exp, gc_saved, o_sq, o_root, o_ms = (sem(n) for n in ("qd_ready", "row_exp", "gc_saved", "o_sq", "o_root", "o_ms"))


        def ring(ph, c):
            return (RING0[ph] + c) % 4

        def bank_ready(pe, ph, c, i=0):
            pe.wait_ge(bank_free, RING0[ph] + c + 1 + i * 4)

        def seg_ready(eng, ph, s, i=0, per=4):
            eng.wait_ge(seg_done, SEG0[ph] + s + 1 + i * per)

        def feature_major(pe, ph, xh, xl, first_wait=None):
            def body(i, last):
                for b in range(2):
                    weights_ready(pe, ph, i, b)
                    for s in range(2):
                        c = 2 * b + s
                        bank_ready(pe, ph, c, i)
                        product(ps[:, ring(ph, c), :], b, 8 * s, DC, xh, xl).then_inc(seg_done, 1)
            pairs(pe, ph, body)

        def gdn_pe(pe):
            pe.wait_ge(ws_split, 2)
            for t in range(T):
                for k in range(DC):
                    tok = slice(t * P, (t + 1) * P)
                    w = slice(k * 32, (k + 1) * 32)
                    nc.tensor.matmul(ps[:, 4, t * 32:(t + 1) * 32], AH[:, k, tok], WSH[:, w], start=k == 0, stop=False)
                    nc.tensor.matmul(ps[:, 4, t * 32:(t + 1) * 32], AL[:, k, tok], WSH[:, w], start=False, stop=False)
                    last = nc.tensor.matmul(ps[:, 4, t * 32:(t + 1) * 32], AH[:, k, tok], WSL[:, w], start=False,
                                            stop=k == DC - 1)
            last.then_inc(small_done, 1)
            for n in range(2):
                pe.wait_ge(l2_sq, n + 1)
                if n:
                    pe.wait_ge(l2_root, n)
                else:
                    pe.wait_ge(sm_saved, 1)
                for h in range(GH):
                    last = nc.tensor.matmul(ps[:, 4 + h, :], ones[:, :], Tm[:, h, :, :], start=True, stop=True)
                last.then_inc(l2_sum, 1)
            pe.wait_ge(g_ready, 1)
            pe.wait_ge(bank_free, RING0["nq"] + 4)
            for n, c0 in enumerate((CON["tri"], CON["after"], CON["half"], CON["half"] + P)):
                last = nc.tensor.matmul(ps[:, 0, n * 16:(n + 1) * 16], CS[:, c0:c0 + P],
                                        G[:, :, :].rearrange("p t h -> p (t h)"), start=True, stop=True)
            last.then_inc(gsum_done, 1)
            pe.wait_ge(l2_done, 2)
            for t in range(T):
                tok = slice(t * P, (t + 1) * P)
                o = 4 * (t % 2)
                if t == 0:
                    pe.wait_ge(gc_saved, 1)
                elif t >= 2:
                    pe.wait_ge(at_ready, t - 1)
                for h in range(GH):
                    f = slice(h * P, (h + 1) * P)
                    nc.tensor.matmul(ps[:, o, f], G[:, t, h:h + 1].to_broadcast([P, P]), CS[:, 0:P], start=True, stop=True)
                    nc.tensor.matmul(ps[:, o + 1, f], SG[:, t, h:h + 1].to_broadcast([P, P]), ident[:, :], start=True, stop=True)
                    nc.tensor.matmul(ps[:, o + 2, f], QKV[:, 4 + h, tok], QKV[:, 4 + h, tok], start=True, stop=True)
                    last = nc.tensor.matmul(ps[:, o + 3, f], QKV[:, 4 + h, tok], QKV[:, h, tok], start=True, stop=True)
                last.then_inc(rows_done, 1)
            pe.wait_ge(at_ready, T)
            for t in range(T):
                pe.wait_ge(tt_ready, t + 1)
                for h in range(GH):
                    last = nc.tensor.transpose(ps[:, t, h * P:(h + 1) * P], TT[:, t, h, :], ident[:, :])
                last.then_inc(y_ps, 1)
            for lev in range(1, 6):
                for t in range(T):
                    n = 4 * lev + t
                    pe.wait_ge(off_ready, n - 3)
                    pe.wait_ge(t_ready, n - 3)
                    pe.wait_ge(tt_ready, n - 3)
                    for h in range(GH):
                        last = nc.tensor.matmul(ps[:, t, h * P:(h + 1) * P], OFF[:, t, h, :], Tm[:, t, h, :], start=True, stop=True)
                    last.then_inc(y_ps, 1)
                for t in range(T):
                    n = 4 * lev + t
                    pe.wait_ge(y_sb, n + 1 - 4)
                    pe.wait_ge(tt_ready, n - 3)
                    for h in range(GH):
                        last = nc.tensor.matmul(ps[:, 4 + t, h * P:(h + 1) * P], TT[:, t, h, :], Y1[:, t, h, :], start=True, stop=True)
                    last.then_inc(d_ps, 1)
                    for h in range(GH):
                        last = nc.tensor.matmul(ps[:, t, h * P:(h + 1) * P], Y1[:, t, h, :], TT[:, t, h, :], start=True, stop=True)
                    last.then_inc(dt_ps, 1)
            for t in range(T):
                tok = slice(t * P, (t + 1) * P)
                pe.wait_ge(tt_ready, 20 + t + 1)
                for n in range(2):
                    for h in range(GH):
                        last = nc.tensor.transpose(ps[:, 4 * n + t, h * P:(h + 1) * P], QKV[:, 4 + 4 * n + h, tok], ident[:, :])
                last.then_inc(kv_ps, 1)
            for t in range(T):
                pe.wait_ge(kv_sb, t + 1)
                for h in range(GH):
                    nc.tensor.matmul(ps[:, t, h * P:(h + 1) * P], OFF[:, t, h, :], TT[:, t, h, :], start=True, stop=True)
                    last = nc.tensor.matmul(ps[:, 4 + t, h * P:(h + 1) * P], TT[:, t, h, :], AT[:, t, h, :], start=True, stop=True)
                last.then_inc(wu_ps, 1)
            pe.wait_ge(wu_sb, 2 * T)
            for c in range(S // C):
                t, r = c // 2, C * (c % 2)
                rows, tok = slice(r, r + C), slice(c * C, (c + 1) * C)
                pe.wait_ge(state_ready, c + 1)
                for h in range(GH):
                    last = nc.tensor.matmul(ps[rows, 0, h * P:(h + 1) * P], Tm[:, t, h, rows], ST[:, c % 2, h, :], start=True, stop=True)
                last.then_inc(ws_ps, 1)
                pe.wait_ge(u_ready, c + 1)
                for h in range(GH):
                    last = nc.tensor.matmul(ps[:, 1 + c % 2, h * P:(h + 1) * P], QKV[rows, 8 + h, t * P:(t + 1) * P],
                                            Y1[rows, t, h, :], start=True, stop=True)
                last.then_inc(ds_ps, 1)
                if c >= 2:
                    pe.wait_ge(o_sb, c - 1)
                for h in range(GH):
                    nc.tensor.matmul(ps[rows, 3 + c % 2, h * P:(h + 1) * P], QKV[:, h, tok], ST[:, c % 2, h, :], start=True, stop=False)
                    last = nc.tensor.matmul(ps[rows, 3 + c % 2, h * P:(h + 1) * P], QK[rows, t, h, rows], Y1[rows, t, h, :],
                                            start=False, stop=True)
                last.then_inc(o_ps, 1)
            for t in range(T):
                pe.wait_ge(on_ready, t + 1)
                for h in range(GH):
                    last = nc.tensor.transpose(ps[:, 5 + t % 2, h * P:(h + 1) * P], AT[:, t, h, :], ident[:, :])
                last.then_inc(ot_ps, 1)
                if t >= 1:
                    pe.wait_ge(yt_ready, t)


        def flat(x):
            return x.rearrange("p a b -> p (a b)")

        def flat4(x):
            return x.rearrange("p a b c -> p (a b c)")

        def chunks(x, c, i, n=1):
            return x[:, c + 4 * i:c + 4 * i + n, :] if isinstance(i, int) else x[:, bass.ds(c + i * 4, n), :]

        def bank_read(eng, ph, c, i=0):
            eng.wait_ge(bank_free, 4 + RING0[ph] + c + 1 + i * 4)

        def qkv_act(act):
            def body(i, last):
                for b in range(2):
                    for s in range(2):
                        c = 2 * b + s
                        seg_ready(act, "qkv", c, i)
                        nc.scalar.mul(flat(Tm[:, c, :, :]), ps[:, ring("qkv", c), :],
                                      col("cqkv", (c * 4 + 3) + i * 16)).then_inc(conv_base, 1)
                    for s in range(2):
                        c = 2 * b + s
                        bank_read(act, "qkv", c, i)
                        nc.scalar.activation(chunks(QKV, c, i), Tm[:, c:c + 1, :, :].rearrange("p c a b -> p c (a b)"),
                                             ACT.Silu).then_inc(silu_done, 1)
                    stage_hi(act, "qkv", i, b, last)
            pairs(act, "qkv", body)

        def z_act(act):
            act.wait_ge(con_landed, 16 * N_CON)
            nc.scalar.activation(WSH[:, :], WSR[:, :], ACT.Copy).then_inc(ws_split, 1)
            for c in range(4):
                seg_ready(act, "z", c)
                nc.scalar.activation(ZS[:, c, :], ps[:, ring("z", c), :], ACT.Silu).then_inc(bank_free, 1)
                if c % 2:
                    stage_hi(act, "z", 0, c // 2, True)

        def gdn_act(act):
            act.wait_ge(small_done, 1)
            nc.scalar.activation(flat(SM[:, :, :]), ps[:, 4, 0:T * 32], ACT.Copy).then_inc(sm_saved, 1)
            for n in range(2):
                act.wait_ge(silu_done, 12) if n == 0 else act.wait_ge(l2_sum, 1)
                nc.scalar.activation(flat4(Tm[:, :, :, :]), flat(QKV[:, 4 * n:4 * n + 4, :]), ACT.Square).then_inc(l2_sq, 1)
                act.wait_ge(l2_sum, n + 1)
                if n:
                    act.wait_ge(l2_done, n)
                nc.scalar.activation(flat4(TT[:, :, :, :]), flat(ps[:, 4:8, :]), ACT.Sqrt, bias=col("eps")).then_inc(l2_root, 1)
            nc.scalar.activation(EA[:, :], col("alog", 0, 4), ACT.Exp).then_inc(soft, 1)
            act.wait_ge(sm_saved, 1)
            nc.scalar.activation(SG[:, :, :], SM[:, :, :], ACT.Tanh, scale=0.5).then_inc(sig_ready, 1)
            act.wait_ge(soft, 2)
            nc.scalar.activation(AA[:, 1, :, :], AA[:, 1, :, :], ACT.Exp, scale=-1.0).then_inc(soft, 1)
            act.wait_ge(soft, 4)
            nc.scalar.activation(AA[:, 1, :, :], AA[:, 1, :, :], ACT.Ln).then_inc(soft, 1)
            act.wait_ge(gsum_done, 1)
            nc.scalar.activation(flat4(EX[:, :, :, :]), ps[:, 0, 0:64], ACT.Exp).then_inc(gsum_read, 1)
            for t in range(T):
                o = 4 * (t % 2)
                act.wait_ge(dec_pre, t + 1)
                nc.scalar.activation(flat(Y1[:, t, :, :]), ps[:, o, :], ACT.Exp).then_inc(row_exp, 1)
                nc.scalar.activation(Tm[:, t, :, :], Tm[:, t, :, :], ACT.Exp).then_inc(dec_exp, 1)
            for t in range(T):
                act.wait_ge(y_ps, t + 1)
                nc.scalar.activation(flat(Tm[:, t, :, :]), ps[:, t, :], ACT.Copy).then_inc(t_ready, 1)
            act.wait_ge(qd_ready, T)
            for lev in range(1, 6):
                for t in range(T):
                    act.wait_ge(y_ps, 4 * lev + t + 1)
                    nc.scalar.activation(flat(Y1[:, t, :, :]), ps[:, t, :], ACT.Copy).then_inc(y_sb, 1)
            for t in range(T):
                act.wait_ge(wu_ps, t + 1)
                nc.scalar.activation(flat(Tm[:, t, :, :]), ps[:, t, :], ACT.Copy).then_inc(wu_sb, 1)
                nc.scalar.activation(flat(Y1[:, t, :, :]), ps[:, 4 + t, :], ACT.Copy).then_inc(wu_sb, 1)
            for c in range(S // C):
                t, rows = c // 2, slice(C * (c % 2), C * (c % 2) + C)
                act.wait_ge(o_ps, c + 1)
                nc.scalar.activation(flat(AT[rows, t, :, :]), ps[rows, 3 + c % 2, :], ACT.Copy).then_inc(o_sb, 1)
                if c % 2:
                    act.wait_ge(o_sb, c + 1)
                    nc.scalar.activation(OFF[:, t, :, :], AT[:, t, :, :], ACT.Square).then_inc(o_sq, 1)
            act.wait_ge(o_ms, 1)
            nc.scalar.activation(RO[:, :, :], RO[:, :, :], ACT.Sqrt).then_inc(o_root, 1)
            for t in range(T):
                act.wait_ge(yt_ready, t + 1)
                nc.scalar.activation(YAH[:, :, t * P:(t + 1) * P], TMP[:, t % 2, :].rearrange("p (h n) -> p h n", h=GH),
                                     ACT.Copy).then_inc(yt_hi, 1)

        def qkv_dve(dve):
            def body(i, last):
                for b in range(2):
                    for s in range(2):
                        c = 2 * b + s
                        y = flat(Tm[:, c, :, :])
                        dve.wait_ge(conv_base, c + 1 + i * 4)
                        for j in range(1, 4):
                            if j > 1:
                                dve.wait_ge(conv_step, 2 * c + j - 1 + i * 8)
                            nc.vector.scalar_tensor_tensor(
                                y[:, j:S], ps[:, ring("qkv", c), 0:S - j], col("cqkv", (c * 4 + 3 - j) + i * 16),
                                y[:, j:S], ALU.mult, ALU.add).then_inc(conv_step if j < 3 else bank_free, 1)
                    stage_lo(dve, "qkv", i, b, last)
            pairs(dve, "qkv", body)

        def z_dve(dve):
            dve.wait_ge(ws_split, 1)
            nc.vector.tensor_tensor(WSL[:, :], WSR[:, :], WSH[:, :].bitcast(F32), ALU.subtract).then_inc(ws_split, 1)
            for b in range(2):
                stage_lo(dve, "z", 0, b, True)

        def gdn_dve(dve, own):
            vec = nc.vector
            for n in range(2):
                dve.wait_ge(l2_root, n + 1)
                vec.reciprocal(flat4(TT[:, :, :, :]), flat4(TT[:, :, :, :])).then_inc(l2_rec, 1)
                dve.wait_ge(l2_rec, n + 1)
                x = flat(QKV[:, 4 * n:4 * n + 4, :])
                vec.scalar_tensor_tensor(x, x, float(P) ** -0.5 if n == 0 else 1.0, flat4(TT[:, :, :, :]),
                                         ALU.mult, ALU.mult).then_inc(l2_done, 1)
            dve.wait_ge(sig_ready, 1)
            own.mark(vec.tensor_scalar(SG[:, :, :], SG[:, :, :], 0.5, 0.5, ALU.mult, ALU.add))
            dtb = col("dtb", 0, 4).unsqueeze(1).to_broadcast([P, T, GH])
            own.link(vec.tensor_tensor(AA[:, 0, :, :], SM[:, :, 4:8], dtb, ALU.add))
            own.link(vec.tensor_scalar(AA[:, 2, :, :], AA[:, 0, :, :], -1.0, None, ALU.mult))
            vec.tensor_tensor(AA[:, 1, :, :], AA[:, 0, :, :], AA[:, 2, :, :], ALU.max).then_inc(soft, 1)
            dve.wait_ge(soft, 3)
            vec.tensor_scalar(AA[:, 1, :, :], AA[:, 1, :, :], 1.0, None, ALU.add).then_inc(soft, 1)
            dve.wait_ge(soft, 5)
            own.link(vec.scalar_tensor_tensor(AA[:, 0, :, :], AA[:, 0, :, :], 0.0, AA[:, 1, :, :], ALU.max, ALU.add))
            ea = EA[:, :].unsqueeze(1).to_broadcast([P, T, GH])
            vec.scalar_tensor_tensor(G[:, :, :], AA[:, 0, :, :], -1.0, ea, ALU.mult, ALU.mult).then_inc(g_ready, 1)
            dve.wait_ge(gsum_read, 1)
            vec.tensor_copy(flat(GC[:, :, :]), ps[:, 0, 0:16]).then_inc(gc_saved, 1)
            dve.wait_ge(gc_saved, 1)
            own.link(vec.tensor_tensor(BG[:, :, :], SG[:, :, 0:GH], EX[:, 0, :, :], ALU.mult))
            nc.vector.memset(ST[:, :, :, :], 0.0).then_inc(state_ready, 1)
            for t in range(T):
                o, tok = 4 * (t % 2), slice(t * P, (t + 1) * P)
                dve.wait_ge(rows_done, t + 1)
                for h in range(GH):
                    ins = vec.tensor_scalar(Tm[:, t, h, :], ps[:, o, h * P:(h + 1) * P], GC[:, t, h:h + 1], 0.0,
                                            ALU.subtract, ALU.min)
                ins.then_inc(dec_pre, 1)
                dve.wait_ge(row_exp, t + 1)
                qd = QKV[:, 0:GH, tok]
                vec.tensor_tensor(qd, qd, Y1[:, t, :, :], ALU.mult).then_inc(qd_ready, 1)
                dve.wait_ge(dec_exp, t + 1)
                incl = CS[:, CON["tri"]:CON["tri"] + P].unsqueeze(1).to_broadcast([P, GH, P])
                own.link(vec.tensor_tensor(Tm[:, t, :, :], Tm[:, t, :, :], incl, ALU.mult))
                own.mark(vec.tensor_tensor(flat(QK[:, t, :, :]), ps[:, o + 3, :], flat(Tm[:, t, :, :]), ALU.mult))
                own.link(vec.tensor_tensor(flat(AT[:, t, :, :]), ps[:, o + 2, :], flat(Tm[:, t, :, :]), ALU.mult))
                vec.tensor_tensor(flat(AT[:, t, :, :]), flat(AT[:, t, :, :]), ps[:, o + 1, :], ALU.mult).then_inc(at_ready, 1)
            level = [CS[:, CON["level"] + n * P:CON["level"] + (n + 1) * P].unsqueeze(1).to_broadcast([P, GH, P])
                     for n in range(6)]
            eye = ident[:, :].unsqueeze(1).to_broadcast([P, GH, P])
            for t in range(T):
                dve.wait_ge(at_ready, t + 1)
                own.link(vec.tensor_tensor(TT[:, t, :, :], AT[:, t, :, :], level[0], ALU.mult))
                vec.scalar_tensor_tensor(TT[:, t, :, :], TT[:, t, :, :], -1.0, eye, ALU.mult, ALU.add).then_inc(tt_ready, 1)
            for lev in range(1, 6):
                for t in range(T):
                    n = 4 * lev + t
                    if lev < 5:
                        dve.wait_ge(d_ps, n - 3)
                        vec.tensor_tensor(flat(Tm[:, t, :, :]), flat(Tm[:, t, :, :]), ps[:, 4 + t, :],
                                          ALU.subtract).then_inc(t_ready, 1)
                    dve.wait_ge(dt_ps, n - 3)
                    vec.tensor_tensor(flat(TT[:, t, :, :]), flat(TT[:, t, :, :]), ps[:, t, :],
                                      ALU.subtract).then_inc(tt_ready, 1)
            for t in range(T):
                tok = slice(t * P, (t + 1) * P)
                wide = lambda x: x.unsqueeze(2).to_broadcast([P, GH, P])
                heads = lambda x: x.rearrange("p (h n) -> p h n", h=GH)
                dve.wait_ge(kv_ps, t + 1)
                vec.tensor_tensor(OFF[:, t, :, :], heads(ps[:, t, :]), wide(BG[:, t, :]), ALU.mult)
                vec.tensor_tensor(AT[:, t, :, :], heads(ps[:, 4 + t, :]), wide(SG[:, t, 0:GH]), ALU.mult)
                vec.tensor_tensor(QKV[:, 8:12, tok], heads(ps[:, t, :]), wide(EX[:, 1, t, :]), ALU.mult).then_inc(kv_sb, 1)
            for c in range(S // C):
                t, rows = c // 2, slice(C * (c % 2), C * (c % 2) + C)
                dve.wait_ge(ws_ps, c + 1)
                u = flat(Y1[rows, t, :, :])
                vec.tensor_tensor(u, u, ps[rows, 0, :], ALU.subtract).then_inc(u_ready, 1)
                dve.wait_ge(ds_ps, c + 1)
                if c:
                    dve.wait_ge(o_ps, c)
                for h in range(GH):
                    ins = vec.scalar_tensor_tensor(ST[:, (c + 1) % 2, h, :], ST[:, c % 2, h, :], EX[:, 2 + c % 2, t, h:h + 1],
                                                   ps[:, 1 + c % 2, h * P:(h + 1) * P], ALU.mult, ALU.add)
                ins.then_inc(state_ready, 1)
            for t in range(T):
                dve.wait_ge(o_sq, t + 1)
                ins = vec.tensor_reduce(RO[:, t, :], OFF[:, t, :, :], AX, ALU.add)
            own.link(ins)
            vec.tensor_scalar(RO[:, :, :], RO[:, :, :], 1.0 / P, EPS, ALU.mult, ALU.add).then_inc(o_ms, 1)
            dve.wait_ge(o_root, 1)
            own.link(vec.reciprocal(RO[:, :, :], RO[:, :, :]))
            for t in range(T):
                vec.tensor_tensor(AT[:, t, :, :], AT[:, t, :, :], RO[:, t, :].unsqueeze(2).to_broadcast([P, GH, P]),
                                  ALU.mult).then_inc(on_ready, 1)
            for t in range(T):
                tok = slice(t * P, (t + 1) * P)
                dve.wait_ge(ot_ps, t + 1)
                tmp = TMP[:, t % 2, :].rearrange("p (h n) -> p h n", h=GH)
                if t >= 2:
                    dve.wait_ge(yt_lo, t - 1)
                vec.scalar_tensor_tensor(tmp, ps[:, 5 + t % 2, :].rearrange("p (h n) -> p h n", h=GH), col("gdn"),
                                         ZS[:, :, tok], ALU.mult, ALU.mult).then_inc(yt_ready, 1)
                dve.wait_ge(yt_hi, t + 1)
                vec.tensor_tensor(YAL[:, :, tok], tmp, YAH[:, :, tok].bitcast(F32), ALU.subtract).then_inc(yt_lo, 1)

        def gdn_pool(pool):
            for lev in range(1, 6):
                m = CS[:, CON["level"] + lev * P:CON["level"] + (lev + 1) * P].unsqueeze(1).to_broadcast([P, GH, P])
                for t in range(T):
                    pool.wait_ge(at_ready, T)
                    if lev > 1:
                        pool.wait_ge(y_ps, 4 * (lev - 1) + t + 1)
                    nc.gpsimd.tensor_tensor(OFF[:, t, :, :], AT[:, t, :, :], m, ALU.mult).then_inc(off_ready, 1)

        comp_ready, z_ready, hid_ps, hid_ready, kv_c_ps, kv_c_sb = (sem(n) for n in (
            "comp_ready", "z_ready", "hid_ps", "hid_ready", "kv_c_ps", "kv_c_sb"))
        cs_ps, cs_max, cs_exp, cs_pr, cp_ps, cp_sb, co_ps, co_done = (sem(n) for n in (
            "cs_ps", "cs_max", "cs_exp", "cs_pr", "cp_ps", "cp_sb", "co_ps", "co_done"))
        s_ps, s_max, p_ready, pt_ps, pt_sb, o2_ps, o2_done = (sem(n) for n in (
            "s_ps", "s_max", "p_ready", "pt_ps", "pt_sb", "o2_ps", "o2_done"))
        yb_ps, yb_hi, yb_lo, mb_ready = (sem(n) for n in ("yb_ps", "yb_hi", "yb_lo", "mb_ready"))
        gate_ready, mix_sum, mix_hi, mix_lo, mix_ab = (sem(n) for n in (
            "gate_ready", "mix_sum", "mix_hi", "mix_lo", "mix_ab"))
        UNITS = [(qt, h) for qt in range(T) for h in range(NH)]

        def nsa_proj_pe(pe):
            feature_major(pe, "nq", AH, AL)
            for b in range(2):
                weights_ready(pe, "ncmp", 0, b)
                bank_ready(pe, "ncmp", b)
                product(ps[:, ring("ncmp", b), :], b, 0, DC, AH, AL).then_inc(seg_done, 1)
            weights_ready(pe, "nk", 0, 0)
            for s in range(2):
                bank_ready(pe, "nk", s)
                product(ps[:, ring("nk", s), :], 0, 8 * s, DC, AH, AL).then_inc(seg_done, 1)
            pe.wait_ge(w_lo_done, PIECE0["nv"] + 1)
            for t in range(T):
                tok, c = slice(t * P, (t + 1) * P), t // 2
                if t % 2 == 0:
                    bank_ready(pe, "nv", c)
                o = ps[:, ring("nv", c), (t % 2) * 256:(t % 2) * 256 + 256]
                for k in range(DC):
                    w = slice(k * 256, (k + 1) * 256)
                    nc.tensor.matmul(o, AH[:, k, tok], WH[1][:, w], start=k == 0, stop=False)
                    nc.tensor.matmul(o, AL[:, k, tok], WH[1][:, w], start=False, stop=False)
                    last = nc.tensor.matmul(o, AH[:, k, tok], WL[1][:, w], start=False, stop=k == DC - 1)
                if t % 2:
                    last.then_inc(seg_done, 1)

        def nsa_proj_act(act):
            for b in range(2):
                stage_hi(act, "nq", 0, b, True)
            for b in range(2):
                stage2_hi(act, "ncmp", b)
            stage2_hi(act, "nk", 0)
            stage2_hi(act, "nv", 1)

        def nsa_proj_dve(dve):
            for m in range(4):
                seg_ready(dve, "nq", m)
                for s in range(2):
                    ins = nc.vector.tensor_scalar(QT[0:DK, 2 * m + s, :], ps[s * DK:(s + 1) * DK, ring("nq", m), :],
                                                  DK ** -0.5, None, ALU.mult)
                ins.then_inc(bank_free, 1)
                if m % 2:
                    stage_lo(dve, "nq", 0, m // 2, True)
            dve.wait_ge(cols_landed, 16)
            for x in range(2):
                dve.wait_ge(seg_done, SEG0["ncmp"] + x + 1)
                pos = cols[:, COLS["posk" if x == 0 else "posv"]:][:, 0:16]
                for g in range(NG):
                    src = ps[g * DK:(g + 1) * DK, ring("ncmp", x), :].rearrange("p (n k j) -> p j k n", k=8, j=2)
                    for par in range(2):
                        half = slice(par * DK, (par + 1) * DK)
                        for late in range(2):
                            ins = nc.vector.tensor_tensor(
                                Z[x][half, 8 * late:8 * late + 8, g * NC:(g + 1) * NC],
                                src[:, par, :, late:late + NC],
                                pos[half, 8 * late:8 * late + 8].unsqueeze(2).to_broadcast([DK, 8, NC]), ALU.add)
                ins.then_inc(bank_free, 1)
                stage2_lo(dve, "ncmp", x)
            for x in range(2):
                seg_ready(dve, "nk", x)
                for g in range(NG):
                    ins = nc.vector.tensor_copy(KT[0:DK, x, g, :], ps[g * DK:(g + 1) * DK, ring("nk", x), :])
                ins.then_inc(bank_free, 1)
            stage2_lo(dve, "nk", 0)
            for c in range(2):
                seg_ready(dve, "nv", c)
                nc.vector.tensor_copy(flat(V1[:, 2 * c:2 * c + 2, :]), ps[:, ring("nv", c), :]).then_inc(bank_free, 1)
            stage2_lo(dve, "nv", 1)

        def stage2_hi(act, ph, b):
            piece = PIECE0[ph] + (b if NPIECE[ph] > 1 else 0)
            n = PIECE_NB[piece + 2] * P
            act.wait_ge(raw_landed[b], 16 * ((piece + 2) // 2 + 1))
            act.wait_ge(seg_done, PIECE_SEG[piece + 1])
            nc.scalar.activation(WH[b][:, 0:n], RAW[b][:, 0:n], ACT.Copy).then_inc(w_hi_done, 1)

        def stage2_lo(dve, ph, b):
            piece = PIECE0[ph] + (b if NPIECE[ph] > 1 else 0)
            n = PIECE_NB[piece + 2] * P
            dve.wait_ge(w_hi_done, piece + 3)
            nc.vector.tensor_tensor(WL[b][:, 0:n], RAW[b][:, 0:n], WH[b][:, 0:n].bitcast(F32),
                                    ALU.subtract).then_inc(w_lo_done, 1)

        def nsa_pe(pe):
            pe.wait_ge(w1_landed, 32)
            pe.wait_ge(nsa_landed, 16 * N_NSA)
            pe.wait_ge(bank_free, 4 + RING0["mix"])
            for x in range(2):
                for f in range(2):
                    o = ps[:, 4, (2 * x + f) * 64:(2 * x + f) * 64 + 2 * NC]
                    for k in range(16):
                        last = nc.tensor.matmul(o, W1[x][:, k, f * P:(f + 1) * P], Z[x][:, k, :], start=k == 0, stop=k == 15)
            last.then_inc(hid_ps, 1)
            pe.wait_ge(hid_ready, 1)
            for f in range(2):
                nc.tensor.matmul(ps[0:DK, 5, 0:2 * NC], W2[:, f, :], HID[:, f, :], start=f == 0, stop=f == 1)
            for g in range(NG):
                for r in range(R):
                    for f in range(2):
                        last = nc.tensor.matmul(ps[32 * r:32 * r + NC, 6 + g, 0:DK], HID[:, 2 + f, g * NC:(g + 1) * NC],
                                                W2[:, 2 + f, :], start=f == 0, stop=f == 1)
            last.then_inc(kv_c_ps, 1)
            pe.wait_ge(kv_c_sb, 1)
            for qt in range(T):
                for h in range(NH):
                    last = nc.tensor.matmul(ps[:, qt // 2, (qt % 2) * 256 + h * 32:(qt % 2) * 256 + h * 32 + 32],
                                            QT[0:66, h, qt * P:(qt + 1) * P], KC[0:66, h // R, :], start=True, stop=True)
            last.then_inc(cs_ps, 1)
            pe.wait_ge(cs_pr, 1)
            for qt in range(T):
                for g in range(NG):
                    j = (qt % 2) * 2 + g
                    last = nc.tensor.transpose(ps[:, 2 + qt // 2, j * P:(j + 1) * P],
                                               SC[:, qt, g * R:(g + 1) * R, :].rearrange("p a b -> p (a b)"), ident[:, :])
            last.then_inc(cp_ps, 1)
            pe.wait_ge(cp_sb, 1)
            for qt in range(T):
                for g in range(NG):
                    j = (qt % 2) * 2 + g
                    last = nc.tensor.matmul(ps[:, 4 + qt, g * 256:(g + 1) * 256], PT[:, 0, qt // 2, j * P:(j + 1) * P],
                                            VB[:, g, :], start=True, stop=True)
            last.then_inc(co_ps, 1)
            def scores(u):
                qt, h = UNITS[u]
                n = (qt + 1) * P
                pe.wait_ge(p_ready, 2 * (u - 1)) if u >= 2 else pe.wait_ge(cp_sb, 1)
                for x in range(2):
                    bank = 2 * (u % 2) + x
                    nc.tensor.matmul(ps[:, bank, 0:n], QT[0:66, h, qt * P:n], KT[0:66, x, h // R, 0:n], start=True, stop=False)
                    last = nc.tensor.matmul(ps[:, bank, qt * P:n], MB[:, 0, :], MB[:, 1, :], start=False, stop=True)
                last.then_inc(s_ps, 1)

            def turn(u):
                qt, h = UNITS[u]
                pe.wait_ge(p_ready, 2 * (u + 1))
                pe.wait_ge(pt_sb, u) if u else pe.wait_ge(co_done, 1)
                for x in range(2):
                    for kt in range(qt + 1):
                        last = nc.tensor.transpose(ps[:, 4 + x, kt * P:(kt + 1) * P], PR[:, u % 2, x, kt * P:(kt + 1) * P], ident[:, :])
                last.then_inc(pt_ps, 1)

            def values(u):
                qt, h = UNITS[u]
                g = h // R
                pe.wait_ge(pt_sb, u + 1)
                if u >= 2:
                    pe.wait_ge(o2_done, u - 1)
                for x in range(2):
                    for kt in range(qt + 1):
                        last = nc.tensor.matmul(ps[:, 6 + u % 2, x * DK:(x + 1) * DK], PT[:, u % 2, x, kt * P:(kt + 1) * P],
                                                V1[:, kt, x * P + g * DK:x * P + (g + 1) * DK], start=kt == 0, stop=kt == qt)
                last.then_inc(o2_ps, 1)

            pe.wait_ge(mb_ready, 2)
            n = len(UNITS)
            scores(0)
            for u in range(n + 1):
                if u + 1 < n:
                    scores(u + 1)
                if u < n:
                    turn(u)
                if u:
                    values(u - 1)
            pe.wait_ge(o2_done, n)
            for qt in range(T):
                for c in range(4):
                    last = nc.tensor.transpose(ps[:, qt, c * P:(c + 1) * P], Y[:, qt, c * P:(c + 1) * P], ident[:, :])
                last.then_inc(yb_ps, 1)

        def nsa_act(act):
            act.wait_ge(hid_ps, 1)
            nc.scalar.activation(HID[:, :, :], ps[:, 4, 0:256].rearrange("p (a n) -> p a n", a=4)[:, :, 0:2 * NC],
                                 ACT.Gelu_apprx_tanh).then_inc(hid_ready, 1)
            act.wait_ge(cs_max, 1)
            nc.scalar.activation(SC[:, :, :, :], SC[:, :, :, :], ACT.Exp).then_inc(cs_exp, 1)
            for u, (qt, h) in enumerate(UNITS):
                n = (qt + 1) * P
                act.wait_ge(s_max, u + 1)
                if u >= 2:
                    act.wait_ge(pt_ps, u - 1)
                    act.wait_ge(o2_done, u - 1)
                for x in range(2):
                    nc.scalar.activation(PR[:, u % 2, x, 0:n], ps[:, 2 * (u % 2) + x, 0:n], ACT.Exp,
                                         bias=NM[:, u % 2, x:x + 1], accum_out=LS[:, u % 2, x:x + 1]).then_inc(p_ready, 1)
            for qt in range(T):
                act.wait_ge(yb_ps, qt + 1)
                nc.scalar.activation(YBH[:, :, qt * P:(qt + 1) * P], ps[:, qt, :].rearrange("p (c n) -> p c n", c=4),
                                     ACT.Copy).then_inc(yb_hi, 1)

        def nsa_dve(dve, own):
            vec = nc.vector
            dve.wait_ge(nsa_landed, 16 * N_NSA)
            own.mark(vec.memset(KC[0:DK, :, :], 0.0))
            own.link(vec.memset(VB[:, :, :], 0.0))
            dve.wait_ge(kv_c_ps, 1)
            for g in range(NG):
                vec.tensor_copy(KC[0:DK, g, 0:NC], ps[0:DK, 5, g * NC:(g + 1) * NC])
                for r in range(R):
                    ins = vec.tensor_copy(VB[32 * r:32 * r + NC, g, r * DK:(r + 1) * DK], ps[32 * r:32 * r + NC, 6 + g, 0:DK])
            ins.then_inc(kv_c_sb, 1)
            dve.wait_ge(cs_ps, 1)
            rows = SC[:, :, :, :].rearrange("p t h n -> p (t h) n")
            for b in range(2):
                cn = CN[:, 2 * b:2 * b + 2, :].unsqueeze(2).to_broadcast([P, 2, NH, 32])
                ins = vec.tensor_tensor(SC[:, 2 * b:2 * b + 2, :, :], ps[:, b, :].rearrange("p (t h n) -> p t h n", t=2, h=NH),
                                        cn, ALU.add)
                own.mark(ins)
            own.wait()
            mx, l, gl = (SX[:, n, :, :].rearrange("p t h -> p (t h)") for n in range(3))
            own.link(vec.tensor_reduce(mx, rows, AX, ALU.max))
            vec.tensor_tensor(rows, rows, mx.unsqueeze(2).to_broadcast([P, T * NH, 32]), ALU.subtract).then_inc(cs_max, 1)
            dve.wait_ge(cs_exp, 1)
            c01 = C01[:, :, :].unsqueeze(2).to_broadcast([P, T, NH, 32])
            vec.tensor_tensor(SC[:, :, :, :], SC[:, :, :, :], c01, ALU.mult).then_inc(cs_pr, 1)
            dve.wait_ge(cs_pr, 1)
            own.link(vec.tensor_reduce(l, rows, AX, ALU.add))
            own.link(vec.tensor_scalar(l, l, 1e-30, None, ALU.max))
            own.link(vec.reciprocal(l, l))
            gate = lambda t, h, j: SG[:, t, 8 + 3 * h + j:8 + 3 * h + j + 1]
            own.link(vec.tensor_tensor(SX[:, 2, :, :], SX[:, 1, :, :],
                                       SG[:, :, 8:32].rearrange("p t (h j) -> p t h j", j=3)[:, :, :, 0], ALU.mult))
            dve.wait_ge(cp_ps, 1)
            vec.tensor_copy(PT[:, 0, :, :], ps[:, 2:4, :]).then_inc(cp_sb, 1)
            dve.wait_ge(co_ps, 1)
            for qt in range(T):
                ins = vec.tensor_tensor(Y[:, qt, :].rearrange("p (h d) -> p h d", h=NH),
                                        ps[:, 4 + qt, :].rearrange("p (h d) -> p h d", h=NH),
                                        SX[:, 2, qt, :].unsqueeze(2).to_broadcast([P, NH, DK]), ALU.mult)
            ins.then_inc(co_done, 1)
            dve.wait_ge(co_done, 1)

            def top(u):
                qt, h = UNITS[u]
                dve.wait_ge(s_ps, u + 1)
                vec.tensor_reduce(NM[:, u % 2, :], ps[:, 2 * (u % 2):2 * (u % 2) + 2, 0:(qt + 1) * P], AX, ALU.max,
                                  negate=True).then_inc(s_max, 1)

            def save(u):
                qt, h = UNITS[u]
                n = (qt + 1) * P
                dve.wait_ge(pt_ps, u + 1)
                if u >= 2:
                    dve.wait_ge(o2_ps, u - 1)
                vec.tensor_copy(PT[:, u % 2, :, 0:n], ps[:, 4:6, 0:n]).then_inc(pt_sb, 1)

            def add(u):
                qt, h = UNITS[u]
                b = u % 2
                dve.wait_ge(o2_ps, u + 1)
                own.link(vec.reciprocal(RL[:, b, :], LS[:, b, :]))
                own.link(vec.tensor_tensor(RL[:, b, :], RL[:, b, :], SG[:, qt, 9 + 3 * h:11 + 3 * h], ALU.mult))
                y = Y[:, qt, h * DK:(h + 1) * DK]
                own.link(vec.scalar_tensor_tensor(y, ps[:, 6 + b, 0:DK], RL[:, b, 0:1], y, ALU.mult, ALU.add))
                vec.scalar_tensor_tensor(y, ps[:, 6 + b, DK:2 * DK], RL[:, b, 1:2], y, ALU.mult, ALU.add).then_inc(o2_done, 1)

            top(0)
            for u in range(len(UNITS) + 1):
                if u + 1 < len(UNITS):
                    top(u + 1)
                if u < len(UNITS):
                    save(u)
                if u:
                    add(u - 1)
            for qt in range(T):
                tok = slice(qt * P, (qt + 1) * P)
                dve.wait_ge(yb_hi, qt + 1)
                vec.tensor_tensor(YBL[:, :, tok], ps[:, qt, :].rearrange("p (c n) -> p c n", c=4),
                                  YBH[:, :, tok].bitcast(F32), ALU.subtract).then_inc(yb_lo, 1)

        def mix_pe(pe):
            pe.wait_ge(yb_lo, T)
            pe.wait_ge(yt_lo, T)
            def body(i, last):
                for b in range(2):
                    weights_ready(pe, "mix", i, b)
                    y_h, y_l = (YAH, YAL) if b == 0 else (YBH, YBL)
                    bank_ready(pe, "mix", 2 * b, i)
                    product(ps[:, ring("mix", 2 * b), :], b, 0, DC, AH, AL).then_inc(seg_done, 1)
                    bank_ready(pe, "mix", 2 * b + 1, i)
                    product(ps[:, ring("mix", 2 * b + 1), :], b, DC, 4, y_h, y_l).then_inc(seg_done, 1)
            pairs(pe, "mix", body)

        def at(x, m):
            return x[:, m:m + 1, :] if isinstance(m, int) else x[:, bass.ds(m, 1), :]

        def mix_act(act):
            def body(i, last):
                for b in range(2):
                    seg_ready(act, "mix", 2 * b, i)
                    nc.scalar.activation(SQ[:, b, :], ps[:, ring("mix", 2 * b), :], ACT.Tanh, scale=0.5).then_inc(gate_ready, 1)
                    stage_hi(act, "mix", i, b, last)
                act.wait_ge(mix_sum, i + 1)
                nc.scalar.activation(at(GHI, i), TMP[:, 0:1, :], ACT.Copy, scale=0.5).then_inc(mix_hi, 1)
            pairs(act, "mix", body)

        def mix_dve(dve):
            def body(i, last):
                for b in range(2):
                    dve.wait_ge(gate_ready, b + 1 + i * 2)
                    seg_ready(dve, "mix", 2 * b + 1, i)
                    nc.vector.scalar_tensor_tensor(TMP[:, b, :], SQ[:, b, :], 1.0, ps[:, ring("mix", 2 * b + 1), :],
                                                   ALU.add, ALU.mult).then_inc(bank_free, 2)
                    stage_lo(dve, "mix", i, b, last)
                bank_read(dve, "mix", 3, i)
                nc.vector.tensor_tensor(TMP[:, 0, :], TMP[:, 0, :], TMP[:, 1, :], ALU.add).then_inc(mix_sum, 1)
                dve.wait_ge(mix_hi, i + 1)
                nc.vector.scalar_tensor_tensor(at(GLO, i), TMP[:, 0:1, :], 0.5, at(GHI, i).bitcast(F32),
                                               ALU.mult, ALU.subtract).then_inc(mix_lo, 1)
                dve.wait_ge(mix_lo, i + 1)
            pairs(dve, "mix", body)

        def wide_product(pe, ph, k, xh, xl, freed, count):
            for m in range(DC):
                if m % 2 == 0:
                    weights_ready(pe, ph, m // 4, m // 2 % 2)
                if m == 7:
                    pe.wait_ge(freed, count)
                product(y_bank(m), m // 2 % 2, 8 * (m % 2), DC, xh, xl).then_inc(seg_done, 1)
                if m:
                    add_squares(pe, k, m - 1)
            add_squares(pe, k, DC - 1)

        def square_at(act, k, m, par, src):
            act.wait_ge(sq_used, m + (8 * k - 1))
            nc.scalar.activation(SQ[:, par:par + 1, :], src, ACT.Square).then_inc(sq_ready, 1)

        def sum_at(pe, k, m, par, first=False, last=False):
            pe.wait_ge(sq_ready, m + (8 * k + 1))
            nc.tensor.matmul(ps[:, 7, :], ones[:, :], SQ[:, par, :], start=first, stop=last).then_inc(sq_used, 1)

        def down_pe(pe, ph, k, freed, count):
            def chunk(m, par, bank):
                for b in range(2):
                    weights_ready(pe, ph, m, b)
                    product(bank, b, 0, FC // 2, HH[:, b * 11:b * 11 + 11, :], HL[:, b * 11:b * 11 + 11, :],
                            start=b == 0, stop=b == 1).then_inc(seg_done, 1)
            chunk(0, 0, ps[:, 0:1, :])
            chunk(1, 1, ps[:, 1:2, :])
            sum_at(pe, k, 0, 0, first=True)
            with pe.Fori(0, 2) as i:
                chunk(i * 2 + 2, 0, ps[:, bass.ds(i * 2 + 2, 1), :])
                sum_at(pe, k, i * 2 + 1, 1)
                chunk(i * 2 + 3, 1, ps[:, bass.ds(i * 2 + 3, 1), :])
                sum_at(pe, k, i * 2 + 2, 0)
            chunk(6, 0, ps[:, 6:7, :])
            sum_at(pe, k, 5, 1)
            pe.wait_ge(freed, count)
            chunk(7, 1, ps[:, 0:1, :])
            sum_at(pe, k, 6, 0)
            sum_at(pe, k, 7, 1, last=True)

        def wo_act(act):
            for m in range(DC):
                seg_ready(act, "wo", m)
                square(act, 1, m, y_bank(m))
                if m % 2:
                    stage_hi(act, "wo", m // 4, m // 2 % 2, m >= 4)

        def wo_dve(dve):
            dve.wait_ge(sq_ready, 8 + 1)
            nc.vector.tensor_copy(YX[:, :], ps[:, 0, :]).then_inc(y0_saved, 1)
            for p in range(4):
                stage_lo(dve, "wo", p // 2, p % 2, p >= 2)

        def up_pe(pe, ph, j):
            pe.wait_ge(in_lo, 8 * j + 1)
            def body(i, last):
                for b in range(2):
                    weights_ready(pe, ph, i, b)
                    for s in range(2):
                        bank_ready(pe, ph, 2 * b + s, i)
                        product(ps[:, ring(ph, 2 * b + s), :], b, 8 * s, DC, AH, AL).then_inc(seg_done, 1)
            pairs(pe, ph, body)

        up_base, up_step, up_gelu, up_prod, hid_hi, hid_lo = (sem(n) for n in (
            "up_base", "up_step", "up_gelu", "up_prod", "hid_hi", "hid_lo"))

        def up_act(act):
            def body(i, last):
                for b in range(2):
                    for s, buf in enumerate((CG, CV)):
                        seg_ready(act, "up", 2 * b + s, i)
                        nc.scalar.activation(buf[:, b, :], ps[:, ring("up", 2 * b + s), :], ACT.Identity,
                                             bias=col("cffnb", (2 * b + s) + i * 4),
                                             scale=col("cffn", (6 * b + 3 * s + 2) + i * 12)).then_inc(up_base, 1)
                    stage_hi(act, "up", i, b, last)
                    bank_read(act, "up", 2 * b, i)
                    nc.scalar.activation(CG[:, b, :], CG[:, b, :], ACT.Gelu_apprx_tanh).then_inc(up_gelu, 1)
                    act.wait_ge(up_prod, b + 1 + i * 2)
                    nc.scalar.activation(at(HH, i * 2 + b), CG[:, b:b + 1, :], ACT.Copy).then_inc(hid_hi, 1)
            pairs(act, "up", body)

        def up_dve(dve):
            def body(i, last):
                for b in range(2):
                    for s, buf in enumerate((CG, CV)):
                        dve.wait_ge(up_base, 2 * b + s + 1 + i * 4)
                        for j in (1, 2):
                            if j == 2:
                                dve.wait_ge(up_step, 2 * b + s + 1 + i * 4)
                            nc.vector.scalar_tensor_tensor(
                                buf[:, b, j:S], ps[:, ring("up", 2 * b + s), 0:S - j],
                                col("cffn", (6 * b + 3 * s + 2 - j) + i * 12), buf[:, b, j:S], ALU.mult,
                                ALU.add).then_inc(up_step if j == 1 else bank_free, 1)
                    stage_lo(dve, "up", i, b, last)
                    bank_read(dve, "up", 2 * b + 1, i)
                    dve.wait_ge(up_gelu, b + 1 + i * 2)
                    nc.vector.tensor_tensor(CG[:, b, :], CG[:, b, :], CV[:, b, :], ALU.mult).then_inc(up_prod, 1)
                    dve.wait_ge(hid_hi, b + 1 + i * 2)
                    nc.vector.tensor_tensor(at(HL, i * 2 + b), CG[:, b:b + 1, :], at(HH, i * 2 + b).bitcast(F32),
                                            ALU.subtract).then_inc(hid_lo, 1)
            pairs(dve, "up", body)

        def up2_act(act):
            def body(i, last):
                for b in range(2):
                    seg_ready(act, "up2", 2 * b, i)
                    nc.scalar.activation(CG[:, b, :], ps[:, ring("up2", 2 * b), :], ACT.Silu).then_inc(up_gelu, 1)
                    stage_hi(act, "up2", i, b, last)
                    bank_read(act, "up2", 2 * b + 1, i)
                    nc.scalar.activation(at(HH, i * 2 + b), CG[:, b:b + 1, :], ACT.Copy).then_inc(hid_hi, 1)
            pairs(act, "up2", body)

        def up2_dve(dve):
            def body(i, last):
                for b in range(2):
                    dve.wait_ge(up_gelu, FC + b + 1 + i * 2)
                    seg_ready(dve, "up2", 2 * b + 1, i)
                    nc.vector.tensor_tensor(CG[:, b, :], CG[:, b, :], ps[:, ring("up2", 2 * b + 1), :],
                                            ALU.mult).then_inc(bank_free, 2)
                    stage_lo(dve, "up2", i, b, last)
                    dve.wait_ge(hid_hi, FC + b + 1 + i * 2)
                    nc.vector.tensor_tensor(at(HL, i * 2 + b), CG[:, b:b + 1, :], at(HH, i * 2 + b).bitcast(F32),
                                            ALU.subtract).then_inc(hid_lo, 1)
            pairs(dve, "up2", body)

        def down_chunks(eng, chunk):
            chunk(0, 0, False)
            with eng.Fori(0, 3) as i:
                chunk(i * 2 + 1, 1, False)
                chunk(i * 2 + 2, 0, False)
            chunk(7, 1, True)

        def down_seg(eng, ph, m):
            eng.wait_ge(seg_done, m * 2 + (SEG0[ph] + 2))

        def down_act(act):
            def chunk(m, par, last):
                stage_hi(act, "down", m, 0, last)
                down_seg(act, "down", m)
                square_at(act, 3, m, par, ps[:, 0:1, :] if last else at(ps, m))
                stage_hi(act, "down", m, 1, last)
            down_chunks(act, chunk)

        def down_dve(dve):
            def chunk(m, par, last):
                stage_lo(dve, "down", m, 0, last)
                if isinstance(m, int) and m == 0:
                    dve.wait_ge(sq_ready, 8 * 3 + 1)
                    nc.vector.tensor_copy(YX[:, :], ps[:, 0, :]).then_inc(y0_saved, 1)
                stage_lo(dve, "down", m, 1, last)
            down_chunks(dve, chunk)

        ph_ready, pl_ready, e_gate, e_half, e_ready = (sem(n) for n in (
            "ph_ready", "pl_ready", "e_gate", "e_half", "e_ready"))

        def ple_pe(pe):
            pe.wait_ge(pl_ready, 1)
            pe.wait_ge(in_lo, 8 * 2 + 1)
            for m in range(DC):
                b, i = m % 2, m // 2
                weights_ready(pe, "ple", i, b)
                bank_ready(pe, "ple", 2 * b, i)
                product(ps[:, ring("ple", 2 * b), :], b, 0, 2, PH, PL).then_inc(seg_done, 1)
                bank_ready(pe, "ple", 2 * b + 1, i)
                if m == 0:
                    pe.wait_ge(in_lo, 8 * 3)
                product(ps[:, ring("ple", 2 * b + 1), :], b, 2, DC, AH, AL).then_inc(seg_done, 1)
                if m:
                    add_squares(pe, 4, m - 1)
            add_squares(pe, 4, DC - 1)

        def ple_act(act):
            act.wait_ge(p_landed, 16)
            nc.scalar.activation(PH[:, :, :], PX[:, :, :], ACT.Copy).then_inc(ph_ready, 1)
            for m in range(DC):
                b, i = m % 2, m // 2
                seg_ready(act, "ple", 2 * b + 1, i)
                if m >= 2:
                    bank_read(act, "ple", 2 * b + 1, i - 1)
                nc.scalar.activation(GP[:, b, :], ps[:, ring("ple", 2 * b + 1), :], ACT.Tanh, scale=0.5).then_inc(e_gate, 1)
                stage_hi(act, "ple", i, b, m >= 6)
                act.wait_ge(bank_free, 4 + RING0["ple"] + 2 * m + 2)
                square(act, 4, m, E[:, m, :])

        def ple_dve(dve):
            dve.wait_ge(ph_ready, 1)
            nc.vector.tensor_tensor(PL[:, :, :], PX[:, :, :], PH[:, :, :].bitcast(F32), ALU.subtract).then_inc(pl_ready, 1)
            for m in range(DC):
                b, i = m % 2, m // 2
                dve.wait_ge(e_gate, m + 1)
                nc.vector.tensor_scalar(GP[:, b, :], GP[:, b, :], 0.5, 0.5, ALU.mult, ALU.add).then_inc(e_half, 1)
                dve.wait_ge(e_half, m + 1)
                nc.vector.tensor_tensor(E[:, m, :], GP[:, b, :], ps[:, ring("ple", 2 * b), :], ALU.mult).then_inc(bank_free, 2)
                stage_lo(dve, "ple", i, b, m >= 6)

        glu_gate, u_done, bt_ready, b_added, s2_ps, s2_max, p2_ready = (sem(n) for n in (
            "glu_gate", "u_done", "bt_ready", "b_added", "s2_ps", "s2_max", "p2_ready"))
        pt2_ps, pt2_sb, o3_ps, o3_done, y2_ps, y2_hi, y2_lo = (sem(n) for n in (
            "pt2_ps", "pt2_sb", "o3_ps", "o3_done", "y2_ps", "y2_hi", "y2_lo"))
        taps_done, conv_biased, mu_ps, centred, csq_ready, var_ps, var_ready, var_root, normed, cu_ready, cu_hi, cu_lo = (
            sem(n) for n in ("taps_done", "conv_biased", "mu_ps", "centred", "csq_ready", "var_ps", "var_ready",
                             "var_root", "normed", "cu_ready", "cu_hi", "cu_lo"))
        PAIRS = [(qt, hp) for qt in range(T) for hp in range(NH // 2)]

        def blk2_pe(pe):
            pe.wait_ge(in_lo, 8 * 4)
            feature_major(pe, "qk2", AH, AL)
            feature_major(pe, "glu", AH, AL)
            for b in range(2):
                weights_ready(pe, "v2", 0, b)
                for t in range(T):
                    tok = slice(t * P, (t + 1) * P)
                    if b == 0:
                        bank_ready(pe, "v2", t)
                    for k in range(4):
                        w = slice(k * 512, (k + 1) * 512)
                        o, kk = ps[:, ring("v2", t), :], 4 * b + k
                        nc.tensor.matmul(o, AH[:, kk, tok], WH[b][:, w], start=kk == 0, stop=False)
                        nc.tensor.matmul(o, AL[:, kk, tok], WH[b][:, w], start=False, stop=False)
                        last = nc.tensor.matmul(o, AH[:, kk, tok], WL[b][:, w], start=False, stop=kk == DC - 1)
                    if t % 2:
                        last.then_inc(seg_done, 1)

            def scores(u):
                qt, hp = PAIRS[u]
                n = (qt + 1) * P
                pe.wait_ge(p2_ready, 2 * (u - 1)) if u >= 2 else pe.wait_ge(bank_free, 4 + RING0["up2"])
                for x in range(2):
                    r = slice(x * DK, (x + 1) * DK)
                    last = nc.tensor.matmul(ps[:, 2 * (u % 2) + x, 0:n], QT2[r, hp, qt * P:n], KT2[r, hp, 0:n], start=True, stop=True)
                last.then_inc(s2_ps, 1)

            def turn(u):
                qt, hp = PAIRS[u]
                pe.wait_ge(p2_ready, 2 * (u + 1))
                if u:
                    pe.wait_ge(pt2_sb, u)
                for x in range(2):
                    for kt in range(qt + 1):
                        last = nc.tensor.transpose(ps[:, 4 + x, kt * P:(kt + 1) * P], PR2[:, u % 2, x, kt * P:(kt + 1) * P], ident[:, :])
                last.then_inc(pt2_ps, 1)

            def values(u):
                qt, hp = PAIRS[u]
                pe.wait_ge(pt2_sb, u + 1)
                if u >= 2:
                    pe.wait_ge(o3_done, u - 1)
                for x in range(2):
                    for kt in range(qt + 1):
                        last = nc.tensor.matmul(ps[:, 6 + u % 2, x * DK:(x + 1) * DK], PT2[:, u % 2, x, kt * P:(kt + 1) * P],
                                                V2[:, kt, (2 * hp + x) * DK:(2 * hp + x + 1) * DK], start=kt == 0, stop=kt == qt)
                last.then_inc(o3_ps, 1)

            n = len(PAIRS)
            scores(0)
            for u in range(n + 1):
                if u + 1 < n:
                    scores(u + 1)
                if u < n:
                    turn(u)
                if u:
                    values(u - 1)
            pe.wait_ge(o3_done, n)
            for qt in range(T):
                for c in range(4):
                    last = nc.tensor.transpose(ps[:, qt, c * P:(c + 1) * P], Y2[:, qt, c * P:(c + 1) * P], ident[:, :])
                last.then_inc(y2_ps, 1)
            pe.wait_ge(conv_biased, CC)
            for c in range(CC):
                last = nc.tensor.matmul(ps[:, 4, :], ones[:, :], CU[:, c, :], start=c == 0, stop=c == CC - 1)
            last.then_inc(mu_ps, 1)
            pe.wait_ge(csq_ready, 1)
            for c in range(CC):
                last = nc.tensor.matmul(ps[:, 5, :], ones[:, :], flat(PT2[:, :, :, :].rearrange("p a b s -> p (a b) s"))[:, c * S:(c + 1) * S],
                                        start=c == 0, stop=c == CC - 1)
            last.then_inc(var_ps, 1)
            pe.wait_ge(y2_lo, T)
            pe.wait_ge(cu_lo, CC)
            for m in range(DC):
                if m % 2 == 0:
                    weights_ready(pe, "wo2", m // 4, m // 2 % 2)
                if m == 7:
                    pe.wait_ge(h_ready, 25)
                product(y_bank(m), m // 2 % 2, 8 * (m % 2), DC, AH, AL).then_inc(seg_done, 1)
                if m:
                    add_squares(pe, 6, m - 1)
            add_squares(pe, 6, DC - 1)

        def blk2_act(act):
            def body(i, last):
                for b in range(2):
                    stage_hi(act, "qk2", i, b, last)
            pairs(act, "qk2", body)
            for c in range(CC):
                i, b = c // 2, c % 2
                seg_ready(act, "glu", 2 * b + 1, i)
                if c >= 2:
                    act.wait_ge(bank_free, 4 + RING0["glu"] + 2 * c - 2)
                nc.scalar.activation(SQ[:, b, :], ps[:, ring("glu", 2 * b + 1), :], ACT.Tanh, scale=0.5).then_inc(glu_gate, 1)
                stage_hi(act, "glu", i, b, i == 1)
            for b in range(2):
                stage_hi(act, "v2", 0, b, True)
            for u, (qt, hp) in enumerate(PAIRS):
                n = (qt + 1) * P
                act.wait_ge(s2_max, u + 1)
                if u >= 2:
                    act.wait_ge(pt2_ps, u - 1)
                    act.wait_ge(o3_done, u - 1)
                for x in range(2):
                    nc.scalar.activation(PR2[:, u % 2, x, 0:n], ps[:, 2 * (u % 2) + x, 0:n], ACT.Exp,
                                         bias=NM2[:, u % 2, x:x + 1], accum_out=LS2[:, u % 2, x:x + 1]).then_inc(p2_ready, 1)
            for qt in range(T):
                act.wait_ge(y2_ps, qt + 1)
                nc.scalar.activation(AH[:, 0:4, qt * P:(qt + 1) * P], ps[:, qt, :].rearrange("p (c n) -> p c n", c=4),
                                     ACT.Copy).then_inc(y2_hi, 1)
            act.wait_ge(taps_done, CC)
            for c in range(CC):
                nc.scalar.activation(CU[:, c, :], CU[:, c, :], ACT.Identity, bias=col("cb2", c), scale=0.5).then_inc(conv_biased, 1)
            act.wait_ge(centred, 1)
            nc.scalar.activation(PT2[:, :, :, :].rearrange("p a b s -> p (a b) s"), CU[:, :, :], ACT.Square).then_inc(csq_ready, 1)
            act.wait_ge(var_ready, 1)
            nc.scalar.activation(RR[:, :], RR[:, :], ACT.Sqrt).then_inc(var_root, 1)
            for c in range(CC):
                act.wait_ge(normed, c + 1)
                nc.scalar.activation(CU[:, c, :], CU[:, c, :], ACT.Silu, bias=col("lnb", c), scale=col("lng", c)).then_inc(cu_ready, 1)
                act.wait_ge(cu_ready, c + 1)
                nc.scalar.activation(AH[:, 4 + c, :], CU[:, c, :], ACT.Copy).then_inc(cu_hi, 1)
            for m in range(DC):
                act.wait_ge(h_ready, 25 + m)
                square(act, 6, m, hT[:, m, :])
                if m % 2:
                    stage_hi(act, "wo2", m // 4, m // 2 % 2, m >= 4)

        def blk2_dve(dve, own):
            vec = nc.vector
            def body(i, last):
                for b in range(2):
                    for s in range(2):
                        c = 2 * b + s
                        seg_ready(dve, "qk2", c, i)
                        if i == 0:
                            ins = vec.tensor_scalar(QT2[:, c, :], ps[:, ring("qk2", c), :], DK ** -0.5, None, ALU.mult)
                        else:
                            ins = vec.tensor_copy(KT2[:, c, :], ps[:, ring("qk2", c), :])
                        ins.then_inc(bank_free, 1)
                    stage_lo(dve, "qk2", i, b, last)
            pairs(dve, "qk2", body)
            own.mark(vec.memset(UG[:, :, 0:CT - 1], 0.0))
            for c in range(CC):
                i, b = c // 2, c % 2
                dve.wait_ge(glu_gate, c + 1)
                vec.scalar_tensor_tensor(UG[:, c, CT - 1:], SQ[:, b, :], 1.0, ps[:, ring("glu", 2 * b), :], ALU.add,
                                         ALU.mult).then_inc(bank_free, 2)
                stage_lo(dve, "glu", i, b, i == 1)
            dve.wait_ge(seg_done, SEG0["wo2"])
            for t in range(T):
                vec.tensor_copy(V2[:, t, :], ps[:, ring("v2", t), :]).then_inc(bank_free, 1)
                if t % 2:
                    stage_lo(dve, "v2", 0, t // 2, True)
            dve.wait_ge(blk2_landed, 32)
            own.link(vec.tensor_tensor(BT[:, :, :], BT[:, :, :], col("far", 0, 8).unsqueeze(2).to_broadcast([P, NH, 256]), ALU.subtract))
            own.link(vec.tensor_tensor(BT[:, :, P:], BT[:, :, P:], MB2[:, :].unsqueeze(1).to_broadcast([P, NH, P]), ALU.add))
            dve.wait_ge(bank_free, 4 + RING0["up2"])
            own.wait()
            for c in range(CC):
                own.mark(vec.tensor_scalar(CU[:, c, :], UG[:, c, 0:S], col("cw2", c * CT), None, ALU.mult))
            for j in range(1, CT):
                for c in range(CC):
                    own.wait(3)
                    ins = vec.scalar_tensor_tensor(CU[:, c, :], UG[:, c, j:j + S], col("cw2", c * CT + j), CU[:, c, :],
                                                   ALU.mult, ALU.add)
                    if j < CT - 1:
                        own.mark(ins)
                    else:
                        ins.then_inc(taps_done, 1)
                        own.n += 1
            own.n -= CC

            def top(u):
                qt, hp = PAIRS[u]
                n, w = (qt + 1) * P, min((qt + 1) * P, 256)
                banks = slice(2 * (u % 2), 2 * (u % 2) + 2)
                dve.wait_ge(s2_ps, u + 1)
                vec.tensor_tensor(ps[:, banks, n - w:n], ps[:, banks, n - w:n], BT[:, 2 * hp:2 * hp + 2, 256 - w:256],
                                  ALU.add).then_inc(b_added, 1)
                dve.wait_ge(b_added, u + 1)
                vec.tensor_reduce(NM2[:, u % 2, :], ps[:, banks, 0:n], AX, ALU.max, negate=True).then_inc(s2_max, 1)

            def save(u):
                n = (PAIRS[u][0] + 1) * P
                dve.wait_ge(pt2_ps, u + 1)
                if u >= 2:
                    dve.wait_ge(o3_ps, u - 1)
                vec.tensor_copy(PT2[:, u % 2, :, 0:n], ps[:, 4:6, 0:n]).then_inc(pt2_sb, 1)

            def add(u):
                qt, hp = PAIRS[u]
                b = u % 2
                dve.wait_ge(o3_ps, u + 1)
                own.link(vec.reciprocal(RL2[:, b, :], LS2[:, b, :]))
                y = Y2[:, qt, 2 * hp * DK:(2 * hp + 2) * DK].rearrange("p (x d) -> p x d", x=2)
                vec.tensor_tensor(y, ps[:, 6 + b, 0:2 * DK].rearrange("p (x d) -> p x d", x=2),
                                  RL2[:, b, :].unsqueeze(2).to_broadcast([P, 2, DK]), ALU.mult).then_inc(o3_done, 1)

            top(0)
            for u in range(len(PAIRS) + 1):
                if u + 1 < len(PAIRS):
                    top(u + 1)
                if u < len(PAIRS):
                    save(u)
                if u:
                    add(u - 1)
            for qt in range(T):
                tok = slice(qt * P, (qt + 1) * P)
                dve.wait_ge(y2_hi, qt + 1)
                vec.tensor_tensor(AL[:, 0:4, tok], ps[:, qt, :].rearrange("p (c n) -> p c n", c=4),
                                  AH[:, 0:4, tok].bitcast(F32), ALU.subtract).then_inc(y2_lo, 1)
            dve.wait_ge(mu_ps, 1)
            own.link(vec.tensor_scalar(RR[:, :], ps[:, 4, :], 1.0 / 512, None, ALU.mult))
            vec.tensor_tensor(CU[:, :, :], CU[:, :, :], RR[:, :].unsqueeze(1).to_broadcast([P, CC, S]), ALU.subtract).then_inc(centred, 1)
            dve.wait_ge(var_ps, 1)
            vec.tensor_scalar(RR[:, :], ps[:, 5, :], 1.0 / 512, LN_EPS, ALU.mult, ALU.add).then_inc(var_ready, 1)
            dve.wait_ge(var_root, 1)
            own.link(vec.reciprocal(RR[:, :], RR[:, :]))
            for c in range(CC):
                vec.tensor_tensor(CU[:, c, :], CU[:, c, :], RR[:, :], ALU.mult).then_inc(normed, 1)
            for c in range(CC):
                dve.wait_ge(cu_hi, c + 1)
                vec.tensor_tensor(AL[:, 4 + c, :], CU[:, c, :], AH[:, 4 + c, :].bitcast(F32), ALU.subtract).then_inc(cu_lo, 1)
            for m in range(DC):
                seg_ready(dve, "wo2", m)
                vec.tensor_tensor(hT[:, m, :], hT[:, m, :], y_bank(m), ALU.add).then_inc(h_ready, 1)
                if m % 2:
                    stage_lo(dve, "wo2", m // 4, m // 2 % 2, m >= 4)

        def down2_act(act):
            def chunk(m, par, last):
                stage_hi(act, "down2", m, 0, last)
                act.wait_ge(h_ready, m + 33)
                square_at(act, 7, m, par, at(hT, m))
                stage_hi(act, "down2", m, 1, last)
            down_chunks(act, chunk)

        def down2_dve(dve):
            def chunk(m, par, last):
                stage_lo(dve, "down2", m, 0, last)
                down_seg(dve, "down2", m)
                nc.vector.tensor_tensor(at(hT, m), at(hT, m), ps[:, 0:1, :] if last else at(ps, m), ALU.add).then_inc(h_ready, 1)
                stage_lo(dve, "down2", m, 1, last)
            down_chunks(dve, chunk)

        def out_dve(dve):
            for m in range(DC):
                if m >= 2:
                    dve.wait_ge(out_stored[m % 2], 16 * (m // 2))
                nc.vector.scalar_tensor_tensor(TMP[:, m % 2, :], hT[:, m, :], col("final", m), RR[:, :], ALU.mult,
                                               ALU.mult).then_inc(out_ready, 1)

        block = ctx.enter_context(nc.Block())

        @block.sync
        def _(sp):
            xv = xT.rearrange("(c p) s -> p c s", p=P)
            for q in range(4):
                sp.dma_start(hT[:, 2 * q:2 * q + 2, :], xv[:, 2 * q:2 * q + 2, :]).then_inc(x_landed[q], 16)

            def load(name, b, piece):
                n = NB[name] * P
                sp.dma_start(RAW[b][:, 0:n], wstream[piece, :, 0:n] if isinstance(piece, int) else
                             wstream[bass.ds(piece, 1), :, 0:n].rearrange("a p n -> p (a n)")).then_inc(raw_landed[b], 16)

            for name, n, nb, _ in PHASES:
                first = 0
                if PIECE0[name] == 0:
                    load(name, 0, 0)
                    load(name, 1, 1)
                    first = 1
                if n == 1:
                    sp.wait_ge(w_lo_done, PIECE0[name] - 1)
                    load(name, PIECE0[name] % 2, PIECE0[name])
                elif n // 2 - first > 1:
                    with sp.Fori(first, n // 2) as i:
                        for b in range(2):
                            sp.wait_ge(w_lo_done, PIECE0[name] + b - 1 + i * 2)
                            load(name, b, i * 2 + (PIECE0[name] + b))
                else:
                    for i in range(first, n // 2):
                        for b in range(2):
                            sp.wait_ge(w_lo_done, PIECE0[name] + b - 1 + i * 2)
                            load(name, b, i * 2 + (PIECE0[name] + b))
            ov = out.rearrange("(c p) s -> p c s", p=P)
            for m in range(DC):
                sp.wait_ge(out_ready, m + 1)
                sp.dma_start(ov[:, m, :], TMP[:, m % 2, :]).then_inc(out_stored[m % 2], 16)
            for b in range(2):
                sp.wait_ge(out_stored[b], 16 * DC // 2)

        @block.gpsimd
        def _(pool):
            pool.memset(ones[:, :], 1.0).then_inc(set_up, 1)
            gdn_pool(pool)
            pool.wait_ge(yt_lo, T)
            nc.gpsimd.tensor_copy(MB[:, 0, :], ident[:, :]).then_inc(mb_ready, 1)
            nc.gpsimd.tensor_copy(MB[:, 1, :], NG_T[:, :]).then_inc(mb_ready, 1)
            pool.dma_start(QT[64:66, :, :], alibi_d).then_inc(nsa_landed, 16)
            pool.dma_start(KT[64:66, :, :, :], krow_d).then_inc(nsa_landed, 16)
            pool.dma_start(KC[64:66, :, :], crow_d).then_inc(nsa_landed, 16)
            pool.dma_start(W2[:, :, :], w2_d).then_inc(nsa_landed, 16)
            pool.dma_start(CN[:, :, :], cneg_d).then_inc(nsa_landed, 16)
            pool.dma_start(C01[:, :, :], c01_d).then_inc(nsa_landed, 16)
            pool.dma_start(W1[0][:, :, :], w1k_d).then_inc(w1_landed, 16)
            pool.dma_start(W1[1][:, :, :], w1v_d).then_inc(w1_landed, 16)
            pool.wait_ge(seg_done, SEG0["ple"])
            pool.dma_start(PX[:, :, :], pT.rearrange("(c p) s -> p c s", p=P)).then_inc(p_landed, 16)
            pool.wait_ge(h_ready, 24)
            pool.dma_start(BT[:, :, :], bias2_d).then_inc(blk2_landed, 16)
            pool.dma_start(MB2[:, :], causal_d).then_inc(blk2_landed, 16)

        @block.scalar
        def _(act):
            act.dma_start(cols[:, :], cols_d).then_inc(cols_landed, 16)
            for dst, src in ((ident[:, :], ident_d), (NG_T[:, :], causal_d), (CS[:, :], consts_d), (WSR[:, :], wsm_d)):
                act.dma_start(dst, src).then_inc(con_landed, 16)
            for m in range(DC):
                if m % 2 == 0:
                    act.wait_ge(x_landed[m // 2], 16)
                square(act, 0, m, hT[:, m, :])
            rms_root(act, 0)
            for b in range(2):
                act.wait_ge(raw_landed[b], 16)
                nc.scalar.activation(WH[b][:, :], RAW[b][:, :], ACT.Copy).then_inc(w_hi_done, 1)
            pre_hi(act, 0)
            qkv_act(act)
            z_act(act)
            gdn_act(act)
            nsa_proj_act(act)
            nsa_act(act)
            mix_act(act)
            wo_act(act)
            rms_root(act, 1)
            for m in range(DC):
                act.wait_ge(h_ready, m + 1)
                square(act, 2, m, hT[:, m, :])
            rms_root(act, 2)
            pre_hi(act, 1)
            up_act(act)
            down_act(act)
            rms_root(act, 3)
            pre_hi(act, 2)
            ple_act(act)
            rms_root(act, 4)
            for m in range(DC):
                act.wait_ge(h_ready, 16 + m + 1)
                square(act, 5, m, hT[:, m, :])
            rms_root(act, 5)
            pre_hi(act, 3)
            blk2_act(act)
            rms_root(act, 6)
            pre_hi(act, 4)
            up2_act(act)
            down2_act(act)
            rms_root(act, 7)

        @block.vector
        def _(dve):
            own = Own(dve, dve_own)
            dve.memset(YX[:, 0:1], 0.0).then_inc(bank_free, 4)
            dve.wait_ge(cols_landed, 16)
            rms_rest(dve, 0)
            for b in range(2):
                dve.wait_ge(w_hi_done, b + 1)
                nc.vector.tensor_tensor(WL[b][:, :], RAW[b][:, :], WH[b][:, :].bitcast(F32), ALU.subtract).then_inc(w_lo_done, 1)
            pre_rest(dve, 0, "mix_pre")
            qkv_dve(dve)
            z_dve(dve)
            gdn_dve(dve, own)
            nsa_proj_dve(dve)
            nsa_dve(dve, own)
            mix_dve(dve)
            wo_dve(dve)
            rms_rest(dve, 1)
            post_add(dve, 0, "mix_post", YX, y_bank)
            rms_rest(dve, 2)
            pre_rest(dve, 1, "ffn_pre")
            up_dve(dve)
            down_dve(dve)
            rms_rest(dve, 3)
            post_add(dve, 1, "ffn_post", YX, y_bank)
            dve.wait_ge(h_ready, 16)
            pre_rest(dve, 2, None)
            ple_dve(dve)
            rms_rest(dve, 4)
            post_add(dve, 2, "ple_post", None, lambda m: E[:, m, :])
            rms_rest(dve, 5)
            pre_rest(dve, 3, "mix2")
            blk2_dve(dve, own)
            rms_rest(dve, 6)
            pre_rest(dve, 4, "ffn2")
            up2_dve(dve)
            down2_dve(dve)
            rms_rest(dve, 7)
            out_dve(dve)

        @block.tensor
        def _(pe):
            pe.wait_ge(set_up, 1)
            for m in range(DC):
                add_squares(pe, 0, m)
            pe.wait_ge(in_lo, DC)
            feature_major(pe, "qkv", AH, AL)
            feature_major(pe, "z", AH, AL)
            gdn_pe(pe)
            nsa_proj_pe(pe)
            nsa_pe(pe)
            mix_pe(pe)
            pe.wait_ge(mix_lo, DC)
            pe.wait_ge(bank_free, 4 + RING0["up"])
            wide_product(pe, "wo", 1, GHI, GLO, y0_saved, 1)
            for m in range(DC):
                add_squares(pe, 2, m)
            pe.wait_ge(in_lo, 2 * DC)
            feature_major(pe, "up", AH, AL)
            pe.wait_ge(hid_lo, FC)
            down_pe(pe, "down", 3, y0_saved, 2)
            ple_pe(pe)
            for m in range(DC):
                add_squares(pe, 5, m)
            blk2_pe(pe)
            pe.wait_ge(in_lo, 5 * DC)
            feature_major(pe, "up2", AH, AL)
            pe.wait_ge(hid_lo, 2 * FC)
            down_pe(pe, "down2", 7, h_ready, 33)


def shape_tables():
    i = np.arange(P)
    same = lambda w: i[:, None] // w == i[None, :] // w
    parts = [(i[:, None] <= i[None, :]) & same(C), (i[:, None] > i[None, :]) & same(C),
             np.broadcast_to(i[:, None] < C, (P, P)), np.broadcast_to(i[:, None] >= C, (P, P))]
    for w in (1, 2, 4, 8, 16, 32):
        parts.append(same(2 * w) & (i[:, None] // w % 2 == 0) & (i[None, :] // w % 2 == 1))
    consts = np.concatenate([x.astype(np.float32) for x in parts], axis=1)
    ident = np.eye(P, dtype=np.float32)
    causal = np.where(i[None, :] > i[:, None], np.float32(NEG), np.float32(0))
    t = (np.arange(T)[:, None, None] * P + i[None, :, None])
    ends = np.arange(32)[None, None, :] * CMP_STRIDE + CMP_LEN - 1
    seen = ((t >= ends) & (np.arange(32) < NC)).transpose(1, 0, 2)
    cneg = np.where(seen, np.float32(0), np.float32(NEG))
    c01 = seen.astype(np.float32)
    slope = 2.0 ** (-8.0 * np.arange(1, NH + 1) / NH)
    alibi = np.stack([np.repeat(slope[:, None], S, 1), -slope[:, None] * np.arange(S)]).astype(np.float32)
    krow = np.stack([np.broadcast_to(np.arange(S), (2, NG, S)), np.ones((2, NG, S))]).astype(np.float32)
    crow = np.stack([np.broadcast_to(ends[0, 0], (NG, 32)), np.ones((NG, 32))]).astype(np.float32)
    return consts, ident, causal, cneg, c01, alibi, krow, crow


def t5_bucket(dist):
    d = np.maximum(dist, 1).astype(np.float32)
    large = 16 + (np.log(d / np.float32(16)) / np.float32(np.log(128 / 16)) * np.float32(16)).astype(np.int32)
    return np.where(dist < 16, dist, np.minimum(large, 31))


def blocks(w, k0, k1, c0, c1):
    return w[k0:k1, c0:c1].reshape((k1 - k0) // P, P, c1 - c0).transpose(1, 0, 2)


def weight_stream(a):
    w = a["w_in"][0]
    ks, fm = [], lambda w_, cols_: [np.concatenate([blocks(w_, 0, w_.shape[0], c, c + P).reshape(P, -1) for c in cs], 1) for cs in cols_]
    two = lambda c0, n: [[c0 + 2 * P * j, c0 + 2 * P * j + P] for j in range(n)]
    ks += fm(w, two(0, 6)) + fm(w, two(1536, 2))
    ks += fm(w, two(2056, 2)) + fm(w, [[2568], [2696]]) + fm(w, [[2824, 3080]])
    ks += [np.concatenate([blocks(w, 0, D, 2952, 3080), blocks(w, 0, D, 3208, 3336)], 2).reshape(P, -1)]
    for j in range(DC):
        for g0, y in ((3360, a["w_a2d"][0]), (3360 + D, a["w_b2d"][0])):
            ks.append(np.concatenate([blocks(w, 0, D, g0 + j * P, g0 + j * P + P).reshape(P, -1),
                                      blocks(y, 0, 512, j * P, j * P + P).reshape(P, -1)], 1))
    ks += fm(a["w_o"][0], two(0, 4))
    ks += fm(a["w_up"][0], [[j * P, FF + j * P] for j in range(FC)])

    def down(w_):
        return [blocks(w_, x * 11 * P, (x + 1) * 11 * P, j * P, j * P + P).reshape(P, -1) for j in range(DC) for x in range(2)]
    ks += down(a["w_down"][0])
    ks += [np.concatenate([blocks(a["w_ple"][0], 0, PLE, j * P, j * P + P).reshape(P, -1),
                           blocks(a["w_ple_gate"][0], 0, D, j * P, j * P + P).reshape(P, -1)], 1) for j in range(DC)]
    w2 = a["w_in_2"][0]
    ks += fm(w2, two(0, 4)) + fm(w2, [[1536 + j * P, 2048 + j * P] for j in range(CC)])
    ks += [blocks(w2, x * 512, (x + 1) * 512, 1024, 1536).reshape(P, -1) for x in range(2)]
    ks += fm(a["w_out_2"][0], two(0, 4))
    ks += [np.concatenate([blocks(a["w_gate_2"][0], 0, D, j * P, j * P + P).reshape(P, -1),
                           blocks(a["w_up_2"][0], 0, D, j * P, j * P + P).reshape(P, -1)], 1) for j in range(FC)]
    ks += down(a["w_down_2"][0])
    assert [x.shape[1] // P for x in ks] == PIECE_NB[:PIECES]
    stream = np.zeros((PIECES, P, BLK * P), np.float32)
    for j, x in enumerate(ks):
        stream[j, :, :x.shape[1]] = x
    return stream


def lay_out(a):
    a = {k: np.asarray(v) for k, v in a.items()}
    consts, ident, causal, cneg, c01, alibi, krow, crow = shape_tables()
    cols = np.zeros((P, NCOLS), np.float32)

    def put(name, x):
        cols[:, COLS[name]:COLS[name] + x.shape[1]] = x

    vec = lambda x: x.reshape(-1, P).T
    for name, key in (("mix_pre", "norm_mix_pre"), ("mix_post", "norm_mix_post"), ("ffn_pre", "norm_ffn_pre"),
                      ("ffn_post", "norm_ffn_post"), ("ple_post", "norm_ple_post"), ("mix2", "mix_norm_g_2"),
                      ("ffn2", "ffn_norm_g_2"), ("final", "final_norm_g_2"), ("gdn", "gdn_norm"),
                      ("cb2", "conv_b_2"), ("lng", "conv_ln_g_2"), ("lnb", "conv_ln_b_2")):
        put(name, vec(a[key]))
    put("cqkv", a["conv_qkv"][0].reshape(4, 12, P).transpose(2, 1, 0).reshape(P, -1))
    put("cffn", a["conv_ffn"][0].reshape(3, 2, FC, P).transpose(3, 2, 1, 0).reshape(P, -1))
    put("cffnb", a["conv_ffn_b"][0].reshape(2, FC, P).transpose(2, 1, 0).reshape(P, -1))
    put("cw2", a["conv_w_2"][0].reshape(CT, CC, P).transpose(2, 1, 0).reshape(P, -1))
    put("alog", np.broadcast_to(a["a_log"], (P, GH)))
    put("dtb", np.broadcast_to(a["dt_bias"], (P, GH)))
    put("far", np.broadcast_to(a["rel_bias_2"][31], (P, NH)))
    put("posk", a["cmp_pos_k"][0].reshape(16, P).T)
    put("posv", a["cmp_pos_v"][0].reshape(16, P).T)
    put("eps", np.full((P, 1), EPS, np.float32))
    w = a["w_in"][0]
    wsm = np.concatenate([blocks(w, 0, D, 2048, 2056), blocks(w, 0, D, 3336, 3360)], 2).reshape(P, -1)
    q, kk = np.arange(P)[:, None], np.arange(256)[None, :]
    bias = a["rel_bias_2"][t5_bucket(np.maximum(q + P - kk, 0))].transpose(0, 2, 1)
    w2 = np.concatenate([blocks(a["cmp_w2_k"][0], 0, CMP_HID, 0, DK), blocks(a["cmp_w2_v"][0], 0, CMP_HID, 0, DK)], 1)
    return {
        "wstream": weight_stream(a), "xT": a["x"][0].T, "pT": a["p"][0, 0].T, "cols_d": cols, "ident_d": ident,
        "causal_d": causal, "consts_d": consts, "cneg_d": cneg, "c01_d": c01, "alibi_d": alibi, "krow_d": krow,
        "crow_d": crow, "wsm_d": wsm, "w1k_d": blocks(a["cmp_w1_k"][0], 0, 2048, 0, CMP_HID),
        "w1v_d": blocks(a["cmp_w1_v"][0], 0, 2048, 0, CMP_HID), "w2_d": w2, "bias2_d": bias,
    }


def kernel(**inputs):
    import concourse.bacc as bacc
    from concourse.bass_utils import run_bass_kernel_spmd

    nc = bacc.Bacc("TRN2", target_bir_lowering=False, num_devices=1)
    arrays, args = {}, {}
    for name, x in lay_out(inputs).items():
        arrays[name] = np.ascontiguousarray(x)
        args[name] = nc.dram_tensor(name, x.shape, mybir.dt.from_np(x.dtype), kind="ExternalInput").ap()
    args["out"] = nc.dram_tensor("out", (D, S), F32, kind="ExternalOutput").ap()
    build(nc, **args)
    r = run_bass_kernel_spmd(nc, [arrays], core_ids=[0])
    return np.ascontiguousarray(r.results[0]["out"].T).reshape(1, S, D)
```

```python
from contextlib import ExitStack

import numpy as np

import concourse.bass as bass
from concourse import mybir

F32 = mybir.dt.float32
F32R = mybir.dt.float32r
BF16 = mybir.dt.bfloat16
ALU = mybir.AluOpType
ACT = mybir.ActivationFunctionType
AX = mybir.AxisListType.X

P = 128
D = 1024
S = 512
DC = D // P
T = S // P
EPS = 1e-6
LN_EPS = 1e-5
NEG = -1e30

GH = 4
C = 64
NH, NG, DK = 8, 2, 64
R = NH // NG
CMP_LEN, CMP_STRIDE, CMP_HID = 32, 16, 256
NC = S // CMP_STRIDE - 1
PLE = 256
FF = 2816
FC = FF // P
CT = 31
CC = 512 // P

BLK = 16
PHASES = [
    ("qkv", 6, 16, 2), ("z", 2, 16, 2),
    ("nq", 2, 16, 2), ("ncmp", 2, 8, 1), ("nk", 1, 16, 2), ("nv", 1, 16, 2),
    ("mix", 16, 12, 2), ("wo", 4, 16, 2), ("up", 22, 16, 2), ("down", 16, 11, 1), ("ple", 8, 10, 2),
    ("glu", 4, 16, 2), ("qk2", 4, 16, 2), ("v2", 2, 16, 2), ("wo2", 4, 16, 2),
    ("up2", 22, 16, 2), ("down2", 16, 11, 1),
]
PIECE0, SEG0, NB, NSEG, NPIECE, NEXT = {}, {}, {}, {}, {}, {}
_piece = _seg = 0
for _k, (_name, _n, _nb, _s) in enumerate(PHASES):
    PIECE0[_name], SEG0[_name], NB[_name], NSEG[_name], NPIECE[_name] = _piece, _seg, _nb, _s, _n
    NEXT[_name] = PHASES[_k + 1][0] if _k + 1 < len(PHASES) else None
    _piece += _n
    _seg += _n * _s
PIECES = _piece
PIECE_NB = [nb for _, n, nb, _ in PHASES for _ in range(n)]
PIECE_SEG = (
    np.cumsum([0] + [s for _, n, _, s in PHASES for _ in range(n)]).tolist())
RING = {"qkv": 12, "z": 4, "nq": 4, "ncmp": 2, "nk": 2, "nv": 2, "mix": 32, "up": 44,
        "ple": 16, "glu": 8, "qk2": 8, "v2": 4, "up2": 44}
RING0, _n = {}, 0
for _name, _, _, _ in PHASES:
    if _name in RING:
        RING0[_name] = _n
        _n += RING[_name]

COLS = {}
_n = 0
for _name, _w in (("mix_pre", 8), ("mix_post", 8), ("ffn_pre", 8), ("ffn_post", 8), ("ple_post", 8),
                  ("mix2", 8), ("ffn2", 8), ("final", 8), ("cqkv", 48), ("gdn", 1), ("cffn", 132),
                  ("cffnb", 44), ("cw2", 124), ("cb2", 4), ("lng", 4), ("lnb", 4), ("alog", 4),
                  ("dtb", 4), ("far", 8), ("posk", 16), ("posv", 16), ("eps", 1), ("lneps", 1)):
    COLS[_name] = _n
    _n += _w
NCOLS = _n
CON = {}
_n = 0
for _name, _w in (("tri", 128), ("after", 128), ("half", 256), ("seen", 128), ("level", 6 * 128)):
    CON[_name] = _n
    _n += _w
NCON = _n


def build(nc, wstream, xT, pT, cols_d, ident_d, causal_d, consts_d, cneg_d, c01_d, alibi_d, krow_d, crow_d,
          wsm_d, w1k_d, w1v_d, w2_d, bias2_d, out):
    with ExitStack() as ctx:
        def sb(name, shape, dt=F32, scope=ctx):
            return scope.enter_context(nc.sbuf_tensor(name, shape, dt))

        def sem(name):
            return ctx.enter_context(nc.semaphore(name))

        hT = sb("hT", [P, DC, S])
        AH = sb("AH", [P, DC, S], F32R)
        AL = sb("AL", [P, DC, S], F32R)
        RAW = [sb(f"raw{b}", [P, BLK * P]) for b in range(2)]
        WH = [sb(f"whi{b}", [P, BLK * P], F32R) for b in range(2)]
        WL = [sb(f"wlo{b}", [P, BLK * P], F32R) for b in range(2)]
        cols = sb("cols", [P, NCOLS])
        ones = sb("ones", [P, P])
        ident = sb("ident", [P, P])
        RR = sb("RR", [P, S])
        SQ = sb("SQ", [P, 2, S])
        TMP = sb("TMP", [P, 2, S])
        YX = sb("YX", [P, S])
        SF = YX
        RC = sb("RC", [P, T])

        def col(name, j=0, n=1):
            if isinstance(j, int):
                return cols[:, COLS[name] + j:COLS[name] + j + n]
            return cols[:, bass.ds(j + COLS[name], n)]

        blk1 = ExitStack()
        SG = sb("SG", [P, T, 32], F32, blk1)
        NG_T = sb("NG_T", [P, P], F32, blk1)
        MB = sb("MB", [P, 2, P], BF16, blk1)
        with ExitStack() as x:
            Tm = sb("Tm", [P, T, GH, P], F32, x)
            TT = sb("TT", [P, T, GH, P], F32, x)
        YAH = sb("YAH", [P, 4, S], F32R, blk1)
        YAL = sb("YAL", [P, 4, S], F32R, blk1)
        with ExitStack() as x:
            QKV = sb("QKV", [P, 12, S], F32, x)
            ZS = sb("ZS", [P, 4, S], F32, x)
            Y1 = sb("Y1", [P, T, GH, P], F32, x)
            AT = sb("AT", [P, T, GH, P], F32, x)
            OFF = sb("OFF", [P, T, GH, P], F32, x)
            QK = sb("QK", [P, T, GH, P], F32, x)
            ST = sb("ST", [P, 2, GH, P], F32, x)
            CS = sb("CS", [P, NCON], F32, x)
            WSR = sb("WSR", [P, DC * 32], F32, x)
            WSH = sb("WSH", [P, DC * 32], F32R, x)
            WSL = sb("WSL", [P, DC * 32], F32R, x)
            SM = sb("SM", [P, T, 32], F32, x)
            AA = sb("AA", [P, 4, T, GH], F32, x)
            EA = sb("EA", [P, GH], F32, x)
            G = sb("G", [P, T, GH], F32, x)
            EX = sb("EX", [P, 4, T, GH], F32, x)
            GC = sb("GC", [P, T, GH], F32, x)
            BG = sb("BG", [P, T, GH], F32, x)
            RO = sb("RO", [P, T, GH], F32, x)
            L2 = sb("L2", [P, 2 * GH * T], F32, x)
        with ExitStack() as x:
            W1v = sb("W1v", [P, 16, CMP_HID], F32, x)
        YBH = sb("YBH", [P, 4, S], F32R, blk1)
        YBL = sb("YBL", [P, 4, S], F32R, blk1)
        with ExitStack() as x:
            QT = sb("QT", [P, NH, S], F32, x)
            KT = sb("KT", [P, 2, NG, S], F32, x)
            V1 = sb("V1", [P, T, 2 * P], F32, x)
            KC = sb("KC", [P, NG, 32], F32, x)
            VB = sb("VB", [P, NG, R * DK], F32, x)
            W2 = sb("W2", [P, 4, DK], F32, x)
            SC = sb("SC", [P, T, NH, 32], F32, x)
            CN = sb("CN", [P, T, 32], F32, x)
            C01 = sb("C01", [P, T, 32], F32, x)
            HID = sb("HID", [P, 4, 2 * NC], F32, x)
            SX = sb("SX", [P, 3, T, NH], F32, x)
            NM = sb("NM", [P, 4, 1], F32, x)
            LS = sb("LS", [P, 4, 2], F32, x)
            RL = sb("RL", [P, 2, 2], F32, x)
            with ExitStack() as y:
                W1 = [sb("W1k", [P, 16, CMP_HID], F32, y), W1v]
                Z = [sb(f"z{n}", [P, 16, 2 * NC], F32, y) for n in "kv"]
            PR = sb("PR", [P, 4, S], F32, x)
            PT = sb("PT", [P, 4, S], F32, x)
            Y = sb("Y", [P, T, NH * DK], F32, x)
        with ExitStack() as x:
            GHI = sb("GHI", [P, DC, S], F32R, x)
            GLO = sb("GLO", [P, DC, S], F32R, x)
        blk1.close()
        with ExitStack() as x:
            HH = sb("HH", [P, FC, S], F32R, x)
            HL = sb("HL", [P, FC, S], F32R, x)
            CG = sb("CG", [P, 2, S], F32, x)
            CV = sb("CV", [P, 2, S], F32, x)
        with ExitStack() as x:
            E = sb("E", [P, DC, S], F32, x)
            PX = sb("PX", [P, 2, S], F32, x)
            PH = sb("PH", [P, 2, S], F32R, x)
            PL = sb("PL", [P, 2, S], F32R, x)
            GP = sb("GP", [P, 2, S], F32, x)
        with ExitStack() as x:
            MB2 = sb("MB2", [P, P], F32, x)
            QT2 = sb("QT2", [P, 4, S], F32, x)
            KT2 = sb("KT2", [P, 4, S], F32, x)
            V2 = sb("V2", [P, T, 512], F32, x)
            BT = sb("BT", [P, NH, 256], F32, x)
            PR2 = sb("PR2", [P, 4, S], F32, x)
            PT2 = sb("PT2", [P, 4, S], F32, x)
            Y2 = sb("Y2", [P, T, 512], F32, x)
            UG = sb("UG", [P, CC, S + CT - 1], F32, x)
            CU = sb("CU", [P, CC, S], F32, x)
            NM2 = sb("NM2", [P, 4, 1], F32, x)
            LS2 = sb("LS2", [P, 4, 2], F32, x)
            RL2 = sb("RL2", [P, 2, 2], F32, x)
        ps = ctx.enter_context(nc.psum_tensor("ps", [P, 8, 512], F32))

        raw_landed = [sem(f"raw{b}_landed") for b in range(2)]
        w_hi_done, w_lo_done = sem("w_hi_done"), sem("w_lo_done")
        seg_done = sem("seg_done")
        bank_free = sem("bank_free")
        N_CON, N_NSA = 3, 6
        x_landed, cols_landed, con_landed = [sem(f"x{q}_landed") for q in range(4)], sem("cols_landed"), sem("con_landed")
        ident_landed = sem("ident_landed")
        nsa_landed, w1_landed, p_landed, blk2_landed = (sem("nsa_landed"), sem("w1_landed"),
                                                         sem("p_landed"), sem("blk2_landed"))
        set_up, ws_split = sem("set_up"), sem("ws_split")
        rc_ready, rows_ps = sem("rc_ready"), sem("rows_ps")
        sq_ready, sq_used, ms_ready = sem("sq_ready"), sem("sq_used"), sem("ms_ready")
        rt_ready, rr_ready, h_ready, y0_saved = sem("rt_ready"), sem("rr_ready"), sem("h_ready"), sem("y0_saved")
        in_tmp, in_hi, in_lo = sem("in_tmp"), sem("in_hi"), sem("in_lo")
        out_ready, out_stored = sem("out_ready"), [sem(f"out_stored{b}") for b in range(2)]
        post_tmp = sem("post_tmp")
        dve_own, act_own, pool_own = sem("dve_own"), sem("act_own"), sem("pool_own")

        class Own:

            def __init__(self, eng, sem_):
                self.eng, self.sem, self.n = eng, sem_, 0

            def mark(self, ins):
                ins.then_inc(self.sem, 1)
                self.n += 1

            def wait(self, back=0):
                self.eng.wait_ge(self.sem, self.n - back)

            def link(self, ins):
                self.mark(ins)
                self.wait()

        def staged(ph, last):
            return NB[ph] if not last else (NB[NEXT[ph]] if NEXT[ph] else None)

        def pairs(eng, ph, body, first=0):
            n = NPIECE[ph] // 2
            if n - first > 2:
                with eng.Fori(first, n - 1) as i:
                    body(i, False)
            else:
                for i in range(first, n - 1):
                    body(i, False)
            body(n - 1, True)

        def stage_hi(act, ph, i, b, last):
            if staged(ph, last) is None:
                return
            n = staged(ph, last) * P
            act.wait_ge(raw_landed[b], 16 * (PIECE0[ph] // 2 + 2) + i * 16)
            act.wait_ge(seg_done, SEG0[ph] + NSEG[ph] * (b + 1) + i * (2 * NSEG[ph]))
            nc.scalar.activation(WH[b][:, 0:n], RAW[b][:, 0:n], ACT.Copy).then_inc(w_hi_done, 1)

        def stage_lo(dve, ph, i, b, last):
            if staged(ph, last) is None:
                return
            n = staged(ph, last) * P
            dve.wait_ge(w_hi_done, PIECE0[ph] + b + 3 + i * 2)
            nc.vector.tensor_tensor(WL[b][:, 0:n], RAW[b][:, 0:n], WH[b][:, 0:n].bitcast(F32),
                                    ALU.subtract).then_inc(w_lo_done, 1)

        def weights_ready(pe, ph, i, b):
            pe.wait_ge(w_lo_done, PIECE0[ph] + b + 1 + i * 2)

        def product(out_, b, j0, n, xh, xl, start=True, stop=True, ready=None):
            for k in range(n):
                if ready:
                    ready(k)
                w = slice((j0 + k) * P, (j0 + k + 1) * P)
                nc.tensor.matmul(out_, WH[b][:, w], xh[:, k, :], start=start and k == 0, stop=False)
                nc.tensor.matmul(out_, WH[b][:, w], xl[:, k, :], start=False, stop=False)
                last = nc.tensor.matmul(out_, WL[b][:, w], xh[:, k, :], start=False,
                                        stop=stop and k == n - 1)
            return last

        def turned(out_, x, eye):
            return nc.tensor.transpose(out_, x, eye)

        def square(act, k, m, src):
            if 8 * k + m >= 2:
                act.wait_ge(sq_used, 8 * k + m - 1)
            nc.scalar.activation(SQ[:, m % 2, :], src, ACT.Square).then_inc(sq_ready, 1)

        def add_squares(pe, k, m):
            pe.wait_ge(sq_ready, 8 * k + m + 1)
            column_sums(SQ[:, m % 2, :], m == 0, m == DC - 1).then_inc(sq_used, 1)

        def column_sums(sq, first, last):
            for t in range(T):
                ins = nc.tensor.matmul(ps[:, 7, t:t + 1], sq[:, t * P:(t + 1) * P], ones[:, 0:1],
                                       start=first and t == 0, stop=last and t == T - 1)
            return ins

        def spread_rms(pe, k):
            pe.wait_ge(rc_ready, k + 1)
            for t in range(T):
                last = nc.tensor.matmul(ps[:, 7, t * P:(t + 1) * P], RC[:, t:t + 1].to_broadcast([P, P]), ident[:, :],
                                        start=True, stop=True)
            last.then_inc(rows_ps, 1)

        def square_in(act, k, m, par, src):
            start = isinstance(m, int) and m == 0
            act.wait_ge(sq_used, 8 * k if start else m + (8 * k - 2))
            dst = TMP[:, 1:2, :] if start else SQ[:, par:par + 1, :]
            nc.scalar.activation(dst, src, ACT.Square).then_inc(sq_ready, 1)

        def gather(dve, k, m, par):
            dve.wait_ge(sq_ready, m + (8 * k + 1))
            dve.wait_ge(sq_used, m + (8 * k - 1))
            nc.vector.tensor_tensor(TMP[:, 1, :], TMP[:, 1, :], SQ[:, par, :], ALU.add).then_inc(sq_used, 1)

        def add_gathered(pe, k):
            pe.wait_ge(sq_used, 8 * k + 7)
            column_sums(TMP[:, 1, :], True, True).then_inc(sq_used, 1)

        def rms_root(act, k):
            act.wait_ge(ms_ready, k + 1)
            nc.scalar.activation(RC[:, :], RC[:, :], ACT.Sqrt).then_inc(rt_ready, 1)

        def rms_rest(dve, k):
            dve.wait_ge(sq_used, 8 * k + 8)
            nc.vector.tensor_scalar(RC[:, :], ps[:, 7, 0:T], 1.0 / D, EPS, ALU.mult, ALU.add).then_inc(ms_ready, 1)
            dve.wait_ge(rt_ready, k + 1)
            nc.vector.reciprocal(RC[:, :], RC[:, :]).then_inc(rc_ready, 1)
            dve.wait_ge(rows_ps, k + 1)
            nc.vector.tensor_copy(RR[:, :], ps[:, 7, :]).then_inc(rr_ready, 1)
            dve.wait_ge(rr_ready, k + 1)

        def pre_hi(act, j):
            for m in range(DC):
                act.wait_ge(in_tmp, 8 * (j - (j > 2)) + m + 1)
                nc.scalar.activation(AH[:, m, :], TMP[:, m % 2, :], ACT.Copy).then_inc(in_hi, 1)

        def pre_rest(dve, j, name):
            for m in range(DC + 1):
                if m < DC:
                    if m >= 2:
                        dve.wait_ge(in_lo, 8 * j + m - 1)
                    nc.vector.scalar_tensor_tensor(TMP[:, m % 2, :], hT[:, m, :], col(name, m),
                                                   RR[:, :], ALU.mult, ALU.mult).then_inc(in_tmp, 1)
                if m >= 1:
                    dve.wait_ge(in_hi, 8 * j + m)
                    nc.vector.tensor_tensor(AL[:, m - 1, :], TMP[:, (m - 1) % 2, :], AH[:, m - 1, :].bitcast(F32),
                                            ALU.subtract).then_inc(in_lo, 1)

        def y_bank(m):
            return ps[:, m % 7, :]

        def post_add(dve, j, name, first, y_of):
            for m in range(DC):
                post_chunk(dve, j, m, name, first[:, :] if first is not None and m == 0 else y_of(m))

        def post_chunk(dve, j, m, name, y):
            nc.vector.scalar_tensor_tensor(TMP[:, m % 2, :], y, col(name, m), RR[:, :], ALU.mult,
                                           ALU.mult).then_inc(post_tmp, 1)
            dve.wait_ge(post_tmp, 8 * j + m + 1)
            nc.vector.tensor_tensor(hT[:, m, :], hT[:, m, :], TMP[:, m % 2, :], ALU.add).then_inc(h_ready, 1)
        sf_saved = sem("sf_saved")
        small_done, sm_saved, l2_sq, l2_sum, l2_root, l2_rec, l2_done = (sem(n) for n in (
            "small_done", "sm_saved", "l2_sq", "l2_sum", "l2_root", "l2_rec", "l2_done"))
        g_ready, gsum_done, gsum_read, rows_done, at_ready = (sem(n) for n in (
            "g_ready", "gsum_done", "gsum_read", "rows_done", "at_ready"))
        tt_ready, t_ready, off_ready, y_ps, y_sb, d_ps, dt_ps = (sem(n) for n in (
            "tt_ready", "t_ready", "off_ready", "y_ps", "y_sb", "d_ps", "dt_ps"))
        kv_ps, kv_sb, wu_ps, wu_sb, state_ready, ws_ps, u_ready = (sem(n) for n in (
            "kv_ps", "kv_sb", "wu_ps", "wu_sb", "state_ready", "ws_ps", "u_ready"))
        ds_ps, o_sb, o_ps, on_ready, ot_ps, yt_ready, yt_hi, yt_lo = (sem(n) for n in (
            "ds_ps", "o_sb", "o_ps", "on_ready", "ot_ps", "yt_ready", "yt_hi", "yt_lo"))
        conv_base, conv_step, silu_done, dec_pre, dec_exp, sig_ready, soft = (sem(n) for n in (
            "conv_base", "conv_step", "silu_done", "dec_pre", "dec_exp", "sig_ready", "soft"))
        l2_rows, qd_ready, row_exp, gc_saved, o_sq, o_root, o_ms = (sem(n) for n in ("l2_rows", "qd_ready", "row_exp", "gc_saved", "o_sq", "o_root", "o_ms"))


        def ring(ph, c):
            return (RING0[ph] + c) % 4

        def bank_ready(pe, ph, c, i=0):
            pe.wait_ge(bank_free, RING0[ph] + c + 1 + i * 4)

        def seg_ready(eng, ph, s, i=0, per=4):
            eng.wait_ge(seg_done, SEG0[ph] + s + 1 + i * per)

        def feature_major(pe, ph, xh, xl, new=None):
            def body(i, last):
                for b in range(2):
                    weights_ready(pe, ph, i, b)
                    for s in range(2):
                        c = 2 * b + s
                        bank_ready(pe, ph, c, i)
                        product(ps[:, ring(ph, c), :], b, 8 * s, DC, xh, xl).then_inc(seg_done, 1)
            if new is None:
                return pairs(pe, ph, body)
            weights_ready(pe, ph, 0, 0)
            bank_ready(pe, ph, 1)
            for k in range(DC):
                pe.wait_ge(in_lo, 8 * new + k + 1)
                for s in range(2):
                    ins = product(ps[:, ring(ph, s), :], 0, 8 * s + k, 1, xh[:, k:k + 1, :], xl[:, k:k + 1, :],
                                  start=k == 0, stop=k == DC - 1)
                    if k == DC - 1:
                        ins.then_inc(seg_done, 1)
            weights_ready(pe, ph, 0, 1)
            for s in range(2):
                bank_ready(pe, ph, 2 + s)
                product(ps[:, ring(ph, 2 + s), :], 1, 8 * s, DC, xh, xl).then_inc(seg_done, 1)
            pairs(pe, ph, body, 1)

        def z_piece(pe, b):
            weights_ready(pe, "z", 0, b)
            for s in range(2):
                bank_ready(pe, "z", 2 * b + s)
                product(ps[:, ring("z", 2 * b + s), :], b, 8 * s, DC, AH, AL).then_inc(seg_done, 1)

        def z_bank(c):
            return ring("z", c) if c < 2 else 4 + c

        def gdn_pe(pe):
            pe.wait_ge(ws_split, 2)
            for k in range(DC):
                w = slice(k * 32, (k + 1) * 32)
                nc.tensor.matmul(ps[0:32, 7, :], WSH[:, w], AH[:, k, :], start=k == 0, stop=False)
                nc.tensor.matmul(ps[0:32, 7, :], WSH[:, w], AL[:, k, :], start=False, stop=False)
                last = nc.tensor.matmul(ps[0:32, 7, :], WSL[:, w], AH[:, k, :], start=False, stop=k == DC - 1)
            last.then_inc(small_done, 1)
            for n, sq in enumerate((TT, Y1)):
                pe.wait_ge(l2_sq, n + 1)
                for h in range(GH):
                    for t in range(T):
                        j = (n * GH + h) * T + t
                        last = nc.tensor.matmul(ps[:, 6, j:j + 1], sq[:, h, t, :], ones[:, 0:1], start=True, stop=True)
            last.then_inc(l2_sum, 1)
            pe.wait_ge(sf_saved, 1)
            for t in range(T):
                last = turned(ps[:, 5, t * 32:(t + 1) * 32], SF[0:32, t * P:(t + 1) * P], ident[0:32, 0:32])
            last.then_inc(small_done, 1)
            z_piece(pe, 0)
            pe.wait_ge(g_ready, 1)
            for n, c0 in enumerate((CON["tri"], CON["after"], CON["half"], CON["half"] + P)):
                last = nc.tensor.matmul(ps[:, 7, n * 16:(n + 1) * 16], CS[:, c0:c0 + P],
                                        G[:, :, :].rearrange("p t h -> p (t h)"), start=True, stop=True)
            last.then_inc(gsum_done, 1)
            pe.wait_ge(l2_rec, 1)
            for n in range(2):
                pe.wait_ge(bank_free, 4 + RING0["z"] + 2) if n == 0 else pe.wait_ge(gc_saved, 1)
                for h in range(GH):
                    for t in range(T):
                        j = (n * GH + h) * T + t
                        last = nc.tensor.matmul(ps[:, 4 * n + h, t * P:(t + 1) * P], L2[:, j:j + 1].to_broadcast([P, P]),
                                                ident[:, :], start=True, stop=True)
                last.then_inc(l2_rows, 1)
            pe.wait_ge(l2_done, 2)
            for t in range(T):
                tok = slice(t * P, (t + 1) * P)
                o = 4 * (t % 2)
                if t >= 2:
                    pe.wait_ge(at_ready, t - 1)
                for h in range(GH):
                    f = slice(h * P, (h + 1) * P)
                    nc.tensor.matmul(ps[:, o, f], G[:, t, h:h + 1].to_broadcast([P, P]), CS[:, 0:P], start=True, stop=True)
                    nc.tensor.matmul(ps[:, o + 1, f], SG[:, t, h:h + 1].to_broadcast([P, P]), ident[:, :], start=True, stop=True)
                    nc.tensor.matmul(ps[:, o + 2, f], QKV[:, 4 + h, tok], QKV[:, 4 + h, tok], start=True, stop=True)
                    last = nc.tensor.matmul(ps[:, o + 3, f], QKV[:, 4 + h, tok], QKV[:, h, tok], start=True, stop=True)
                last.then_inc(rows_done, 1)
            pe.wait_ge(at_ready, T)
            for t in range(T):
                pe.wait_ge(tt_ready, t + 1)
                for h in range(GH):
                    last = turned(ps[:, t, h * P:(h + 1) * P], TT[:, t, h, :], ident[:, :])
                last.then_inc(y_ps, 1)
            for lev in range(1, 6):
                for t in range(T):
                    n = 4 * lev + t
                    pe.wait_ge(off_ready, n - 3)
                    pe.wait_ge(t_ready, n - 3)
                    pe.wait_ge(tt_ready, n - 3)
                    for h in range(GH):
                        last = nc.tensor.matmul(ps[:, t, h * P:(h + 1) * P], OFF[:, t, h, :], Tm[:, t, h, :], start=True, stop=True)
                    last.then_inc(y_ps, 1)
                for t in range(T):
                    n = 4 * lev + t
                    pe.wait_ge(y_sb, n + 1 - 4)
                    pe.wait_ge(tt_ready, n - 3)
                    for h in range(GH):
                        last = nc.tensor.matmul(ps[:, 4 + t, h * P:(h + 1) * P], TT[:, t, h, :], Y1[:, t, h, :], start=True, stop=True)
                    last.then_inc(d_ps, 1)
                    for h in range(GH):
                        last = nc.tensor.matmul(ps[:, t, h * P:(h + 1) * P], Y1[:, t, h, :], TT[:, t, h, :], start=True, stop=True)
                    last.then_inc(dt_ps, 1)
            for t in range(T):
                tok = slice(t * P, (t + 1) * P)
                pe.wait_ge(tt_ready, 20 + t + 1)
                for n in range(2):
                    for h in range(GH):
                        last = turned(ps[:, 4 * n + t, h * P:(h + 1) * P], QKV[:, 4 + 4 * n + h, tok], ident[:, :])
                last.then_inc(kv_ps, 1)
            for t in range(T):
                pe.wait_ge(kv_sb, t + 1)
                for h in range(GH):
                    nc.tensor.matmul(ps[:, t, h * P:(h + 1) * P], OFF[:, t, h, :], TT[:, t, h, :], start=True, stop=True)
                    last = nc.tensor.matmul(ps[:, 4 + t, h * P:(h + 1) * P], TT[:, t, h, :], AT[:, t, h, :], start=True, stop=True)
                last.then_inc(wu_ps, 1)
            def z_late():
                weights_ready(pe, "z", 0, 1)
                for s in range(2):
                    for k in range(DC):
                        yield product(ps[:, 6 + s, :], 1, 8 * s + k, 1, AH[:, k:k + 1, :], AL[:, k:k + 1, :],
                                      start=k == 0, stop=k == DC - 1), k == DC - 1

            z_steps = z_late()

            def z_step():
                ins, whole = next(z_steps)
                if whole:
                    ins.then_inc(seg_done, 1)

            pe.wait_ge(wu_sb, 2 * T)
            for c in range(S // C):
                t, r = c // 2, C * (c % 2)
                rows, tok = slice(r, r + C), slice(c * C, (c + 1) * C)
                pe.wait_ge(state_ready, c + 1)
                for h in range(GH):
                    last = nc.tensor.matmul(ps[rows, 0, h * P:(h + 1) * P], Tm[:, t, h, rows], ST[:, c % 2, h, :], start=True, stop=True)
                last.then_inc(ws_ps, 1)
                z_step()
                pe.wait_ge(u_ready, c + 1)
                for h in range(GH):
                    last = nc.tensor.matmul(ps[:, 1 + c % 2, h * P:(h + 1) * P], QKV[rows, 8 + h, t * P:(t + 1) * P],
                                            Y1[rows, t, h, :], start=True, stop=True)
                last.then_inc(ds_ps, 1)
                if c >= 2:
                    pe.wait_ge(o_sb, c - 1)
                for h in range(GH):
                    nc.tensor.matmul(ps[rows, 3 + c % 2, h * P:(h + 1) * P], QKV[:, h, tok], ST[:, c % 2, h, :], start=True, stop=False)
                    last = nc.tensor.matmul(ps[rows, 3 + c % 2, h * P:(h + 1) * P], QK[rows, t, h, rows], Y1[rows, t, h, :],
                                            start=False, stop=True)
                last.then_inc(o_ps, 1)
                z_step()
            for t in range(T):
                pe.wait_ge(on_ready, t + 1)
                for h in range(GH):
                    last = turned(ps[:, 4 + t % 2, h * P:(h + 1) * P], AT[:, t, h, :], ident[:, :])
                last.then_inc(ot_ps, 1)
                if t >= 1:
                    pe.wait_ge(yt_ready, t)


        def flat(x):
            return x.rearrange("p a b -> p (a b)")

        def flat4(x):
            return x.rearrange("p a b c -> p (a b c)")

        def chunks(x, c, i, n=1):
            return x[:, c + 4 * i:c + 4 * i + n, :] if isinstance(i, int) else x[:, bass.ds(c + i * 4, n), :]

        def bank_read(eng, ph, c, i=0):
            eng.wait_ge(bank_free, 4 + RING0[ph] + c + 1 + i * 4)

        def qkv_act(act):
            def body(i, last):
                for b in range(2):
                    for s in range(2):
                        c = 2 * b + s
                        seg_ready(act, "qkv", c, i)
                        nc.scalar.mul(flat(Tm[:, c, :, :]), ps[:, ring("qkv", c), :],
                                      col("cqkv", (c * 4 + 3) + i * 16)).then_inc(conv_base, 1)
                    for s in range(2):
                        c = 2 * b + s
                        bank_read(act, "qkv", c, i)
                        nc.scalar.activation(chunks(QKV, c, i), Tm[:, c:c + 1, :, :].rearrange("p c a b -> p c (a b)"),
                                             ACT.Silu).then_inc(silu_done, 1)
                    stage_hi(act, "qkv", i, b, last)
            pairs(act, "qkv", body)

        def z_act(act, c):
            seg_ready(act, "z", c)
            nc.scalar.activation(ZS[:, c, :], ps[:, z_bank(c), :], ACT.Silu).then_inc(bank_free, 1)
            if c % 2:
                stage_hi(act, "z", 0, c // 2, True)

        def gdn_act(act):
            act.wait_ge(small_done, 1)
            nc.scalar.activation(SF[0:32, :], ps[0:32, 7, :], ACT.Copy).then_inc(sf_saved, 1)
            act.wait_ge(silu_done, 12)
            for n, sq in enumerate((TT, Y1)):
                nc.scalar.activation(flat4(sq[:, :, :, :]), flat(QKV[:, 4 * n:4 * n + 4, :]), ACT.Square).then_inc(l2_sq, 1)
            act.wait_ge(l2_sum, 1)
            nc.scalar.activation(L2[:, :], ps[:, 6, 0:2 * GH * T], ACT.Sqrt, bias=col("eps")).then_inc(l2_root, 1)
            act.wait_ge(small_done, 2)
            nc.scalar.activation(flat(SM[:, :, :]), ps[:, 5, 0:T * 32], ACT.Copy).then_inc(sm_saved, 1)
            nc.scalar.activation(EA[:, :], col("alog", 0, 4), ACT.Exp).then_inc(soft, 1)
            act.wait_ge(sm_saved, 1)
            nc.scalar.activation(SG[:, :, :], SM[:, :, :], ACT.Tanh, scale=0.5).then_inc(sig_ready, 1)
            act.wait_ge(soft, 2)
            nc.scalar.activation(AA[:, 1, :, :], AA[:, 1, :, :], ACT.Exp, scale=-1.0).then_inc(soft, 1)
            act.wait_ge(soft, 4)
            nc.scalar.activation(AA[:, 1, :, :], AA[:, 1, :, :], ACT.Ln).then_inc(soft, 1)
            z_act(act, 0)
            z_act(act, 1)
            act.wait_ge(gsum_done, 1)
            nc.scalar.activation(flat4(EX[:, :, :, :]), ps[:, 7, 0:64], ACT.Exp).then_inc(gsum_read, 1)
            for t in range(T):
                o = 4 * (t % 2)
                act.wait_ge(dec_pre, t + 1)
                nc.scalar.activation(flat(Y1[:, t, :, :]), ps[:, o, :], ACT.Exp).then_inc(row_exp, 1)
                nc.scalar.activation(Tm[:, t, :, :], Tm[:, t, :, :], ACT.Exp).then_inc(dec_exp, 1)
            for t in range(T):
                act.wait_ge(y_ps, t + 1)
                nc.scalar.activation(flat(Tm[:, t, :, :]), ps[:, t, :], ACT.Copy).then_inc(t_ready, 1)
            act.wait_ge(qd_ready, T)
            for lev in range(1, 6):
                for t in range(T):
                    act.wait_ge(y_ps, 4 * lev + t + 1)
                    nc.scalar.activation(flat(Y1[:, t, :, :]), ps[:, t, :], ACT.Copy).then_inc(y_sb, 1)
            for t in range(T):
                act.wait_ge(wu_ps, t + 1)
                nc.scalar.activation(flat(Tm[:, t, :, :]), ps[:, t, :], ACT.Copy).then_inc(wu_sb, 1)
                nc.scalar.activation(flat(Y1[:, t, :, :]), ps[:, 4 + t, :], ACT.Copy).then_inc(wu_sb, 1)
            for c in range(S // C):
                t, rows = c // 2, slice(C * (c % 2), C * (c % 2) + C)
                act.wait_ge(o_ps, c + 1)
                nc.scalar.activation(flat(AT[rows, t, :, :]), ps[rows, 3 + c % 2, :], ACT.Copy).then_inc(o_sb, 1)
                if c % 2:
                    act.wait_ge(o_sb, c + 1)
                    nc.scalar.activation(OFF[:, t, :, :], AT[:, t, :, :], ACT.Square).then_inc(o_sq, 1)
                if c == 5:
                    z_act(act, 2)
            z_act(act, 3)
            act.wait_ge(o_ms, 1)
            nc.scalar.activation(RO[:, :, :], RO[:, :, :], ACT.Sqrt).then_inc(o_root, 1)
            for t in range(T):
                act.wait_ge(yt_ready, t + 1)
                nc.scalar.activation(YAH[:, :, t * P:(t + 1) * P], TMP[:, t % 2, :].rearrange("p (h n) -> p h n", h=GH),
                                     ACT.Copy).then_inc(yt_hi, 1)

        def qkv_dve(dve):
            def body(i, last):
                for b in range(2):
                    for s in range(2):
                        c = 2 * b + s
                        y = flat(Tm[:, c, :, :])
                        dve.wait_ge(conv_base, c + 1 + i * 4)
                        for j in range(1, 4):
                            if j > 1:
                                dve.wait_ge(conv_step, 2 * c + j - 1 + i * 8)
                            nc.vector.scalar_tensor_tensor(
                                y[:, j:S], ps[:, ring("qkv", c), 0:S - j], col("cqkv", (c * 4 + 3 - j) + i * 16),
                                y[:, j:S], ALU.mult, ALU.add).then_inc(conv_step if j < 3 else bank_free, 1)
                    stage_lo(dve, "qkv", i, b, last)
            pairs(dve, "qkv", body)

        def split_small_act(act):
            act.wait_ge(con_landed, 16 * N_CON)
            nc.scalar.activation(WSH[:, :], WSR[:, :], ACT.Copy).then_inc(ws_split, 1)

        def split_small_dve(dve):
            dve.wait_ge(ws_split, 1)
            nc.vector.tensor_tensor(WSL[:, :], WSR[:, :], WSH[:, :].bitcast(F32), ALU.subtract).then_inc(ws_split, 1)

        def gdn_dve(dve, own):
            vec = nc.vector
            dve.wait_ge(l2_root, 1)
            vec.reciprocal(L2[:, :], L2[:, :]).then_inc(l2_rec, 1)
            dve.wait_ge(sig_ready, 1)
            own.mark(vec.tensor_scalar(SG[:, :, :], SG[:, :, :], 0.5, 0.5, ALU.mult, ALU.add))
            dtb = col("dtb", 0, 4).unsqueeze(1).to_broadcast([P, T, GH])
            own.link(vec.tensor_tensor(AA[:, 0, :, :], SM[:, :, 4:8], dtb, ALU.add))
            own.link(vec.tensor_scalar(AA[:, 2, :, :], AA[:, 0, :, :], -1.0, None, ALU.mult))
            vec.tensor_tensor(AA[:, 1, :, :], AA[:, 0, :, :], AA[:, 2, :, :], ALU.max).then_inc(soft, 1)
            dve.wait_ge(soft, 3)
            vec.tensor_scalar(AA[:, 1, :, :], AA[:, 1, :, :], 1.0, None, ALU.add).then_inc(soft, 1)
            dve.wait_ge(soft, 5)
            own.link(vec.scalar_tensor_tensor(AA[:, 0, :, :], AA[:, 0, :, :], 0.0, AA[:, 1, :, :], ALU.max, ALU.add))
            ea = EA[:, :].unsqueeze(1).to_broadcast([P, T, GH])
            vec.scalar_tensor_tensor(G[:, :, :], AA[:, 0, :, :], -1.0, ea, ALU.mult, ALU.mult).then_inc(g_ready, 1)
            stage_lo(dve, "z", 0, 0, True)
            dve.wait_ge(gsum_read, 1)
            vec.tensor_copy(flat(GC[:, :, :]), ps[:, 7, 0:16]).then_inc(gc_saved, 1)
            dve.wait_ge(gc_saved, 1)
            own.link(vec.tensor_tensor(BG[:, :, :], SG[:, :, 0:GH], EX[:, 0, :, :], ALU.mult))
            nc.vector.memset(ST[:, :, :, :], 0.0).then_inc(state_ready, 1)
            for n in range(2):
                dve.wait_ge(l2_rows, n + 1)
                x = flat(QKV[:, 4 * n:4 * n + 4, :])
                vec.scalar_tensor_tensor(x, x, float(P) ** -0.5 if n == 0 else 1.0, flat(ps[:, 4 * n:4 * n + 4, :]),
                                         ALU.mult, ALU.mult).then_inc(l2_done, 1)
            for t in range(T):
                o = 4 * (t % 2)
                dve.wait_ge(rows_done, t + 1)
                for h in range(GH):
                    ins = vec.scalar_tensor_tensor(Tm[:, t, h, :], ps[:, o, h * P:(h + 1) * P], GC[:, t, h:h + 1],
                                                   CS[:, CON["seen"]:CON["seen"] + P], ALU.subtract, ALU.min)
                ins.then_inc(dec_pre, 1)
                dve.wait_ge(dec_exp, t + 1)
                own.mark(vec.tensor_tensor(flat(QK[:, t, :, :]), ps[:, o + 3, :], flat(Tm[:, t, :, :]), ALU.mult))
                own.link(vec.tensor_tensor(flat(AT[:, t, :, :]), ps[:, o + 2, :], flat(Tm[:, t, :, :]), ALU.mult))
                vec.tensor_tensor(flat(AT[:, t, :, :]), flat(AT[:, t, :, :]), ps[:, o + 1, :], ALU.mult).then_inc(at_ready, 1)
            level = [CS[:, CON["level"] + n * P:CON["level"] + (n + 1) * P].unsqueeze(1).to_broadcast([P, GH, P])
                     for n in range(6)]
            eye = ident[:, :].unsqueeze(1).to_broadcast([P, GH, P])
            for t in range(T):
                dve.wait_ge(at_ready, t + 1)
                own.link(vec.tensor_tensor(TT[:, t, :, :], AT[:, t, :, :], level[0], ALU.mult))
                vec.scalar_tensor_tensor(TT[:, t, :, :], TT[:, t, :, :], -1.0, eye, ALU.mult, ALU.add).then_inc(tt_ready, 1)
            for lev in range(1, 6):
                for t in range(T):
                    n = 4 * lev + t
                    if lev < 5:
                        dve.wait_ge(d_ps, n - 3)
                        vec.tensor_tensor(flat(Tm[:, t, :, :]), flat(Tm[:, t, :, :]), ps[:, 4 + t, :],
                                          ALU.subtract).then_inc(t_ready, 1)
                    dve.wait_ge(dt_ps, n - 3)
                    vec.tensor_tensor(flat(TT[:, t, :, :]), flat(TT[:, t, :, :]), ps[:, t, :],
                                      ALU.subtract).then_inc(tt_ready, 1)
            for t in range(T):
                tok = slice(t * P, (t + 1) * P)
                wide = lambda x: x.unsqueeze(2).to_broadcast([P, GH, P])
                heads = lambda x: x.rearrange("p (h n) -> p h n", h=GH)
                dve.wait_ge(kv_ps, t + 1)
                vec.tensor_tensor(OFF[:, t, :, :], heads(ps[:, t, :]), wide(BG[:, t, :]), ALU.mult)
                vec.tensor_tensor(AT[:, t, :, :], heads(ps[:, 4 + t, :]), wide(SG[:, t, 0:GH]), ALU.mult)
                vec.tensor_tensor(QKV[:, 8:12, tok], heads(ps[:, t, :]), wide(EX[:, 1, t, :]), ALU.mult).then_inc(kv_sb, 1)
            for c in range(S // C):
                t, rows = c // 2, slice(C * (c % 2), C * (c % 2) + C)
                dve.wait_ge(ws_ps, c + 1)
                u = flat(Y1[rows, t, :, :])
                vec.tensor_tensor(u, u, ps[rows, 0, :], ALU.subtract).then_inc(u_ready, 1)
                dve.wait_ge(ds_ps, c + 1)
                if c:
                    dve.wait_ge(o_ps, c)
                for h in range(GH):
                    ins = vec.scalar_tensor_tensor(ST[:, (c + 1) % 2, h, :], ST[:, c % 2, h, :], EX[:, 2 + c % 2, t, h:h + 1],
                                                   ps[:, 1 + c % 2, h * P:(h + 1) * P], ALU.mult, ALU.add)
                ins.then_inc(state_ready, 1)
            stage_lo(dve, "z", 0, 1, True)
            for t in range(T):
                dve.wait_ge(o_sq, t + 1)
                ins = vec.tensor_reduce(RO[:, t, :], OFF[:, t, :, :], AX, ALU.add)
            own.link(ins)
            vec.tensor_scalar(RO[:, :, :], RO[:, :, :], 1.0 / P, EPS, ALU.mult, ALU.add).then_inc(o_ms, 1)
            dve.wait_ge(o_root, 1)
            own.link(vec.reciprocal(RO[:, :, :], RO[:, :, :]))
            for t in range(T):
                vec.tensor_tensor(AT[:, t, :, :], AT[:, t, :, :], RO[:, t, :].unsqueeze(2).to_broadcast([P, GH, P]),
                                  ALU.mult).then_inc(on_ready, 1)
            bank_read(dve, "z", 3)
            for t in range(T):
                tok = slice(t * P, (t + 1) * P)
                dve.wait_ge(ot_ps, t + 1)
                tmp = TMP[:, t % 2, :].rearrange("p (h n) -> p h n", h=GH)
                if t >= 2:
                    dve.wait_ge(yt_lo, t - 1)
                vec.scalar_tensor_tensor(tmp, ps[:, 4 + t % 2, :].rearrange("p (h n) -> p h n", h=GH), col("gdn"),
                                         ZS[:, :, tok], ALU.mult, ALU.mult).then_inc(yt_ready, 1)
                dve.wait_ge(yt_hi, t + 1)
                vec.tensor_tensor(YAL[:, :, tok], tmp, YAH[:, :, tok].bitcast(F32), ALU.subtract).then_inc(yt_lo, 1)

        def gdn_pool(pool):
            for t in range(T):
                qd = QKV[:, 0:GH, t * P:(t + 1) * P]
                pool.wait_ge(row_exp, t + 1)
                nc.gpsimd.tensor_tensor(qd, qd, Y1[:, t, :, :], ALU.mult).then_inc(qd_ready, 1)
            for lev in range(1, 6):
                m = CS[:, CON["level"] + lev * P:CON["level"] + (lev + 1) * P].unsqueeze(1).to_broadcast([P, GH, P])
                for t in range(T):
                    pool.wait_ge(at_ready, T)
                    if lev > 1:
                        pool.wait_ge(y_ps, 4 * (lev - 1) + t + 1)
                    nc.gpsimd.tensor_tensor(OFF[:, t, :, :], AT[:, t, :, :], m, ALU.mult).then_inc(off_ready, 1)

        comp_ready, z_ready, hid_ps, hid_ready, kv_c_ps, kv_c_sb = (sem(n) for n in (
            "comp_ready", "z_ready", "hid_ps", "hid_ready", "kv_c_ps", "kv_c_sb"))
        cs_ps, cs_max, cs_exp, cs_pr, cp_ps, cp_sb, co_ps, co_done = (sem(n) for n in (
            "cs_ps", "cs_max", "cs_exp", "cs_pr", "cp_ps", "cp_sb", "co_ps", "co_done"))
        s_ps, s_max, p_ready, pt_ps, o2_ps, o2_done = (sem(n) for n in (
            "s_ps", "s_max", "p_ready", "pt_ps", "o2_ps", "o2_done"))
        pt_sb = [sem(f"pt_sb{b}") for b in range(2)]
        yb_ps, yb_hi, yb_lo, mb_ready = (sem(n) for n in ("yb_ps", "yb_hi", "yb_lo", "mb_ready"))
        gate_ready, mix_sum, mix_hi, mix_lo, mix_ab = (sem(n) for n in (
            "gate_ready", "mix_sum", "mix_hi", "mix_lo", "mix_ab"))
        UNITS = [(qt, h, x) for qt in reversed(range(T)) for h in range(NH) for x in range(2)]

        def nsa_proj_pe(pe):
            feature_major(pe, "nq", AH, AL)
            for b in range(2):
                weights_ready(pe, "ncmp", 0, b)
                bank_ready(pe, "ncmp", b)
                product(ps[:, ring("ncmp", b), :], b, 0, DC, AH, AL).then_inc(seg_done, 1)
            weights_ready(pe, "nk", 0, 0)
            for s in range(2):
                bank_ready(pe, "nk", s)
                product(ps[:, ring("nk", s), :], 0, 8 * s, DC, AH, AL).then_inc(seg_done, 1)

        def nv_pe(pe, c):
            pe.wait_ge(w_lo_done, PIECE0["nv"] + 1)
            bank_ready(pe, "nv", c)
            for t in (2 * c, 2 * c + 1):
                tok = slice(t * P, (t + 1) * P)
                o = ps[:, ring("nv", c), (t % 2) * 256:(t % 2) * 256 + 256]
                for k in range(DC):
                    w = slice(k * 256, (k + 1) * 256)
                    nc.tensor.matmul(o, AH[:, k, tok], WH[1][:, w], start=k == 0, stop=False)
                    nc.tensor.matmul(o, AL[:, k, tok], WH[1][:, w], start=False, stop=False)
                    last = nc.tensor.matmul(o, AH[:, k, tok], WL[1][:, w], start=False, stop=k == DC - 1)
            last.then_inc(seg_done, 1)

        def nsa_proj_act(act):
            for b in range(2):
                stage_hi(act, "nq", 0, b, True)
            for b in range(2):
                stage2_hi(act, "ncmp", b)
            stage2_hi(act, "nk", 0)

        def nsa_proj_dve(dve):
            for m in range(4):
                seg_ready(dve, "nq", m)
                for s in range(2):
                    ins = nc.vector.tensor_scalar(QT[0:DK, 2 * m + s, :], ps[s * DK:(s + 1) * DK, ring("nq", m), :],
                                                  DK ** -0.5, None, ALU.mult)
                ins.then_inc(bank_free, 1)
                if m % 2:
                    stage_lo(dve, "nq", 0, m // 2, True)
            dve.wait_ge(cols_landed, 16)
            for x in range(2):
                dve.wait_ge(seg_done, SEG0["ncmp"] + x + 1)
                pos = cols[:, COLS["posk" if x == 0 else "posv"]:][:, 0:16]
                for g in range(NG):
                    src = ps[g * DK:(g + 1) * DK, ring("ncmp", x), :].rearrange("p (n k j) -> p j k n", k=8, j=2)
                    for par in range(2):
                        half = slice(par * DK, (par + 1) * DK)
                        for late in range(2):
                            ins = nc.vector.tensor_tensor(
                                Z[x][half, 8 * late:8 * late + 8, g * NC:(g + 1) * NC],
                                src[:, par, :, late:late + NC],
                                pos[half, 8 * late:8 * late + 8].unsqueeze(2).to_broadcast([DK, 8, NC]), ALU.add)
                ins.then_inc(bank_free, 1)
                stage2_lo(dve, "ncmp", x)
            for x in range(2):
                seg_ready(dve, "nk", x)
                for g in range(NG):
                    ins = nc.vector.tensor_copy(KT[0:DK, x, g, :], ps[g * DK:(g + 1) * DK, ring("nk", x), :])
                ins.then_inc(bank_free, 1)
            stage2_lo(dve, "nk", 0)

        def nv_dve(dve, c):
            seg_ready(dve, "nv", c)
            nc.vector.tensor_copy(flat(V1[:, 2 * c:2 * c + 2, :]), ps[:, ring("nv", c), :]).then_inc(bank_free, 1)

        def stage2_hi(act, ph, b):
            piece = PIECE0[ph] + (b if NPIECE[ph] > 1 else 0)
            n = PIECE_NB[piece + 2] * P
            act.wait_ge(raw_landed[b], 16 * ((piece + 2) // 2 + 1))
            act.wait_ge(seg_done, PIECE_SEG[piece + 1])
            nc.scalar.activation(WH[b][:, 0:n], RAW[b][:, 0:n], ACT.Copy).then_inc(w_hi_done, 1)

        def stage2_lo(dve, ph, b):
            piece = PIECE0[ph] + (b if NPIECE[ph] > 1 else 0)
            n = PIECE_NB[piece + 2] * P
            dve.wait_ge(w_hi_done, piece + 3)
            nc.vector.tensor_tensor(WL[b][:, 0:n], RAW[b][:, 0:n], WH[b][:, 0:n].bitcast(F32),
                                    ALU.subtract).then_inc(w_lo_done, 1)

        def nsa_pe(pe):
            def scores(u):
                qt, h, x = UNITS[u]
                n, bank = (qt + 1) * P, u % 4
                if u >= 4:
                    pe.wait_ge(p_ready, u - 3)
                else:
                    bank_read(pe, "nv", u) if u < 2 else pe.wait_ge(cp_sb, 1)
                nc.tensor.matmul(ps[:, bank, 0:n], QT[0:66, h, qt * P:n], KT[0:66, x, h // R, 0:n], start=True, stop=False)
                nc.tensor.matmul(ps[:, bank, qt * P:n], MB[:, 0, :], MB[:, 1, :], start=False, stop=True).then_inc(s_ps, 1)

            pe.wait_ge(w1_landed, 32)
            bank_read(pe, "ncmp", 1)
            for x in range(2):
                for f in range(2):
                    o = ps[:, 4, (2 * x + f) * 64:(2 * x + f) * 64 + 2 * NC]
                    for k in range(16):
                        last = nc.tensor.matmul(o, W1[x][:, k, f * P:(f + 1) * P], Z[x][:, k, :], start=k == 0, stop=k == 15)
            last.then_inc(hid_ps, 1)
            nv_pe(pe, 0)
            pe.wait_ge(nsa_landed, 16 * N_NSA)
            pe.wait_ge(hid_ready, 1)
            for f in range(2):
                nc.tensor.matmul(ps[0:DK, 5, 0:2 * NC], W2[:, f, :], HID[:, f, :], start=f == 0, stop=f == 1)
            for g in range(NG):
                for r in range(R):
                    for f in range(2):
                        last = nc.tensor.matmul(ps[32 * r:32 * r + NC, 6 + g, 0:DK], HID[:, 2 + f, g * NC:(g + 1) * NC],
                                                W2[:, 2 + f, :], start=f == 0, stop=f == 1)
            last.then_inc(kv_c_ps, 1)
            pe.wait_ge(kv_c_sb, 1)
            for qt in range(T):
                for h in range(NH):
                    last = nc.tensor.matmul(ps[:, 4 + qt // 2, (qt % 2) * 256 + h * 32:(qt % 2) * 256 + h * 32 + 32],
                                            QT[0:66, h, qt * P:(qt + 1) * P], KC[0:66, h // R, :], start=True, stop=True)
            last.then_inc(cs_ps, 1)
            nv_pe(pe, 1)
            bank_read(pe, "nk", 1)
            pe.wait_ge(mb_ready, 2)
            pe.wait_ge(cs_pr, 1)
            for qt in range(T):
                for g in range(NG):
                    j = (qt % 2) * 2 + g
                    last = turned(ps[:, 2 + qt // 2, j * P:(j + 1) * P],
                                               SC[:, qt, g * R:(g + 1) * R, :].rearrange("p a b -> p (a b)"), ident[:, :])
            last.then_inc(cp_ps, 1)
            scores(0)
            scores(1)
            pe.wait_ge(cp_sb, 1)
            for qt in range(T):
                for g in range(NG):
                    j = (qt % 2) * 2 + g
                    last = nc.tensor.matmul(ps[:, 4 + qt, g * 256:(g + 1) * 256], PT[:, qt // 2, j * P:(j + 1) * P],
                                            VB[:, g, :], start=True, stop=True)
            last.then_inc(co_ps, 1)
            def turn(u):
                qt, h, x = UNITS[u]
                pe.wait_ge(p_ready, u + 1)
                pe.wait_ge(pt_sb[u % 2], u // 2) if u >= 2 else pe.wait_ge(co_done, 1)
                for kt in range(qt + 1):
                    last = turned(ps[:, 4 + u % 2, kt * P:(kt + 1) * P], PR[:, u % 4, kt * P:(kt + 1) * P], ident[:, :])
                last.then_inc(pt_ps, 1)

            def values(u):
                qt, h, x = UNITS[u]
                g, pair = h // R, u // 2
                pe.wait_ge(pt_sb[u % 2], u // 2 + 1)
                if u == 0:
                    pe.wait_ge(co_done, 2)
                if pair >= 2 and x == 0:
                    pe.wait_ge(o2_done, pair - 1)
                for kt in range(qt + 1):
                    last = nc.tensor.matmul(ps[:, 6 + pair % 2, x * DK:(x + 1) * DK], PT[:, u % 4, kt * P:(kt + 1) * P],
                                            V1[:, kt, x * P + g * DK:x * P + (g + 1) * DK], start=kt == 0, stop=kt == qt)
                last.then_inc(o2_ps, 1)

            n = len(UNITS)
            for u in range(n + 1):
                if u + 2 < n:
                    scores(u + 2)
                if u < n:
                    turn(u)
                if u:
                    values(u - 1)
            pe.wait_ge(o2_done, n // 2)
            for qt in range(T):
                for c in range(4):
                    last = turned(ps[:, qt, c * P:(c + 1) * P], Y[:, qt, c * P:(c + 1) * P], ident[:, :])
                last.then_inc(yb_ps, 1)

        def save_probs(eng, copy, u):
            n = (UNITS[u][0] + 1) * P
            eng.wait_ge(pt_ps, u + 1)
            if u >= 4:
                eng.wait_ge(o2_ps, u - 3)
            copy(PT[:, u % 4, 0:n], ps[:, 4 + u % 2, 0:n]).then_inc(pt_sb[u % 2], 1)

        def nsa_act(act):
            act.wait_ge(hid_ps, 1)
            nc.scalar.activation(HID[:, :, :], ps[:, 4, 0:256].rearrange("p (a n) -> p a n", a=4)[:, :, 0:2 * NC],
                                 ACT.Gelu_apprx_tanh).then_inc(hid_ready, 1)
            act.wait_ge(cs_max, 1)
            nc.scalar.activation(SC[:, :, :, :], SC[:, :, :, :], ACT.Exp).then_inc(cs_exp, 1)
            stage2_hi(act, "nv", 1)
            for u, (qt, h, x) in enumerate(UNITS + [(0, 0, 0)]):
                n, pair = (qt + 1) * P, u // 2
                if u == len(UNITS):
                    save_probs(act, nc.scalar.copy, u - 1)
                    break
                act.wait_ge(s_max, u + 1)
                if u >= 4:
                    act.wait_ge(pt_ps, u - 3)
                if pair >= 4 and x == 0:
                    act.wait_ge(o2_done, pair - 3)
                nc.scalar.activation(PR[:, u % 4, 0:n], ps[:, u % 4, 0:n], ACT.Exp, bias=NM[:, u % 4, :],
                                     accum_out=LS[:, pair % 4, x:x + 1]).then_inc(p_ready, 1)
                if u and u % 2 == 0:
                    save_probs(act, nc.scalar.copy, u - 1)
            for qt in range(T):
                act.wait_ge(yb_ps, qt + 1)
                nc.scalar.activation(YBH[:, :, qt * P:(qt + 1) * P], ps[:, qt, :].rearrange("p (c n) -> p c n", c=4),
                                     ACT.Copy).then_inc(yb_hi, 1)

        def nsa_dve(dve, own):
            vec = nc.vector
            dve.wait_ge(nsa_landed, 16 * N_NSA)
            own.mark(vec.memset(KC[0:DK, :, :], 0.0))
            own.link(vec.memset(VB[:, :, :], 0.0))
            nv_dve(dve, 0)
            dve.wait_ge(kv_c_ps, 1)
            for g in range(NG):
                vec.tensor_copy(KC[0:DK, g, 0:NC], ps[0:DK, 5, g * NC:(g + 1) * NC])
                for r in range(R):
                    ins = vec.tensor_copy(VB[32 * r:32 * r + NC, g, r * DK:(r + 1) * DK], ps[32 * r:32 * r + NC, 6 + g, 0:DK])
            ins.then_inc(kv_c_sb, 1)
            dve.wait_ge(cs_ps, 1)
            rows = SC[:, :, :, :].rearrange("p t h n -> p (t h) n")
            for b in range(2):
                cn = CN[:, 2 * b:2 * b + 2, :].unsqueeze(2).to_broadcast([P, 2, NH, 32])
                ins = vec.tensor_tensor(SC[:, 2 * b:2 * b + 2, :, :], ps[:, 4 + b, :].rearrange("p (t h n) -> p t h n", t=2, h=NH),
                                        cn, ALU.add)
                own.mark(ins)
            own.wait()
            mx, l, gl = (SX[:, n, :, :].rearrange("p t h -> p (t h)") for n in range(3))
            own.link(vec.tensor_reduce(mx, rows, AX, ALU.max))
            vec.tensor_tensor(rows, rows, mx.unsqueeze(2).to_broadcast([P, T * NH, 32]), ALU.subtract).then_inc(cs_max, 1)
            dve.wait_ge(cs_exp, 1)
            c01 = C01[:, :, :].unsqueeze(2).to_broadcast([P, T, NH, 32])
            vec.tensor_tensor(SC[:, :, :, :], SC[:, :, :, :], c01, ALU.mult).then_inc(cs_pr, 1)
            nv_dve(dve, 1)
            dve.wait_ge(cs_pr, 1)
            own.link(vec.tensor_reduce(l, rows, AX, ALU.add))
            own.link(vec.tensor_scalar(l, l, 1e-30, None, ALU.max))
            own.link(vec.reciprocal(l, l))
            gate = lambda t, h, j: SG[:, t, 8 + 3 * h + j:8 + 3 * h + j + 1]
            own.link(vec.tensor_tensor(SX[:, 2, :, :], SX[:, 1, :, :],
                                       SG[:, :, 8:32].rearrange("p t (h j) -> p t h j", j=3)[:, :, :, 0], ALU.mult))
            dve.wait_ge(cp_ps, 1)
            vec.tensor_copy(PT[:, 0:2, :], ps[:, 2:4, :]).then_inc(cp_sb, 1)
            def top(u):
                qt, h, x = UNITS[u]
                dve.wait_ge(s_ps, u + 1)
                vec.tensor_reduce(NM[:, u % 4, :], ps[:, u % 4, 0:(qt + 1) * P], AX, ALU.max, negate=True).then_inc(s_max, 1)

            top(0)
            top(1)
            dve.wait_ge(co_ps, 1)
            for qt in range(T):
                ins = vec.tensor_tensor(Y[:, qt, :].rearrange("p (h d) -> p h d", h=NH),
                                        ps[:, 4 + qt, :].rearrange("p (h d) -> p h d", h=NH),
                                        SX[:, 2, qt, :].unsqueeze(2).to_broadcast([P, NH, DK]), ALU.mult)
                if qt % 2:
                    ins.then_inc(co_done, 1)
            dve.wait_ge(co_done, 2)

            def add(pair):
                qt, h, _ = UNITS[2 * pair]
                b = pair % 2
                dve.wait_ge(o2_ps, 2 * pair + 2)
                own.link(vec.reciprocal(RL[:, b, :], LS[:, pair % 4, :]))
                own.link(vec.tensor_tensor(RL[:, b, :], RL[:, b, :], SG[:, qt, 9 + 3 * h:11 + 3 * h], ALU.mult))
                y = Y[:, qt, h * DK:(h + 1) * DK]
                own.link(vec.scalar_tensor_tensor(y, ps[:, 6 + b, 0:DK], RL[:, b, 0:1], y, ALU.mult, ALU.add))
                vec.scalar_tensor_tensor(y, ps[:, 6 + b, DK:2 * DK], RL[:, b, 1:2], y, ALU.mult, ALU.add).then_inc(o2_done, 1)

            n = len(UNITS)
            for u in range(n + 1):
                if u == 4:
                    stage2_lo(dve, "nv", 1)
                if u + 2 < n:
                    top(u + 2)
                if u < n and u % 2 == 0:
                    save_probs(dve, vec.tensor_copy, u)
                if u and u % 2 == 0:
                    add(u // 2 - 1)
            for qt in range(T):
                tok = slice(qt * P, (qt + 1) * P)
                dve.wait_ge(yb_hi, qt + 1)
                vec.tensor_tensor(YBL[:, :, tok], ps[:, qt, :].rearrange("p (c n) -> p c n", c=4),
                                  YBH[:, :, tok].bitcast(F32), ALU.subtract).then_inc(yb_lo, 1)

        def mix_pe(pe):
            pe.wait_ge(yb_lo, T)
            pe.wait_ge(yt_lo, T)
            def body(i, last):
                for b in range(2):
                    weights_ready(pe, "mix", i, b)
                    y_h, y_l = (YAH, YAL) if b == 0 else (YBH, YBL)
                    bank_ready(pe, "mix", 2 * b, i)
                    product(ps[:, ring("mix", 2 * b), :], b, 0, DC, AH, AL).then_inc(seg_done, 1)
                    bank_ready(pe, "mix", 2 * b + 1, i)
                    product(ps[:, ring("mix", 2 * b + 1), :], b, DC, 4, y_h, y_l).then_inc(seg_done, 1)
            pairs(pe, "mix", body)

        def at(x, m):
            return x[:, m:m + 1, :] if isinstance(m, int) else x[:, bass.ds(m, 1), :]

        def mix_act(act):
            def body(i, last):
                for b in range(2):
                    seg_ready(act, "mix", 2 * b, i)
                    nc.scalar.activation(SQ[:, b, :], ps[:, ring("mix", 2 * b), :], ACT.Tanh, scale=0.5).then_inc(gate_ready, 1)
                    stage_hi(act, "mix", i, b, last)
                act.wait_ge(mix_sum, i + 1)
                nc.scalar.activation(at(GHI, i), TMP[:, 0:1, :], ACT.Copy, scale=0.5).then_inc(mix_hi, 1)
            pairs(act, "mix", body)

        def mix_dve(dve):
            def body(i, last):
                for b in range(2):
                    dve.wait_ge(gate_ready, b + 1 + i * 2)
                    seg_ready(dve, "mix", 2 * b + 1, i)
                    nc.vector.scalar_tensor_tensor(TMP[:, b, :], SQ[:, b, :], 1.0, ps[:, ring("mix", 2 * b + 1), :],
                                                   ALU.add, ALU.mult).then_inc(bank_free, 2)
                    stage_lo(dve, "mix", i, b, last)
                bank_read(dve, "mix", 3, i)
                nc.vector.tensor_tensor(TMP[:, 0, :], TMP[:, 0, :], TMP[:, 1, :], ALU.add).then_inc(mix_sum, 1)
                dve.wait_ge(mix_hi, i + 1)
                nc.vector.scalar_tensor_tensor(at(GLO, i), TMP[:, 0:1, :], 0.5, at(GHI, i).bitcast(F32),
                                               ALU.mult, ALU.subtract).then_inc(mix_lo, 1)
                dve.wait_ge(mix_lo, i + 1)
            pairs(dve, "mix", body)

        def wide_product(pe, ph, k, xh, xl, freed, count):
            for m in range(DC):
                if m % 2 == 0:
                    weights_ready(pe, ph, m // 4, m // 2 % 2)
                if m == 7:
                    pe.wait_ge(freed, count)
                product(y_bank(m), m // 2 % 2, 8 * (m % 2), DC, xh, xl).then_inc(seg_done, 1)
            add_gathered(pe, k)

        def down_pe(pe, ph, k, freed, count):
            def chunk(m, bank):
                for b in range(2):
                    weights_ready(pe, ph, m, b)
                    product(bank, b, 0, FC // 2, HH[:, b * 11:b * 11 + 11, :], HL[:, b * 11:b * 11 + 11, :],
                            start=b == 0, stop=b == 1).then_inc(seg_done, 1)
            with pe.Fori(0, 7) as m:
                chunk(m, ps[:, bass.ds(m, 1), :])
            pe.wait_ge(freed, count)
            chunk(7, ps[:, 0:1, :])
            add_gathered(pe, k)

        def wo_act(act):
            for m in range(DC):
                seg_ready(act, "wo", m)
                square_in(act, 1, m, m % 2, ps[:, m % 7:m % 7 + 1, :])
                if m % 2:
                    stage_hi(act, "wo", m // 4, m // 2 % 2, m >= 4)

        def wo_dve(dve):
            dve.wait_ge(sq_ready, 8 + 1)
            nc.vector.tensor_copy(YX[:, :], ps[:, 0, :]).then_inc(y0_saved, 1)
            for p in range(4):
                for m in (2 * p, 2 * p + 1):
                    if m:
                        gather(dve, 1, m, m % 2)
                stage_lo(dve, "wo", p // 2, p % 2, p >= 2)

        def up_pe(pe, ph, j):
            pe.wait_ge(in_lo, 8 * j + 1)
            def body(i, last):
                for b in range(2):
                    weights_ready(pe, ph, i, b)
                    for s in range(2):
                        bank_ready(pe, ph, 2 * b + s, i)
                        product(ps[:, ring(ph, 2 * b + s), :], b, 8 * s, DC, AH, AL).then_inc(seg_done, 1)
            pairs(pe, ph, body)

        up_base, up_step, up_gelu, up_prod, hid_hi, hid_lo = (sem(n) for n in (
            "up_base", "up_step", "up_gelu", "up_prod", "hid_hi", "hid_lo"))

        def up_act(act):
            def body(i, last):
                for b in range(2):
                    for s, buf in enumerate((CG, CV)):
                        seg_ready(act, "up", 2 * b + s, i)
                        nc.scalar.activation(buf[:, b, :], ps[:, ring("up", 2 * b + s), :], ACT.Identity,
                                             bias=col("cffnb", (2 * b + s) + i * 4),
                                             scale=col("cffn", (6 * b + 3 * s + 2) + i * 12)).then_inc(up_base, 1)
                    stage_hi(act, "up", i, b, last)
                    bank_read(act, "up", 2 * b, i)
                    nc.scalar.activation(CG[:, b, :], CG[:, b, :], ACT.Gelu_apprx_tanh).then_inc(up_gelu, 1)
                    act.wait_ge(up_prod, b + 1 + i * 2)
                    nc.scalar.activation(at(HH, i * 2 + b), CG[:, b:b + 1, :], ACT.Copy).then_inc(hid_hi, 1)
            pairs(act, "up", body)

        def up_dve(dve):
            def body(i, last):
                for b in range(2):
                    for s, buf in enumerate((CG, CV)):
                        dve.wait_ge(up_base, 2 * b + s + 1 + i * 4)
                        for j in (1, 2):
                            if j == 2:
                                dve.wait_ge(up_step, 2 * b + s + 1 + i * 4)
                            nc.vector.scalar_tensor_tensor(
                                buf[:, b, j:S], ps[:, ring("up", 2 * b + s), 0:S - j],
                                col("cffn", (6 * b + 3 * s + 2 - j) + i * 12), buf[:, b, j:S], ALU.mult,
                                ALU.add).then_inc(up_step if j == 1 else bank_free, 1)
                    stage_lo(dve, "up", i, b, last)
                    bank_read(dve, "up", 2 * b + 1, i)
                    dve.wait_ge(up_gelu, b + 1 + i * 2)
                    nc.vector.tensor_tensor(CG[:, b, :], CG[:, b, :], CV[:, b, :], ALU.mult).then_inc(up_prod, 1)
                    dve.wait_ge(hid_hi, b + 1 + i * 2)
                    nc.vector.tensor_tensor(at(HL, i * 2 + b), CG[:, b:b + 1, :], at(HH, i * 2 + b).bitcast(F32),
                                            ALU.subtract).then_inc(hid_lo, 1)
            pairs(dve, "up", body)

        def up2_act(act):
            def body(i, last):
                for b in range(2):
                    seg_ready(act, "up2", 2 * b, i)
                    nc.scalar.activation(CG[:, b, :], ps[:, ring("up2", 2 * b), :], ACT.Silu).then_inc(up_gelu, 1)
                    stage_hi(act, "up2", i, b, last)
                    bank_read(act, "up2", 2 * b + 1, i)
                    nc.scalar.activation(at(HH, i * 2 + b), CG[:, b:b + 1, :], ACT.Copy).then_inc(hid_hi, 1)
            pairs(act, "up2", body)

        def up2_dve(dve):
            def body(i, last):
                for b in range(2):
                    dve.wait_ge(up_gelu, FC + b + 1 + i * 2)
                    seg_ready(dve, "up2", 2 * b + 1, i)
                    nc.vector.tensor_tensor(CG[:, b, :], CG[:, b, :], ps[:, ring("up2", 2 * b + 1), :],
                                            ALU.mult).then_inc(bank_free, 2)
                    stage_lo(dve, "up2", i, b, last)
                    dve.wait_ge(hid_hi, FC + b + 1 + i * 2)
                    nc.vector.tensor_tensor(at(HL, i * 2 + b), CG[:, b:b + 1, :], at(HH, i * 2 + b).bitcast(F32),
                                            ALU.subtract).then_inc(hid_lo, 1)
            pairs(dve, "up2", body)

        def down_chunks(eng, chunk):
            chunk(0, 0, False)
            with eng.Fori(0, 3) as i:
                chunk(i * 2 + 1, 1, False)
                chunk(i * 2 + 2, 0, False)
            chunk(7, 1, True)

        def down_seg(eng, ph, m):
            eng.wait_ge(seg_done, m * 2 + (SEG0[ph] + 2))

        def down_act(act):
            def chunk(m, par, last):
                stage_hi(act, "down", m, 0, last)
                down_seg(act, "down", m)
                square_in(act, 3, m, par, ps[:, 0:1, :] if last else at(ps, m))
                stage_hi(act, "down", m, 1, last)
            down_chunks(act, chunk)

        def down_dve(dve):
            def chunk(m, par, last):
                stage_lo(dve, "down", m, 0, last)
                if isinstance(m, int) and m == 0:
                    dve.wait_ge(sq_ready, 8 * 3 + 1)
                    nc.vector.tensor_copy(YX[:, :], ps[:, 0, :]).then_inc(y0_saved, 1)
                stage_lo(dve, "down", m, 1, last)
                if not isinstance(m, int) or m:
                    gather(dve, 3, m, par)
            down_chunks(dve, chunk)

        ph_ready, pl_ready, e_gate, e_half, e_ready = (sem(n) for n in (
            "ph_ready", "pl_ready", "e_gate", "e_half", "e_ready"))

        def ple_pe(pe):
            pe.wait_ge(pl_ready, 1)
            for m in range(DC):
                b, i = m % 2, m // 2
                weights_ready(pe, "ple", i, b)
                bank_ready(pe, "ple", 2 * b, i)
                if m == 0:
                    pe.wait_ge(h_ready, 8 + max(ring("ple", 0), ring("ple", 1)) + 1)
                product(ps[:, ring("ple", 2 * b), :], b, 0, 2, PH, PL).then_inc(seg_done, 1)
                bank_ready(pe, "ple", 2 * b + 1, i)
                product(ps[:, ring("ple", 2 * b + 1), :], b, 2, DC, AH, AL,
                        ready=(lambda k: pe.wait_ge(in_lo, 8 * 2 + k + 1)) if m == 0 else None).then_inc(seg_done, 1)
            add_gathered(pe, 4)

        def ple_act(act):
            act.wait_ge(p_landed, 16)
            nc.scalar.activation(PH[:, :, :], PX[:, :, :], ACT.Copy).then_inc(ph_ready, 1)
            for m in range(DC):
                act.wait_ge(h_ready, 8 + m + 1)
                nc.scalar.activation(AH[:, m, :], hT[:, m, :], ACT.Copy).then_inc(in_hi, 1)
            for m in range(DC):
                b, i = m % 2, m // 2
                seg_ready(act, "ple", 2 * b + 1, i)
                if m >= 2:
                    bank_read(act, "ple", 2 * b + 1, i - 1)
                nc.scalar.activation(GP[:, b, :], ps[:, ring("ple", 2 * b + 1), :], ACT.Tanh, scale=0.5).then_inc(e_gate, 1)
                stage_hi(act, "ple", i, b, m >= 6)
                act.wait_ge(bank_free, 4 + RING0["ple"] + 2 * m + 2)
                square_in(act, 4, m, b, E[:, m:m + 1, :])

        def ple_input(dve):
            for m in range(DC + 1):
                if m < DC:
                    post_chunk(dve, 1, m, "ffn_post", YX[:, :] if m == 0 else y_bank(m))
                if m == 1:
                    dve.wait_ge(ph_ready, 1)
                    nc.vector.tensor_tensor(PL[:, :, :], PX[:, :, :], PH[:, :, :].bitcast(F32), ALU.subtract).then_inc(pl_ready, 1)
                if m >= 1:
                    dve.wait_ge(in_hi, 8 * 2 + m)
                    nc.vector.tensor_tensor(AL[:, m - 1, :], hT[:, m - 1, :], AH[:, m - 1, :].bitcast(F32),
                                            ALU.subtract).then_inc(in_lo, 1)

        def ple_dve(dve):
            for m in range(DC):
                b, i = m % 2, m // 2
                dve.wait_ge(e_gate, m + 1)
                nc.vector.tensor_scalar(GP[:, b, :], GP[:, b, :], 0.5, 0.5, ALU.mult, ALU.add).then_inc(e_half, 1)
                dve.wait_ge(e_half, m + 1)
                nc.vector.tensor_tensor(E[:, m, :], GP[:, b, :], ps[:, ring("ple", 2 * b), :], ALU.mult).then_inc(bank_free, 2)
                stage_lo(dve, "ple", i, b, m >= 6)
                if m:
                    gather(dve, 4, m, b)

        glu_gate, u_done, bt_ready, b_added, s2_ps, s2_max, p2_ready = (sem(n) for n in (
            "glu_gate", "u_done", "bt_ready", "b_added", "s2_ps", "s2_max", "p2_ready"))
        pt2_ps, pt2_sb, o3_ps, o3_done, y2_ps, y2_hi, y2_lo = (sem(n) for n in (
            "pt2_ps", "pt2_sb", "o3_ps", "o3_done", "y2_ps", "y2_hi", "y2_lo"))
        taps_begun, tap_done, conv_biased, mu_ps, centred, csq_ready, var_ps, var_ready, var_root, normed, cu_ready, cu_hi, cu_lo = (
            sem(n) for n in ("taps_begun", "tap_done", "conv_biased", "mu_ps", "centred", "csq_ready", "var_ps", "var_ready",
                             "var_root", "normed", "cu_ready", "cu_hi", "cu_lo"))
        UNITS2 = [(qt, h) for qt in reversed(range(T)) for h in range(NH)]
        TAPS = [(j, c) for j in range(CT) for c in range(CC)]

        def blk2_pe(pe):
            feature_major(pe, "glu", AH, AL, new=3)
            feature_major(pe, "qk2", AH, AL)
            for b in range(2):
                weights_ready(pe, "v2", 0, b)
                for t in range(T):
                    tok = slice(t * P, (t + 1) * P)
                    if b == 0:
                        bank_ready(pe, "v2", t)
                    for k in range(4):
                        w = slice(k * 512, (k + 1) * 512)
                        o, kk = ps[:, ring("v2", t), :], 4 * b + k
                        nc.tensor.matmul(o, AH[:, kk, tok], WH[b][:, w], start=kk == 0, stop=False)
                        nc.tensor.matmul(o, AL[:, kk, tok], WH[b][:, w], start=False, stop=False)
                        last = nc.tensor.matmul(o, AH[:, kk, tok], WL[b][:, w], start=False, stop=kk == DC - 1)
                    if t % 2:
                        last.then_inc(seg_done, 1)

            def scores(u):
                qt, h = UNITS2[u]
                n, r = (qt + 1) * P, slice((h % 2) * DK, (h % 2 + 1) * DK)
                pe.wait_ge(p2_ready, u - 3) if u >= 4 else pe.wait_ge(bank_free, 4 + RING0["up2"])
                nc.tensor.matmul(ps[:, u % 4, 0:n], QT2[r, h // 2, qt * P:n], KT2[r, h // 2, 0:n], start=True,
                                 stop=True).then_inc(s2_ps, 1)

            def turn(u):
                qt, h = UNITS2[u]
                pe.wait_ge(p2_ready, u + 1)
                if u >= 2:
                    pe.wait_ge(pt2_sb, u - 1)
                for kt in range(qt + 1):
                    last = turned(ps[:, 4 + u % 2, kt * P:(kt + 1) * P], PR2[:, u % 4, kt * P:(kt + 1) * P], ident[:, :])
                last.then_inc(pt2_ps, 1)

            def values(u):
                qt, h = UNITS2[u]
                pe.wait_ge(pt2_sb, u + 1)
                if u >= 4 and h % 2 == 0:
                    pe.wait_ge(o3_done, u // 2 - 1)
                for kt in range(qt + 1):
                    last = nc.tensor.matmul(ps[:, 6 + u // 2 % 2, (h % 2) * DK:(h % 2 + 1) * DK], PT2[:, u % 4, kt * P:(kt + 1) * P],
                                            V2[:, kt, h * DK:(h + 1) * DK], start=kt == 0, stop=kt == qt)
                last.then_inc(o3_ps, 1)

            n = len(UNITS2)
            scores(0)
            scores(1)
            for u in range(n + 1):
                if u + 2 < n:
                    scores(u + 2)
                if u < n:
                    turn(u)
                if u:
                    values(u - 1)
            pe.wait_ge(o3_done, n // 2)
            for qt in range(T):
                for c in range(4):
                    last = turned(ps[:, qt, c * P:(c + 1) * P], Y2[:, qt, c * P:(c + 1) * P], ident[:, :])
                last.then_inc(y2_ps, 1)
            pe.wait_ge(conv_biased, CC)
            for c in range(CC):
                last = nc.tensor.matmul(ps[:, 4, :], ones[:, :], CU[:, c, :], start=c == 0, stop=c == CC - 1)
            last.then_inc(mu_ps, 1)
            pe.wait_ge(csq_ready, 1)
            for c in range(CC):
                last = nc.tensor.matmul(ps[:, 5, :], ones[:, :], PT2[:, c, :],
                                        start=c == 0, stop=c == CC - 1)
            last.then_inc(var_ps, 1)
            pe.wait_ge(y2_lo, T)
            pe.wait_ge(cu_lo, CC)
            for m in range(DC):
                if m % 2 == 0:
                    weights_ready(pe, "wo2", m // 4, m // 2 % 2)
                if m == 7:
                    pe.wait_ge(h_ready, 25)
                product(y_bank(m), m // 2 % 2, 8 * (m % 2), DC, AH, AL).then_inc(seg_done, 1)
            add_gathered(pe, 6)

        def blk2_act(act):
            for c in range(CC):
                i, b = c // 2, c % 2
                seg_ready(act, "glu", 2 * b + 1, i)
                if c >= 2:
                    act.wait_ge(bank_free, 4 + RING0["glu"] + 2 * c - 2)
                nc.scalar.activation(SQ[:, b, :], ps[:, ring("glu", 2 * b + 1), :], ACT.Tanh, scale=0.5).then_inc(glu_gate, 1)
                stage_hi(act, "glu", i, b, i == 1)
            def body(i, last):
                for b in range(2):
                    stage_hi(act, "qk2", i, b, last)
            pairs(act, "qk2", body)
            for b in range(2):
                stage_hi(act, "v2", 0, b, True)
            def save(u):
                n = (UNITS2[u][0] + 1) * P
                act.wait_ge(pt2_ps, u + 1)
                if u >= 4:
                    act.wait_ge(o3_ps, u - 3)
                nc.scalar.copy(PT2[:, u % 4, 0:n], ps[:, 4 + u % 2, 0:n]).then_inc(pt2_sb, 1)

            for u, (qt, h) in enumerate(UNITS2):
                n, pair = (qt + 1) * P, u // 2
                act.wait_ge(s2_max, u + 1)
                if u >= 4:
                    act.wait_ge(pt2_ps, u - 3)
                if pair >= 4 and h % 2 == 0:
                    act.wait_ge(o3_done, pair - 3)
                nc.scalar.activation(PR2[:, u % 4, 0:n], ps[:, u % 4, 0:n], ACT.Exp, bias=NM2[:, u % 4, :],
                                     accum_out=LS2[:, pair % 4, h % 2:h % 2 + 1]).then_inc(p2_ready, 1)
                if u:
                    save(u - 1)
            save(len(UNITS2) - 1)
            for qt in range(T):
                act.wait_ge(y2_ps, qt + 1)
                nc.scalar.activation(AH[:, 0:4, qt * P:(qt + 1) * P], ps[:, qt, :].rearrange("p (c n) -> p c n", c=4),
                                     ACT.Copy).then_inc(y2_hi, 1)
            act.wait_ge(tap_done, len(TAPS))
            for c in range(CC):
                nc.scalar.activation(CU[:, c, :], CU[:, c, :], ACT.Identity, bias=col("cb2", c), scale=0.5).then_inc(conv_biased, 1)
            act.wait_ge(centred, 1)
            nc.scalar.activation(PT2[:, :, :], CU[:, :, :], ACT.Square).then_inc(csq_ready, 1)
            act.wait_ge(var_ready, 1)
            nc.scalar.activation(RR[:, :], RR[:, :], ACT.Sqrt).then_inc(var_root, 1)
            for c in range(CC):
                act.wait_ge(normed, c + 1)
                nc.scalar.activation(CU[:, c, :], CU[:, c, :], ACT.Silu, bias=col("lnb", c), scale=col("lng", c)).then_inc(cu_ready, 1)
                act.wait_ge(cu_ready, c + 1)
                nc.scalar.activation(AH[:, 4 + c, :], CU[:, c, :], ACT.Copy).then_inc(cu_hi, 1)
            for m in range(DC):
                act.wait_ge(h_ready, 25 + m)
                square_in(act, 6, m, m % 2, hT[:, m:m + 1, :])
                if m % 2:
                    stage_hi(act, "wo2", m // 4, m // 2 % 2, m >= 4)

        def blk2_dve(dve, own):
            vec = nc.vector
            vec.memset(UG[:, :, 0:CT - 1], 0.0).then_inc(taps_begun, 1)
            for c in range(CC):
                i, b = c // 2, c % 2
                dve.wait_ge(glu_gate, c + 1)
                vec.scalar_tensor_tensor(UG[:, c, CT - 1:], SQ[:, b, :], 1.0, ps[:, ring("glu", 2 * b), :], ALU.add,
                                         ALU.mult).then_inc(bank_free, 2)
                stage_lo(dve, "glu", i, b, i == 1)
            dve.wait_ge(taps_begun, 1)
            bank_read(dve, "glu", 7)
            left = list(enumerate(TAPS))

            def taps(n):
                for k, (j, c) in left[:n]:
                    src, w = UG[:, c, j:j + S], col("cw2", c * CT + j)
                    if j == 0:
                        ins = vec.tensor_scalar(CU[:, c, :], src, w, None, ALU.mult)
                    else:
                        dve.wait_ge(tap_done, k - CC + 1)
                        ins = vec.scalar_tensor_tensor(CU[:, c, :], src, w, CU[:, c, :], ALU.mult, ALU.add)
                    ins.then_inc(tap_done, 1)
                del left[:n]

            for p in range(NPIECE["qk2"]):
                i, b = p // 2, p % 2
                for s in range(2):
                    c = 2 * b + s
                    seg_ready(dve, "qk2", c, i)
                    if i == 0:
                        ins = vec.tensor_scalar(QT2[:, c, :], ps[:, ring("qk2", c), :], DK ** -0.5, None, ALU.mult)
                    else:
                        ins = vec.tensor_copy(KT2[:, c, :], ps[:, ring("qk2", c), :])
                    ins.then_inc(bank_free, 1)
                    taps(3)
                stage_lo(dve, "qk2", i, b, i == 1)
                taps(4)
            dve.wait_ge(blk2_landed, 32)
            own.link(vec.tensor_tensor(BT[:, :, :], BT[:, :, :], col("far", 0, 8).unsqueeze(2).to_broadcast([P, NH, 256]), ALU.subtract))
            own.link(vec.tensor_tensor(BT[:, :, P:], BT[:, :, P:], MB2[:, :].unsqueeze(1).to_broadcast([P, NH, P]), ALU.add))
            taps(12)
            dve.wait_ge(seg_done, SEG0["wo2"])
            for t in range(T):
                vec.tensor_copy(V2[:, t, :], ps[:, ring("v2", t), :]).then_inc(bank_free, 1)
                if t % 2:
                    stage_lo(dve, "v2", 0, t // 2, True)
            bank_read(dve, "v2", 3)

            def top(u):
                qt, h = UNITS2[u]
                n, w = (qt + 1) * P, min((qt + 1) * P, 256)
                dve.wait_ge(s2_ps, u + 1)
                vec.tensor_tensor(ps[:, u % 4, n - w:n], ps[:, u % 4, n - w:n], BT[:, h, 256 - w:256], ALU.add).then_inc(b_added, 1)
                dve.wait_ge(b_added, u + 1)
                vec.tensor_reduce(NM2[:, u % 4, :], ps[:, u % 4, 0:n], AX, ALU.max, negate=True).then_inc(s2_max, 1)

            def add(pair):
                qt, h = UNITS2[2 * pair]
                b = pair % 2
                dve.wait_ge(o3_ps, 2 * pair + 2)
                own.link(vec.reciprocal(RL2[:, b, :], LS2[:, pair % 4, :]))
                y = Y2[:, qt, h * DK:(h + 2) * DK].rearrange("p (x d) -> p x d", x=2)
                vec.tensor_tensor(y, ps[:, 6 + b, 0:2 * DK].rearrange("p (x d) -> p x d", x=2),
                                  RL2[:, b, :].unsqueeze(2).to_broadcast([P, 2, DK]), ALU.mult).then_inc(o3_done, 1)

            n = len(UNITS2)
            top(0)
            top(1)
            for u in range(n + 1):
                if u + 2 < n:
                    top(u + 2)
                if u and u % 2 == 0:
                    add(u // 2 - 1)
                taps(2)
            taps(len(TAPS))
            for qt in range(T):
                tok = slice(qt * P, (qt + 1) * P)
                dve.wait_ge(y2_hi, qt + 1)
                vec.tensor_tensor(AL[:, 0:4, tok], ps[:, qt, :].rearrange("p (c n) -> p c n", c=4),
                                  AH[:, 0:4, tok].bitcast(F32), ALU.subtract).then_inc(y2_lo, 1)
            dve.wait_ge(mu_ps, 1)
            own.link(vec.tensor_scalar(RR[:, :], ps[:, 4, :], 1.0 / 512, None, ALU.mult))
            vec.tensor_tensor(CU[:, :, :], CU[:, :, :], RR[:, :].unsqueeze(1).to_broadcast([P, CC, S]), ALU.subtract).then_inc(centred, 1)
            dve.wait_ge(var_ps, 1)
            vec.tensor_scalar(RR[:, :], ps[:, 5, :], 1.0 / 512, LN_EPS, ALU.mult, ALU.add).then_inc(var_ready, 1)
            dve.wait_ge(var_root, 1)
            own.link(vec.reciprocal(RR[:, :], RR[:, :]))
            for c in range(CC):
                vec.tensor_tensor(CU[:, c, :], CU[:, c, :], RR[:, :], ALU.mult).then_inc(normed, 1)
            for c in range(CC):
                dve.wait_ge(cu_hi, c + 1)
                vec.tensor_tensor(AL[:, 4 + c, :], CU[:, c, :], AH[:, 4 + c, :].bitcast(F32), ALU.subtract).then_inc(cu_lo, 1)
            for m in range(DC):
                seg_ready(dve, "wo2", m)
                vec.tensor_tensor(hT[:, m, :], hT[:, m, :], y_bank(m), ALU.add).then_inc(h_ready, 1)
                if m >= 2:
                    gather(dve, 6, m - 1, (m - 1) % 2)
                if m % 2:
                    stage_lo(dve, "wo2", m // 4, m // 2 % 2, m >= 4)
            gather(dve, 6, DC - 1, 1)

        def down2_act(act):
            def chunk(m, par, last):
                stage_hi(act, "down2", m, 0, last)
                act.wait_ge(h_ready, m + 33)
                square_in(act, 7, m, par, at(hT, m))
                stage_hi(act, "down2", m, 1, last)
            down_chunks(act, chunk)

        def down2_dve(dve):
            def chunk(m, par, last):
                stage_lo(dve, "down2", m, 0, last)
                down_seg(dve, "down2", m)
                nc.vector.tensor_tensor(at(hT, m), at(hT, m), ps[:, 0:1, :] if last else at(ps, m), ALU.add).then_inc(h_ready, 1)
                stage_lo(dve, "down2", m, 1, last)
                if not isinstance(m, int) or m:
                    gather(dve, 7, m, par)
            down_chunks(dve, chunk)

        def out_dve(dve):
            for m in range(DC):
                if m >= 2:
                    dve.wait_ge(out_stored[m % 2], 16 * (m // 2))
                nc.vector.scalar_tensor_tensor(TMP[:, m % 2, :], hT[:, m, :], col("final", m), RR[:, :], ALU.mult,
                                               ALU.mult).then_inc(out_ready, 1)

        def first_hi(act, b):
            act.wait_ge(raw_landed[b], 16)
            nc.scalar.activation(WH[b][:, :], RAW[b][:, :], ACT.Copy).then_inc(w_hi_done, 1)

        def first_lo(dve, b):
            dve.wait_ge(w_hi_done, b + 1)
            nc.vector.tensor_tensor(WL[b][:, :], RAW[b][:, :], WH[b][:, :].bitcast(F32), ALU.subtract).then_inc(w_lo_done, 1)

        block = ctx.enter_context(nc.Block())

        @block.sync
        def _(sp):
            xv = xT.rearrange("(c p) s -> p c s", p=P)
            for q in range(4):
                sp.dma_start(hT[:, 2 * q:2 * q + 2, :], xv[:, 2 * q:2 * q + 2, :]).then_inc(x_landed[q], 16)

            def load(name, b, piece):
                n = NB[name] * P
                sp.dma_start(RAW[b][:, 0:n], wstream[piece, :, 0:n] if isinstance(piece, int) else
                             wstream[bass.ds(piece, 1), :, 0:n].rearrange("a p n -> p (a n)")).then_inc(raw_landed[b], 16)

            for name, n, nb, _ in PHASES:
                first = 0
                if PIECE0[name] == 0:
                    load(name, 0, 0)
                    load(name, 1, 1)
                    first = 1
                if n == 1:
                    sp.wait_ge(w_lo_done, PIECE0[name] - 1)
                    load(name, PIECE0[name] % 2, PIECE0[name])
                elif n // 2 - first > 1:
                    with sp.Fori(first, n // 2) as i:
                        for b in range(2):
                            sp.wait_ge(w_lo_done, PIECE0[name] + b - 1 + i * 2)
                            load(name, b, i * 2 + (PIECE0[name] + b))
                else:
                    for i in range(first, n // 2):
                        for b in range(2):
                            sp.wait_ge(w_lo_done, PIECE0[name] + b - 1 + i * 2)
                            load(name, b, i * 2 + (PIECE0[name] + b))
            ov = out.rearrange("(c p) s -> p c s", p=P)
            for m in range(DC):
                sp.wait_ge(out_ready, m + 1)
                sp.dma_start(ov[:, m, :], TMP[:, m % 2, :]).then_inc(out_stored[m % 2], 16)
            for b in range(2):
                sp.wait_ge(out_stored[b], 16 * DC // 2)

        @block.gpsimd
        def _(pool):
            pool.memset(ones[:, :], 1.0).then_inc(set_up, 1)
            gdn_pool(pool)
            pool.wait_ge(yt_lo, T)
            nc.gpsimd.tensor_copy(MB[:, 0, :], ident[:, :]).then_inc(mb_ready, 1)
            nc.gpsimd.tensor_copy(MB[:, 1, :], NG_T[:, :]).then_inc(mb_ready, 1)
            pool.dma_start(QT[64:66, :, :], alibi_d).then_inc(nsa_landed, 16)
            pool.dma_start(KT[64:66, :, :, :], krow_d).then_inc(nsa_landed, 16)
            pool.dma_start(KC[64:66, :, :], crow_d).then_inc(nsa_landed, 16)
            pool.dma_start(W2[:, :, :], w2_d).then_inc(nsa_landed, 16)
            pool.dma_start(CN[:, :, :], cneg_d).then_inc(nsa_landed, 16)
            pool.dma_start(C01[:, :, :], c01_d).then_inc(nsa_landed, 16)
            pool.dma_start(W1[0][:, :, :], w1k_d).then_inc(w1_landed, 16)
            pool.dma_start(W1[1][:, :, :], w1v_d).then_inc(w1_landed, 16)
            pool.wait_ge(seg_done, SEG0["ple"])
            pool.dma_start(PX[:, :, :], pT.rearrange("(c p) s -> p c s", p=P)).then_inc(p_landed, 16)
            pool.wait_ge(h_ready, 24)
            pool.dma_start(BT[:, :, :], bias2_d).then_inc(blk2_landed, 16)
            pool.dma_start(MB2[:, :], causal_d).then_inc(blk2_landed, 16)

        @block.scalar
        def _(act):
            act.dma_start(cols[:, :], cols_d).then_inc(cols_landed, 16)
            act.dma_start(ident[:, :], ident_d).then_inc(ident_landed, 16)
            for dst, src in ((NG_T[:, :], causal_d), (CS[:, :], consts_d), (WSR[:, :], wsm_d)):
                act.dma_start(dst, src).then_inc(con_landed, 16)
            for m in range(DC):
                if m % 2 == 0:
                    act.wait_ge(x_landed[m // 2], 16)
                square(act, 0, m, hT[:, m, :])
            rms_root(act, 0)
            first_hi(act, 0)
            pre_hi(act, 0)
            first_hi(act, 1)
            split_small_act(act)
            qkv_act(act)
            gdn_act(act)
            nsa_proj_act(act)
            nsa_act(act)
            mix_act(act)
            wo_act(act)
            rms_root(act, 1)
            for m in range(DC):
                act.wait_ge(h_ready, m + 1)
                square(act, 2, m, hT[:, m, :])
            rms_root(act, 2)
            pre_hi(act, 1)
            up_act(act)
            down_act(act)
            rms_root(act, 3)
            ple_act(act)
            rms_root(act, 4)
            for m in range(DC):
                act.wait_ge(h_ready, 16 + m + 1)
                square(act, 5, m, hT[:, m, :])
            rms_root(act, 5)
            pre_hi(act, 3)
            blk2_act(act)
            rms_root(act, 6)
            pre_hi(act, 4)
            up2_act(act)
            down2_act(act)
            rms_root(act, 7)

        @block.vector
        def _(dve):
            own = Own(dve, dve_own)
            dve.memset(YX[:, 0:1], 0.0).then_inc(bank_free, 4)
            dve.wait_ge(cols_landed, 16)
            rms_rest(dve, 0)
            first_lo(dve, 0)
            pre_rest(dve, 0, "mix_pre")
            first_lo(dve, 1)
            split_small_dve(dve)
            qkv_dve(dve)
            gdn_dve(dve, own)
            nsa_proj_dve(dve)
            nsa_dve(dve, own)
            mix_dve(dve)
            wo_dve(dve)
            rms_rest(dve, 1)
            post_add(dve, 0, "mix_post", YX, y_bank)
            rms_rest(dve, 2)
            pre_rest(dve, 1, "ffn_pre")
            up_dve(dve)
            down_dve(dve)
            rms_rest(dve, 3)
            ple_input(dve)
            ple_dve(dve)
            rms_rest(dve, 4)
            post_add(dve, 2, "ple_post", None, lambda m: E[:, m, :])
            rms_rest(dve, 5)
            pre_rest(dve, 3, "mix2")
            blk2_dve(dve, own)
            rms_rest(dve, 6)
            pre_rest(dve, 4, "ffn2")
            up2_dve(dve)
            down2_dve(dve)
            rms_rest(dve, 7)
            out_dve(dve)

        @block.tensor
        def _(pe):
            pe.wait_ge(set_up, 1)
            for m in range(DC):
                add_squares(pe, 0, m)
            pe.wait_ge(ident_landed, 16)
            spread_rms(pe, 0)
            feature_major(pe, "qkv", AH, AL, new=0)
            gdn_pe(pe)
            nsa_proj_pe(pe)
            nsa_pe(pe)
            mix_pe(pe)
            pe.wait_ge(mix_lo, DC)
            pe.wait_ge(bank_free, 4 + RING0["up"])
            wide_product(pe, "wo", 1, GHI, GLO, y0_saved, 1)
            spread_rms(pe, 1)
            for m in range(DC):
                add_squares(pe, 2, m)
            spread_rms(pe, 2)
            feature_major(pe, "up", AH, AL, new=1)
            pe.wait_ge(hid_lo, FC)
            down_pe(pe, "down", 3, y0_saved, 2)
            spread_rms(pe, 3)
            ple_pe(pe)
            spread_rms(pe, 4)
            for m in range(DC):
                add_squares(pe, 5, m)
            spread_rms(pe, 5)
            blk2_pe(pe)
            spread_rms(pe, 6)
            feature_major(pe, "up2", AH, AL, new=4)
            pe.wait_ge(hid_lo, 2 * FC)
            down_pe(pe, "down2", 7, h_ready, 33)
            spread_rms(pe, 7)


def shape_tables():
    i = np.arange(P)
    same = lambda w: i[:, None] // w == i[None, :] // w
    parts = [(i[:, None] <= i[None, :]) & same(C), (i[:, None] > i[None, :]) & same(C),
             np.broadcast_to(i[:, None] < C, (P, P)), np.broadcast_to(i[:, None] >= C, (P, P))]
    parts.append(np.where(parts[0], 0.0, NEG))
    for w in (1, 2, 4, 8, 16, 32):
        parts.append(same(2 * w) & (i[:, None] // w % 2 == 0) & (i[None, :] // w % 2 == 1))
    consts = np.concatenate([x.astype(np.float32) for x in parts], axis=1)
    ident = np.eye(P, dtype=np.float32)
    causal = np.where(i[None, :] > i[:, None], np.float32(NEG), np.float32(0))
    t = (np.arange(T)[:, None, None] * P + i[None, :, None])
    ends = np.arange(32)[None, None, :] * CMP_STRIDE + CMP_LEN - 1
    seen = ((t >= ends) & (np.arange(32) < NC)).transpose(1, 0, 2)
    cneg = np.where(seen, np.float32(0), np.float32(NEG))
    c01 = seen.astype(np.float32)
    slope = 2.0 ** (-8.0 * np.arange(1, NH + 1) / NH)
    alibi = np.stack([np.repeat(slope[:, None], S, 1), -slope[:, None] * np.arange(S)]).astype(np.float32)
    krow = np.stack([np.broadcast_to(np.arange(S), (2, NG, S)), np.ones((2, NG, S))]).astype(np.float32)
    crow = np.stack([np.broadcast_to(ends[0, 0], (NG, 32)), np.ones((NG, 32))]).astype(np.float32)
    return consts, ident, causal, cneg, c01, alibi, krow, crow


def t5_bucket(dist):
    d = np.maximum(dist, 1).astype(np.float32)
    large = 16 + (np.log(d / np.float32(16)) / np.float32(np.log(128 / 16)) * np.float32(16)).astype(np.int32)
    return np.where(dist < 16, dist, np.minimum(large, 31))


def blocks(w, k0, k1, c0, c1):
    return w[k0:k1, c0:c1].reshape((k1 - k0) // P, P, c1 - c0).transpose(1, 0, 2)


def weight_stream(a):
    w = a["w_in"][0]
    ks, fm = [], lambda w_, cols_: [np.concatenate([blocks(w_, 0, w_.shape[0], c, c + P).reshape(P, -1) for c in cs], 1) for cs in cols_]
    two = lambda c0, n: [[c0 + 2 * P * j, c0 + 2 * P * j + P] for j in range(n)]
    ks += fm(w, two(0, 6)) + fm(w, two(1536, 2))
    ks += fm(w, two(2056, 2)) + fm(w, [[2568], [2696]]) + fm(w, [[2824, 3080]])
    ks += [np.concatenate([blocks(w, 0, D, 2952, 3080), blocks(w, 0, D, 3208, 3336)], 2).reshape(P, -1)]
    for j in range(DC):
        for g0, y in ((3360, a["w_a2d"][0]), (3360 + D, a["w_b2d"][0])):
            ks.append(np.concatenate([blocks(w, 0, D, g0 + j * P, g0 + j * P + P).reshape(P, -1),
                                      blocks(y, 0, 512, j * P, j * P + P).reshape(P, -1)], 1))
    ks += fm(a["w_o"][0], two(0, 4))
    ks += fm(a["w_up"][0], [[j * P, FF + j * P] for j in range(FC)])

    def down(w_):
        return [blocks(w_, x * 11 * P, (x + 1) * 11 * P, j * P, j * P + P).reshape(P, -1) for j in range(DC) for x in range(2)]
    ks += down(a["w_down"][0])
    ks += [np.concatenate([blocks(a["w_ple"][0], 0, PLE, j * P, j * P + P).reshape(P, -1),
                           blocks(a["w_ple_gate"][0], 0, D, j * P, j * P + P).reshape(P, -1)], 1) for j in range(DC)]
    w2 = a["w_in_2"][0]
    ks += fm(w2, [[1536 + j * P, 2048 + j * P] for j in range(CC)]) + fm(w2, two(0, 4))
    ks += [blocks(w2, x * 512, (x + 1) * 512, 1024, 1536).reshape(P, -1) for x in range(2)]
    ks += fm(a["w_out_2"][0], two(0, 4))
    ks += [np.concatenate([blocks(a["w_gate_2"][0], 0, D, j * P, j * P + P).reshape(P, -1),
                           blocks(a["w_up_2"][0], 0, D, j * P, j * P + P).reshape(P, -1)], 1) for j in range(FC)]
    ks += down(a["w_down_2"][0])
    assert [x.shape[1] // P for x in ks] == PIECE_NB[:PIECES]
    stream = np.zeros((PIECES, P, BLK * P), np.float32)
    for j, x in enumerate(ks):
        stream[j, :, :x.shape[1]] = x
    return stream


def lay_out(a):
    a = {k: np.asarray(v) for k, v in a.items()}
    consts, ident, causal, cneg, c01, alibi, krow, crow = shape_tables()
    cols = np.zeros((P, NCOLS), np.float32)

    def put(name, x):
        cols[:, COLS[name]:COLS[name] + x.shape[1]] = x

    vec = lambda x: x.reshape(-1, P).T
    for name, key in (("mix_pre", "norm_mix_pre"), ("mix_post", "norm_mix_post"), ("ffn_pre", "norm_ffn_pre"),
                      ("ffn_post", "norm_ffn_post"), ("ple_post", "norm_ple_post"), ("mix2", "mix_norm_g_2"),
                      ("ffn2", "ffn_norm_g_2"), ("final", "final_norm_g_2"), ("gdn", "gdn_norm"),
                      ("cb2", "conv_b_2"), ("lng", "conv_ln_g_2"), ("lnb", "conv_ln_b_2")):
        put(name, vec(a[key]))
    put("cqkv", a["conv_qkv"][0].reshape(4, 12, P).transpose(2, 1, 0).reshape(P, -1))
    put("cffn", a["conv_ffn"][0].reshape(3, 2, FC, P).transpose(3, 2, 1, 0).reshape(P, -1))
    put("cffnb", a["conv_ffn_b"][0].reshape(2, FC, P).transpose(2, 1, 0).reshape(P, -1))
    put("cw2", a["conv_w_2"][0].reshape(CT, CC, P).transpose(2, 1, 0).reshape(P, -1))
    put("alog", np.broadcast_to(a["a_log"], (P, GH)))
    put("dtb", np.broadcast_to(a["dt_bias"], (P, GH)))
    put("far", np.broadcast_to(a["rel_bias_2"][31], (P, NH)))
    put("posk", a["cmp_pos_k"][0].reshape(16, P).T)
    put("posv", a["cmp_pos_v"][0].reshape(16, P).T)
    put("eps", np.full((P, 1), EPS, np.float32))
    w = a["w_in"][0]
    wsm = np.concatenate([blocks(w, 0, D, 2048, 2056), blocks(w, 0, D, 3336, 3360)], 2).reshape(P, -1)
    q, kk = np.arange(P)[:, None], np.arange(256)[None, :]
    bias = a["rel_bias_2"][t5_bucket(np.maximum(q + P - kk, 0))].transpose(0, 2, 1)
    w2 = np.concatenate([blocks(a["cmp_w2_k"][0], 0, CMP_HID, 0, DK), blocks(a["cmp_w2_v"][0], 0, CMP_HID, 0, DK)], 1)
    return {
        "wstream": weight_stream(a), "xT": a["x"][0].T, "pT": a["p"][0, 0].T, "cols_d": cols, "ident_d": ident,
        "causal_d": causal, "consts_d": consts, "cneg_d": cneg, "c01_d": c01, "alibi_d": alibi, "krow_d": krow,
        "crow_d": crow, "wsm_d": wsm, "w1k_d": blocks(a["cmp_w1_k"][0], 0, 2048, 0, CMP_HID),
        "w1v_d": blocks(a["cmp_w1_v"][0], 0, 2048, 0, CMP_HID), "w2_d": w2, "bias2_d": bias,
    }


def kernel(**inputs):
    import concourse.bacc as bacc
    from concourse.bass_utils import run_bass_kernel_spmd

    nc = bacc.Bacc("TRN2", target_bir_lowering=False, num_devices=1)
    arrays, args = {}, {}
    for name, x in lay_out(inputs).items():
        arrays[name] = np.ascontiguousarray(x)
        args[name] = nc.dram_tensor(name, x.shape, mybir.dt.from_np(x.dtype), kind="ExternalInput").ap()
    args["out"] = nc.dram_tensor("out", (D, S), F32, kind="ExternalOutput").ap()
    build(nc, **args)
    r = run_bass_kernel_spmd(nc, [arrays], core_ids=[0])
    return np.ascontiguousarray(r.results[0]["out"].T).reshape(1, S, D)
```

```python
from contextlib import ExitStack

import numpy as np

import concourse.bass as bass
from concourse import mybir

F32 = mybir.dt.float32
F32R = mybir.dt.float32r
BF16 = mybir.dt.bfloat16
ALU = mybir.AluOpType
ACT = mybir.ActivationFunctionType
AX = mybir.AxisListType.X

P = 128
D = 1024
S = 512
DC = D // P
T = S // P
EPS = 1e-6
LN_EPS = 1e-5
NEG = -1e30

GH = 4
C = 64
NH, NG, DK = 8, 2, 64
R = NH // NG
CMP_LEN, CMP_STRIDE, CMP_HID = 32, 16, 256
NC = S // CMP_STRIDE - 1
PLE = 256
FF = 2816
FC = FF // P
CT = 31
CC = 512 // P

BLK = 16
PHASES = [
    ("qkv", 6, 16, 2), ("z", 2, 16, 2),
    ("nq", 2, 16, 2), ("ncmp", 2, 8, 1), ("nk", 1, 16, 2), ("nv", 1, 16, 2),
    ("mix", 16, 12, 2), ("wo", 4, 16, 2), ("up", 22, 16, 2), ("down", 16, 11, 1), ("ple", 8, 10, 2),
    ("glu", 4, 16, 2), ("qk2", 4, 16, 2), ("v2", 2, 16, 2), ("wo2", 4, 16, 2),
    ("up2", 22, 16, 2), ("down2", 16, 11, 1),
]
PIECE0, SEG0, NB, NSEG, NPIECE, NEXT = {}, {}, {}, {}, {}, {}
_piece = _seg = 0
for _k, (_name, _n, _nb, _s) in enumerate(PHASES):
    PIECE0[_name], SEG0[_name], NB[_name], NSEG[_name], NPIECE[_name] = _piece, _seg, _nb, _s, _n
    NEXT[_name] = PHASES[_k + 1][0] if _k + 1 < len(PHASES) else None
    _piece += _n
    _seg += _n * _s
PIECES = _piece
PIECE_NB = [nb for _, n, nb, _ in PHASES for _ in range(n)]
PIECE_SEG = (
    np.cumsum([0] + [s for _, n, _, s in PHASES for _ in range(n)]).tolist())
RING = {"qkv": 12, "z": 4, "nq": 4, "ncmp": 2, "nk": 2, "nv": 2, "mix": 32, "up": 44,
        "ple": 16, "glu": 8, "qk2": 8, "v2": 4, "up2": 44}
RING0, _n = {}, 0
for _name, _, _, _ in PHASES:
    if _name in RING:
        RING0[_name] = _n
        _n += RING[_name]

COLS = {}
_n = 0
for _name, _w in (("mix_pre", 8), ("mix_post", 8), ("ffn_pre", 8), ("ffn_post", 8), ("ple_post", 8),
                  ("mix2", 8), ("ffn2", 8), ("final", 8), ("cqkv", 48), ("gdn", 1), ("cffn", 132),
                  ("cffnb", 44), ("cw2", 124), ("cb2", 4), ("lng", 4), ("lnb", 4), ("alog", 4),
                  ("dtb", 4), ("far", 8), ("posk", 16), ("posv", 16), ("eps", 1), ("lneps", 1)):
    COLS[_name] = _n
    _n += _w
NCOLS = _n
CON = {}
_n = 0
for _name, _w in (("tri", 128), ("after", 128), ("half", 2), ("seen", 128), ("level", 6 * 128)):
    CON[_name] = _n
    _n += _w
NCON = _n


def build(nc, wstream, xT, pT, cols_d, ident_d, causal_d, consts_d, cneg_d, c01_d, alibi_d, krow_d, crow_d,
          wsm_d, w1k_d, w1v_d, w2_d, bias2_d, out):
    with ExitStack() as ctx:
        def sb(name, shape, dt=F32, scope=ctx):
            return scope.enter_context(nc.sbuf_tensor(name, shape, dt))

        def sem(name):
            return ctx.enter_context(nc.semaphore(name))

        hT = sb("hT", [P, DC, S])
        AH = sb("AH", [P, DC, S], F32R)
        AL = sb("AL", [P, DC, S], F32R)
        RAW = [sb(f"raw{b}", [P, BLK * P]) for b in range(2)]
        WH = [sb(f"whi{b}", [P, BLK * P], F32R) for b in range(2)]
        WL = [sb(f"wlo{b}", [P, BLK * P], F32R) for b in range(2)]
        cols = sb("cols", [P, NCOLS])
        ones = sb("ones", [P, P])
        ident = sb("ident", [P, P])
        RR = sb("RR", [P, S])
        SQ = sb("SQ", [P, 2, S])
        TMP = sb("TMP", [P, 2, S])
        YX = sb("YX", [P, S])
        SF = YX
        RC = sb("RC", [P, T])

        def col(name, j=0, n=1):
            if isinstance(j, int):
                return cols[:, COLS[name] + j:COLS[name] + j + n]
            return cols[:, bass.ds(j + COLS[name], n)]

        blk1 = ExitStack()
        SG = sb("SG", [P, T, 32], F32, blk1)
        NG_T = sb("NG_T", [P, P], F32, blk1)
        MB = sb("MB", [P, 2, P], BF16, blk1)
        with ExitStack() as x:
            Tm = sb("Tm", [P, T, GH, P], F32, x)
            TT = sb("TT", [P, T, GH, P], F32, x)
        YAH = sb("YAH", [P, 4, S], F32R, blk1)
        YAL = sb("YAL", [P, 4, S], F32R, blk1)
        with ExitStack() as x:
            QKV = sb("QKV", [P, 12, S], F32, x)
            ZS = sb("ZS", [P, 4, S], F32, x)
            Y1 = sb("Y1", [P, T, GH, P], F32, x)
            AT = sb("AT", [P, T, GH, P], F32, x)
            OFF = sb("OFF", [P, T, GH, P], F32, x)
            QK = sb("QK", [P, T, GH, P], F32, x)
            ST = sb("ST", [P, 2, GH, P], F32, x)
            CS = sb("CS", [P, NCON], F32, x)
            WSR = sb("WSR", [P, DC * 32], F32, x)
            WSH = sb("WSH", [P, DC * 32], F32R, x)
            WSL = sb("WSL", [P, DC * 32], F32R, x)
            SM = sb("SM", [P, T, 32], F32, x)
            AA = sb("AA", [P, 4, T, GH], F32, x)
            EA = sb("EA", [P, GH], F32, x)
            G = sb("G", [P, T, GH], F32, x)
            EX = sb("EX", [P, 4, T, GH], F32, x)
            GC = sb("GC", [P, T, GH], F32, x)
            BG = sb("BG", [P, T, GH], F32, x)
            RO = sb("RO", [P, T, GH], F32, x)
            L2 = sb("L2", [P, 2 * GH * T], F32, x)
        with ExitStack() as x:
            W1v = sb("W1v", [P, 16, CMP_HID], F32, x)
        YBH = sb("YBH", [P, 4, S], F32R, blk1)
        YBL = sb("YBL", [P, 4, S], F32R, blk1)
        with ExitStack() as x:
            QT = sb("QT", [P, NH, S], F32, x)
            KT = sb("KT", [P, 2, NG, S], F32, x)
            V1 = sb("V1", [P, T, 2 * P], F32, x)
            KC = sb("KC", [P, NG, 32], F32, x)
            VB = sb("VB", [P, NG, R * DK], F32, x)
            W2 = sb("W2", [P, 4, DK], F32, x)
            SC = sb("SC", [P, T, NH, 32], F32, x)
            CN = sb("CN", [P, T, 32], F32, x)
            C01 = sb("C01", [P, T, 32], F32, x)
            HID = sb("HID", [P, 4, 2 * NC], F32, x)
            SX = sb("SX", [P, 3, T, NH], F32, x)
            NM = sb("NM", [P, 4, 1], F32, x)
            LS = sb("LS", [P, 4, 2], F32, x)
            RL = sb("RL", [P, 2, 2], F32, x)
            with ExitStack() as y:
                W1 = [sb("W1k", [P, 16, CMP_HID], F32, y), W1v]
                Z = [sb(f"z{n}", [P, 16, 2 * NC], F32, y) for n in "kv"]
            PR = sb("PR", [P, 4, S], F32, x)
            PT = sb("PT", [P, 4, S], F32, x)
            Y = sb("Y", [P, T, NH * DK], F32, x)
        with ExitStack() as x:
            GHI = sb("GHI", [P, DC, S], F32R, x)
            GLO = sb("GLO", [P, DC, S], F32R, x)
        blk1.close()
        with ExitStack() as x:
            HH = sb("HH", [P, FC, S], F32R, x)
            HL = sb("HL", [P, FC, S], F32R, x)
            CG = sb("CG", [P, 2, S], F32, x)
            CV = sb("CV", [P, 2, S], F32, x)
        with ExitStack() as x:
            E = sb("E", [P, DC, S], F32, x)
            PX = sb("PX", [P, 2, S], F32, x)
            PH = sb("PH", [P, 2, S], F32R, x)
            PL = sb("PL", [P, 2, S], F32R, x)
            GP = sb("GP", [P, 2, S], F32, x)
        with ExitStack() as x:
            MB2 = sb("MB2", [P, P], F32, x)
            QT2 = sb("QT2", [P, 4, S], F32, x)
            KT2 = sb("KT2", [P, 4, S], F32, x)
            V2 = sb("V2", [P, T, 512], F32, x)
            BT = sb("BT", [P, NH, 256], F32, x)
            PR2 = sb("PR2", [P, 4, S], F32, x)
            PT2 = sb("PT2", [P, 4, S], F32, x)
            Y2 = sb("Y2", [P, T, 512], F32, x)
            UG = sb("UG", [P, CC, S + CT - 1], F32, x)
            CU = sb("CU", [P, CC, S], F32, x)
            NM2 = sb("NM2", [P, 4, 1], F32, x)
            LS2 = sb("LS2", [P, 4, 2], F32, x)
            RL2 = sb("RL2", [P, 2, 2], F32, x)
            B2 = sb("B2", [P, CC], F32, x)
            VC = sb("VC", [P, T], F32, x)
        ps = ctx.enter_context(nc.psum_tensor("ps", [P, 8, 512], F32))

        raw_landed = [sem(f"raw{b}_landed") for b in range(2)]
        w_hi_done, w_lo_done = sem("w_hi_done"), sem("w_lo_done")
        seg_done = sem("seg_done")
        bank_free = sem("bank_free")
        N_CON, N_NSA = 3, 6
        x_landed, cols_landed, con_landed = [sem(f"x{q}_landed") for q in range(4)], sem("cols_landed"), sem("con_landed")
        ident_landed = sem("ident_landed")
        nsa_landed, w1_landed, p_landed, blk2_landed = (sem("nsa_landed"), sem("w1_landed"),
                                                         sem("p_landed"), sem("blk2_landed"))
        set_up, ws_split = sem("set_up"), sem("ws_split")
        rc_ready, rows_ps = sem("rc_ready"), sem("rows_ps")
        sq_ready, sq_used, ms_ready = sem("sq_ready"), sem("sq_used"), sem("ms_ready")
        rt_ready, rr_ready, h_ready, y0_saved = sem("rt_ready"), sem("rr_ready"), sem("h_ready"), sem("y0_saved")
        in_tmp, in_hi, in_lo = sem("in_tmp"), sem("in_hi"), sem("in_lo")
        out_ready, out_stored = sem("out_ready"), [sem(f"out_stored{b}") for b in range(2)]
        post_tmp = sem("post_tmp")
        dve_own = sem("dve_own")

        class Own:

            def __init__(self, eng, sem_):
                self.eng, self.sem, self.n = eng, sem_, 0

            def mark(self, ins):
                ins.then_inc(self.sem, 1)
                self.n += 1

            def wait(self, back=0):
                self.eng.wait_ge(self.sem, self.n - back)

            def link(self, ins):
                self.mark(ins)
                self.wait()

        def staged(ph, last):
            return NB[ph] if not last else (NB[NEXT[ph]] if NEXT[ph] else None)

        def pairs(eng, ph, body, first=0):
            n = NPIECE[ph] // 2
            if n - first > 2:
                with eng.Fori(first, n - 1) as i:
                    body(i, False)
            else:
                for i in range(first, n - 1):
                    body(i, False)
            body(n - 1, True)

        def stage_hi(act, ph, i, b, last):
            if staged(ph, last) is None:
                return
            n = staged(ph, last) * P
            act.wait_ge(raw_landed[b], 16 * (PIECE0[ph] // 2 + 2) + i * 16)
            act.wait_ge(seg_done, SEG0[ph] + NSEG[ph] * (b + 1) + i * (2 * NSEG[ph]))
            nc.scalar.activation(WH[b][:, 0:n], RAW[b][:, 0:n], ACT.Copy).then_inc(w_hi_done, 1)

        def stage_lo(dve, ph, i, b, last):
            if staged(ph, last) is None:
                return
            n = staged(ph, last) * P
            dve.wait_ge(w_hi_done, PIECE0[ph] + b + 3 + i * 2)
            nc.vector.tensor_tensor(WL[b][:, 0:n], RAW[b][:, 0:n], WH[b][:, 0:n].bitcast(F32),
                                    ALU.subtract).then_inc(w_lo_done, 1)

        def weights_ready(pe, ph, i, b):
            pe.wait_ge(w_lo_done, PIECE0[ph] + b + 1 + i * 2)

        def product(out_, b, j0, n, xh, xl, start=True, stop=True, ready=None):
            for k in range(n):
                if ready:
                    ready(k)
                w = slice((j0 + k) * P, (j0 + k + 1) * P)
                nc.tensor.matmul(out_, WH[b][:, w], xh[:, k, :], start=start and k == 0, stop=False)
                nc.tensor.matmul(out_, WH[b][:, w], xl[:, k, :], start=False, stop=False)
                last = nc.tensor.matmul(out_, WL[b][:, w], xh[:, k, :], start=False,
                                        stop=stop and k == n - 1)
            return last

        def turned(out_, x, eye):
            return nc.tensor.transpose(out_, x, eye)

        def square(act, k, m, src):
            if 8 * k + m >= 2:
                act.wait_ge(sq_used, 8 * k + m - 1)
            nc.scalar.activation(SQ[:, m % 2, :], src, ACT.Square).then_inc(sq_ready, 1)

        def add_squares(pe, k, m):
            pe.wait_ge(sq_ready, 8 * k + m + 1)
            column_sums(SQ[:, m % 2, :], m == 0, m == DC - 1).then_inc(sq_used, 1)

        def column_sums(sq, first, last):
            for t in range(T):
                ins = nc.tensor.matmul(ps[:, 7, t:t + 1], sq[:, t * P:(t + 1) * P], ones[:, 0:1],
                                       start=first and t == 0, stop=last and t == T - 1)
            return ins

        def spread_rms(pe, k):
            pe.wait_ge(rc_ready, k + 1)
            for t in range(T):
                last = nc.tensor.matmul(ps[:, 7, t * P:(t + 1) * P], RC[:, t:t + 1].to_broadcast([P, P]), ident[:, :],
                                        start=True, stop=True)
            last.then_inc(rows_ps, 1)

        def square_in(act, k, m, par, src, total=None):
            start = isinstance(m, int) and m == 0
            act.wait_ge(sq_used, 8 * k if start else m + (8 * k - 2))
            dst = (TMP[:, 1:2, :] if total is None else total) if start else SQ[:, par:par + 1, :]
            nc.scalar.activation(dst, src, ACT.Square).then_inc(sq_ready, 1)

        def gather(dve, k, m, par):
            dve.wait_ge(sq_ready, m + (8 * k + 1))
            dve.wait_ge(sq_used, m + (8 * k - 1))
            nc.vector.tensor_tensor(TMP[:, 1, :], TMP[:, 1, :], SQ[:, par, :], ALU.add).then_inc(sq_used, 1)

        ORDER = {j: tuple(range(DC)) if j in (0, 3, 4) else (2, 3, 0, 1, 4, 5, 6, 7) for j in range(5)}
        WO_BANK = (4, 5, 2, 3, 6, 1, 0, 4)
        TOTAL = {2: CG[:, 0, :], 5: PR2[:, 0, :]}

        def pool_gather(pool, k):
            total = TOTAL[k]
            for m in range(1, DC):
                pool.wait_ge(sq_ready, 8 * k + m + 1)
                pool.wait_ge(sq_used, 8 * k + m - 1)
                nc.gpsimd.tensor_tensor(total, total, SQ[:, m % 2, :], ALU.add).then_inc(sq_used, 1)

        def add_gathered(pe, k, total=None):
            pe.wait_ge(sq_used, 8 * k + 7)
            column_sums(TMP[:, 1, :] if total is None else total, True, True).then_inc(sq_used, 1)

        def scaled_hi(act, j, m, name):
            nc.scalar.mul(AH[:, m, :], hT[:, m, :], col(name, m)).then_inc(in_hi, 1)

        def scaled_lo(dve, j, n, name, m):
            dve.wait_ge(in_hi, 8 * j + n + 1)
            nc.vector.scalar_tensor_tensor(AL[:, m, :], hT[:, m, :], col(name, m), AH[:, m, :].bitcast(F32),
                                           ALU.mult, ALU.subtract).then_inc(in_lo, 1)

        def normed_input_act(act, j, k, name, h0):
            for n, m in enumerate(ORDER[j]):
                act.wait_ge(h_ready, h0 + n + 1)
                scaled_hi(act, j, m, name)
                square_in(act, k, n, n % 2, hT[:, m:m + 1, :], total=TOTAL[k].unsqueeze(1))

        def normed_input_dve(dve, j, name, post):
            for n in range(DC + 1):
                if n < DC:
                    post(n, ORDER[j][n])
                if n:
                    scaled_lo(dve, j, n - 1, name, ORDER[j][n - 1])

        def rms_root(act, k):
            act.wait_ge(ms_ready, k + 1)
            nc.scalar.activation(RC[:, :], RC[:, :], ACT.Sqrt).then_inc(rt_ready, 1)

        def rms_rest(dve, k, eps=EPS):
            dve.wait_ge(sq_used, 8 * k + 8)
            nc.vector.tensor_scalar(RC[:, :], ps[:, 7, 0:T], 1.0 / D, eps, ALU.mult, ALU.add).then_inc(ms_ready, 1)
            dve.wait_ge(rt_ready, k + 1)
            nc.vector.reciprocal(RC[:, :], RC[:, :]).then_inc(rc_ready, 1)
            dve.wait_ge(rows_ps, k + 1)
            nc.vector.tensor_copy(RR[:, :], ps[:, 7, :]).then_inc(rr_ready, 1)
            dve.wait_ge(rr_ready, k + 1)

        def pre_hi(act, j):
            for m in range(DC):
                act.wait_ge(in_tmp, 8 * j + m + 1)
                nc.scalar.activation(AH[:, m, :], TMP[:, m % 2, :], ACT.Copy).then_inc(in_hi, 1)

        def pre_rest(dve, j, name):
            for m in range(DC + 1):
                if m < DC:
                    if m >= 2:
                        dve.wait_ge(in_lo, 8 * j + m - 1)
                    nc.vector.scalar_tensor_tensor(TMP[:, m % 2, :], hT[:, m, :], col(name, m),
                                                   RR[:, :], ALU.mult, ALU.mult).then_inc(in_tmp, 1)
                if m >= 1:
                    dve.wait_ge(in_hi, 8 * j + m)
                    nc.vector.tensor_tensor(AL[:, m - 1, :], TMP[:, (m - 1) % 2, :], AH[:, m - 1, :].bitcast(F32),
                                            ALU.subtract).then_inc(in_lo, 1)

        def y_bank(m):
            return ps[:, m % 7, :]

        def post_chunk(dve, j, n, m, name, y):
            nc.vector.scalar_tensor_tensor(TMP[:, n % 2, :], y, col(name, m), RR[:, :], ALU.mult,
                                           ALU.mult).then_inc(post_tmp, 1)
            dve.wait_ge(post_tmp, 8 * j + n + 1)
            nc.vector.tensor_tensor(hT[:, m, :], hT[:, m, :], TMP[:, n % 2, :], ALU.add).then_inc(h_ready, 1)
        sf_saved = sem("sf_saved")
        small_done, sm_saved, l2_sq, l2_sum, l2_root, l2_rec, l2_done = (sem(n) for n in (
            "small_done", "sm_saved", "l2_sq", "l2_sum", "l2_root", "l2_rec", "l2_done"))
        g_ready, gsum_done, gsum_read, rows_done, at_ready = (sem(n) for n in (
            "g_ready", "gsum_done", "gsum_read", "rows_done", "at_ready"))
        tt_ready, t_ready, off_ready, y_ps, y_sb, d_ps, dt_ps = (sem(n) for n in (
            "tt_ready", "t_ready", "off_ready", "y_ps", "y_sb", "d_ps", "dt_ps"))
        kv_ps, kv_sb, wu_ps, wu_sb, state_ready, ws_ps, u_ready = (sem(n) for n in (
            "kv_ps", "kv_sb", "wu_ps", "wu_sb", "state_ready", "ws_ps", "u_ready"))
        ds_ps, o_sb, o_ps, on_ready, ot_ps, yt_ready, yt_hi, yt_lo = (sem(n) for n in (
            "ds_ps", "o_sb", "o_ps", "on_ready", "ot_ps", "yt_ready", "yt_hi", "yt_lo"))
        conv_base, conv_step, silu_done, dec_pre, dec_exp, sig_ready, soft = (sem(n) for n in (
            "conv_base", "conv_step", "silu_done", "dec_pre", "dec_exp", "sig_ready", "soft"))
        l2_rows, qd_ready, row_exp, gc_saved, o_sq, o_root, o_ms = (sem(n) for n in ("l2_rows", "qd_ready", "row_exp", "gc_saved", "o_sq", "o_root", "o_ms"))


        def ring(ph, c):
            return (RING0[ph] + c) % 4

        def bank_ready(pe, ph, c, i=0):
            pe.wait_ge(bank_free, RING0[ph] + c + 1 + i * 4)

        def seg_ready(eng, ph, s, i=0, per=4):
            eng.wait_ge(seg_done, SEG0[ph] + s + 1 + i * per)

        def feature_major(pe, ph, xh, xl, new=None, norm=None):
            def body(i, last):
                for b in range(2):
                    weights_ready(pe, ph, i, b)
                    for s in range(2):
                        c = 2 * b + s
                        bank_ready(pe, ph, c, i)
                        product(ps[:, ring(ph, c), :], b, 8 * s, DC, xh, xl).then_inc(seg_done, 1)
            if new is None:
                return pairs(pe, ph, body)
            weights_ready(pe, ph, 0, 0)
            bank_ready(pe, ph, 1)
            for n, k in enumerate(ORDER[new]):
                pe.wait_ge(in_lo, 8 * new + n + 1)
                for s in range(2):
                    ins = product(ps[:, ring(ph, s), :], 0, 8 * s + k, 1, xh[:, k:k + 1, :], xl[:, k:k + 1, :],
                                  start=n == 0, stop=n == DC - 1)
                    if n == DC - 1:
                        ins.then_inc(seg_done, 1)
            if norm is not None:
                add_gathered(pe, norm, total=TOTAL.get(norm))
            weights_ready(pe, ph, 0, 1)
            for s in range(2):
                if s and norm is not None:
                    spread_rms(pe, norm)
                bank_ready(pe, ph, 2 + s)
                product(ps[:, ring(ph, 2 + s), :], 1, 8 * s, DC, xh, xl).then_inc(seg_done, 1)
            pairs(pe, ph, body, 1)

        def one_chunk(pe, ph, c):
            weights_ready(pe, ph, 0, c // 2)
            bank_ready(pe, ph, c)
            product(ps[:, ring(ph, c), :], c // 2, 8 * (c % 2), DC, AH, AL).then_inc(seg_done, 1)

        def z_bank(c):
            return ring("z", c) if c < 2 else 4 + c

        def gdn_pe(pe):
            pe.wait_ge(ws_split, 2)
            for k in range(DC):
                w = slice(k * 32, (k + 1) * 32)
                nc.tensor.matmul(ps[0:32, 7, :], WSH[:, w], AH[:, k, :], start=k == 0, stop=False)
                nc.tensor.matmul(ps[0:32, 7, :], WSH[:, w], AL[:, k, :], start=False, stop=False)
                last = nc.tensor.matmul(ps[0:32, 7, :], WSL[:, w], AH[:, k, :], start=False, stop=k == DC - 1)
            last.then_inc(small_done, 1)
            one_chunk(pe, "z", 0)
            pe.wait_ge(sf_saved, 1)
            for t in range(T):
                last = turned(ps[:, 5, t * 32:(t + 1) * 32], SF[0:32, t * P:(t + 1) * P], ident[0:32, 0:32])
            last.then_inc(small_done, 1)
            one_chunk(pe, "z", 1)
            for n, sq in enumerate((TT, Y1)):
                pe.wait_ge(l2_sq, n + 1)
                for h in range(GH):
                    for t in range(T):
                        j = (n * GH + h) * T + t
                        last = nc.tensor.matmul(ps[:, 6, j:j + 1], sq[:, h, t, :], ones[:, 0:1], start=True, stop=True)
            last.then_inc(l2_sum, 1)
            pe.wait_ge(g_ready, 1)
            half = [CS[:, CON["half"] + n:CON["half"] + n + 1].to_broadcast([P, P]) for n in range(2)]
            for n, which in enumerate([CS[:, CON[x]:CON[x] + P] for x in ("tri", "after")] + half):
                last = nc.tensor.matmul(ps[:, 7, n * 16:(n + 1) * 16], which,
                                        G[:, :, :].rearrange("p t h -> p (t h)"), start=True, stop=True)
            last.then_inc(gsum_done, 1)
            pe.wait_ge(l2_rec, 1)
            for n in range(2):
                pe.wait_ge(bank_free, 4 + RING0["z"] + 2) if n == 0 else pe.wait_ge(gc_saved, 1)
                for h in range(GH):
                    for t in range(T):
                        j = (n * GH + h) * T + t
                        last = nc.tensor.matmul(ps[:, 4 * n + h, t * P:(t + 1) * P], L2[:, j:j + 1].to_broadcast([P, P]),
                                                ident[:, :], start=True, stop=True)
                last.then_inc(l2_rows, 1)
            pe.wait_ge(l2_done, 2)
            for t in range(T):
                tok = slice(t * P, (t + 1) * P)
                o = 4 * (t % 2)
                if t >= 2:
                    pe.wait_ge(at_ready, t - 1)
                for h in range(GH):
                    f = slice(h * P, (h + 1) * P)
                    nc.tensor.matmul(ps[:, o, f], G[:, t, h:h + 1].to_broadcast([P, P]), CS[:, 0:P], start=True, stop=True)
                    nc.tensor.matmul(ps[:, o + 1, f], SG[:, t, h:h + 1].to_broadcast([P, P]), ident[:, :], start=True, stop=True)
                    nc.tensor.matmul(ps[:, o + 2, f], QKV[:, 4 + h, tok], QKV[:, 4 + h, tok], start=True, stop=True)
                    last = nc.tensor.matmul(ps[:, o + 3, f], QKV[:, 4 + h, tok], QKV[:, h, tok], start=True, stop=True)
                last.then_inc(rows_done, 1)
            pe.wait_ge(at_ready, T)
            for t in range(T):
                pe.wait_ge(tt_ready, t + 1)
                for h in range(GH):
                    last = turned(ps[:, t, h * P:(h + 1) * P], TT[:, t, h, :], ident[:, :])
                last.then_inc(y_ps, 1)
            for lev in range(1, 6):
                for t in range(T):
                    n = 4 * lev + t
                    pe.wait_ge(off_ready, n - 3)
                    pe.wait_ge(t_ready, n - 3)
                    pe.wait_ge(tt_ready, n - 3)
                    for h in range(GH):
                        last = nc.tensor.matmul(ps[:, t, h * P:(h + 1) * P], OFF[:, t, h, :], Tm[:, t, h, :], start=True, stop=True)
                    last.then_inc(y_ps, 1)
                for t in range(T):
                    n = 4 * lev + t
                    pe.wait_ge(y_sb, n + 1 - 4)
                    pe.wait_ge(tt_ready, n - 3)
                    for h in range(GH):
                        last = nc.tensor.matmul(ps[:, 4 + t, h * P:(h + 1) * P], TT[:, t, h, :], Y1[:, t, h, :], start=True, stop=True)
                    last.then_inc(d_ps, 1)
                    for h in range(GH):
                        last = nc.tensor.matmul(ps[:, t, h * P:(h + 1) * P], Y1[:, t, h, :], TT[:, t, h, :], start=True, stop=True)
                    last.then_inc(dt_ps, 1)
            for t in range(T):
                tok = slice(t * P, (t + 1) * P)
                pe.wait_ge(tt_ready, 20 + t + 1)
                for n in range(2):
                    for h in range(GH):
                        last = turned(ps[:, 4 * n + t, h * P:(h + 1) * P], QKV[:, 4 + 4 * n + h, tok], ident[:, :])
                last.then_inc(kv_ps, 1)
            for t in range(T):
                pe.wait_ge(kv_sb, t + 1)
                for h in range(GH):
                    nc.tensor.matmul(ps[:, t, h * P:(h + 1) * P], OFF[:, t, h, :], TT[:, t, h, :], start=True, stop=True)
                    last = nc.tensor.matmul(ps[:, 4 + t, h * P:(h + 1) * P], TT[:, t, h, :], AT[:, t, h, :], start=True, stop=True)
                last.then_inc(wu_ps, 1)
            def z_late():
                weights_ready(pe, "z", 0, 1)
                for s in range(2):
                    for k in range(DC):
                        yield product(ps[:, 6 + s, :], 1, 8 * s + k, 1, AH[:, k:k + 1, :], AL[:, k:k + 1, :],
                                      start=k == 0, stop=k == DC - 1), k == DC - 1

            z_steps = z_late()

            def z_step():
                ins, whole = next(z_steps)
                if whole:
                    ins.then_inc(seg_done, 1)

            pe.wait_ge(wu_sb, 2 * T)
            for c in range(S // C):
                t, r = c // 2, C * (c % 2)
                rows, tok = slice(r, r + C), slice(c * C, (c + 1) * C)
                pe.wait_ge(state_ready, c + 1)
                for h in range(GH):
                    last = nc.tensor.matmul(ps[rows, 0, h * P:(h + 1) * P], Tm[:, t, h, rows], ST[:, c % 2, h, :], start=True, stop=True)
                last.then_inc(ws_ps, 1)
                z_step()
                pe.wait_ge(u_ready, c + 1)
                for h in range(GH):
                    last = nc.tensor.matmul(ps[:, 1 + c % 2, h * P:(h + 1) * P], QKV[rows, 8 + h, t * P:(t + 1) * P],
                                            Y1[rows, t, h, :], start=True, stop=True)
                last.then_inc(ds_ps, 1)
                if c >= 2:
                    pe.wait_ge(o_sb, c - 1)
                for h in range(GH):
                    nc.tensor.matmul(ps[rows, 3 + c % 2, h * P:(h + 1) * P], QKV[:, h, tok], ST[:, c % 2, h, :], start=True, stop=False)
                    last = nc.tensor.matmul(ps[rows, 3 + c % 2, h * P:(h + 1) * P], QK[rows, t, h, rows], Y1[rows, t, h, :],
                                            start=False, stop=True)
                last.then_inc(o_ps, 1)
                z_step()
            pe.wait_ge(state_ready, S // C + 1)
            for c in range(2):
                one_chunk(pe, "nq", c)
            for t in range(T):
                pe.wait_ge(on_ready, t + 1)
                for h in range(GH):
                    last = turned(ps[:, 4 + t % 2, h * P:(h + 1) * P], AT[:, t, h, :], ident[:, :])
                last.then_inc(ot_ps, 1)
                if t >= 1:
                    pe.wait_ge(yt_ready, t)


        def flat(x):
            return x.rearrange("p a b -> p (a b)")

        def flat4(x):
            return x.rearrange("p a b c -> p (a b c)")

        def chunks(x, c, i, n=1):
            return x[:, c + 4 * i:c + 4 * i + n, :] if isinstance(i, int) else x[:, bass.ds(c + i * 4, n), :]

        def bank_read(eng, ph, c, i=0):
            eng.wait_ge(bank_free, 4 + RING0[ph] + c + 1 + i * 4)

        def qkv_act(act):
            def body(i, last):
                for b in range(2):
                    for s in range(2):
                        c = 2 * b + s
                        seg_ready(act, "qkv", c, i)
                        nc.scalar.mul(flat(Tm[:, c, :, :]), ps[:, ring("qkv", c), :],
                                      col("cqkv", (c * 4 + 3) + i * 16)).then_inc(conv_base, 1)
                    for s in range(2):
                        c = 2 * b + s
                        bank_read(act, "qkv", c, i)
                        nc.scalar.activation(chunks(QKV, c, i), Tm[:, c:c + 1, :, :].rearrange("p c a b -> p c (a b)"),
                                             ACT.Silu).then_inc(silu_done, 1)
                    stage_hi(act, "qkv", i, b, last)
            pairs(act, "qkv", body)

        def z_act(act, c):
            seg_ready(act, "z", c)
            nc.scalar.activation(ZS[:, c, :], ps[:, z_bank(c), :], ACT.Silu).then_inc(bank_free, 1)
            if c % 2:
                stage_hi(act, "z", 0, c // 2, True)

        def gdn_act(act):
            act.wait_ge(small_done, 1)
            nc.scalar.activation(SF[0:32, :], ps[0:32, 7, :], ACT.Copy).then_inc(sf_saved, 1)
            act.wait_ge(silu_done, 12)
            for n, sq in enumerate((TT, Y1)):
                nc.scalar.activation(flat4(sq[:, :, :, :]), flat(QKV[:, 4 * n:4 * n + 4, :]), ACT.Square).then_inc(l2_sq, 1)
            act.wait_ge(small_done, 2)
            nc.scalar.activation(flat(SM[:, :, :]), ps[:, 5, 0:T * 32], ACT.Copy).then_inc(sm_saved, 1)
            nc.scalar.activation(EA[:, :], col("alog", 0, 4), ACT.Exp).then_inc(soft, 1)
            act.wait_ge(sm_saved, 1)
            nc.scalar.activation(SG[:, :, :], SM[:, :, :], ACT.Tanh, scale=0.5).then_inc(sig_ready, 1)
            act.wait_ge(soft, 2)
            nc.scalar.activation(AA[:, 1, :, :], AA[:, 1, :, :], ACT.Exp, scale=-1.0).then_inc(soft, 1)
            act.wait_ge(soft, 4)
            nc.scalar.activation(AA[:, 1, :, :], AA[:, 1, :, :], ACT.Ln).then_inc(soft, 1)
            act.wait_ge(l2_sum, 1)
            nc.scalar.activation(L2[:, :], ps[:, 6, 0:2 * GH * T], ACT.Sqrt, bias=col("eps")).then_inc(l2_root, 1)
            z_act(act, 0)
            z_act(act, 1)
            act.wait_ge(gsum_done, 1)
            nc.scalar.activation(flat4(EX[:, :, :, :]), ps[:, 7, 0:64], ACT.Exp).then_inc(gsum_read, 1)
            for t in range(T):
                o = 4 * (t % 2)
                act.wait_ge(dec_pre, t + 1)
                nc.scalar.activation(flat(Y1[:, t, :, :]), ps[:, o, :], ACT.Exp).then_inc(row_exp, 1)
                nc.scalar.activation(Tm[:, t, :, :], Tm[:, t, :, :], ACT.Exp).then_inc(dec_exp, 1)
            for t in range(T):
                act.wait_ge(y_ps, t + 1)
                nc.scalar.activation(flat(Tm[:, t, :, :]), ps[:, t, :], ACT.Copy).then_inc(t_ready, 1)
            act.wait_ge(qd_ready, T)
            for lev in range(1, 6):
                for t in range(T):
                    act.wait_ge(y_ps, 4 * lev + t + 1)
                    nc.scalar.activation(flat(Y1[:, t, :, :]), ps[:, t, :], ACT.Copy).then_inc(y_sb, 1)
            for t in range(T):
                act.wait_ge(wu_ps, t + 1)
                nc.scalar.activation(flat(Tm[:, t, :, :]), ps[:, t, :], ACT.Copy).then_inc(wu_sb, 1)
                nc.scalar.activation(flat(Y1[:, t, :, :]), ps[:, 4 + t, :], ACT.Copy).then_inc(wu_sb, 1)
            for c in range(S // C):
                t, rows = c // 2, slice(C * (c % 2), C * (c % 2) + C)
                act.wait_ge(o_ps, c + 1)
                nc.scalar.activation(flat(AT[rows, t, :, :]), ps[rows, 3 + c % 2, :], ACT.Copy).then_inc(o_sb, 1)
                if c % 2:
                    act.wait_ge(o_sb, c + 1)
                    nc.scalar.activation(OFF[:, t, :, :], AT[:, t, :, :], ACT.Square).then_inc(o_sq, 1)
                if c == 5:
                    z_act(act, 2)
            z_act(act, 3)
            act.wait_ge(o_ms, 1)
            nc.scalar.activation(RO[:, :, :], RO[:, :, :], ACT.Sqrt).then_inc(o_root, 1)
            for t in range(T):
                act.wait_ge(yt_ready, t + 1)
                nc.scalar.activation(YAH[:, :, t * P:(t + 1) * P], TMP[:, t % 2, :].rearrange("p (h n) -> p h n", h=GH),
                                     ACT.Copy).then_inc(yt_hi, 1)

        def qkv_dve(dve):
            def body(i, last):
                for b in range(2):
                    for s in range(2):
                        c = 2 * b + s
                        y = flat(Tm[:, c, :, :])
                        dve.wait_ge(conv_base, c + 1 + i * 4)
                        for j in range(1, 4):
                            if j > 1:
                                dve.wait_ge(conv_step, 2 * c + j - 1 + i * 8)
                            nc.vector.scalar_tensor_tensor(
                                y[:, j:S], ps[:, ring("qkv", c), 0:S - j], col("cqkv", (c * 4 + 3 - j) + i * 16),
                                y[:, j:S], ALU.mult, ALU.add).then_inc(conv_step if j < 3 else bank_free, 1)
                    stage_lo(dve, "qkv", i, b, last)
            pairs(dve, "qkv", body)

        def split_small_act(act):
            act.wait_ge(con_landed, 16 * N_CON)
            nc.scalar.activation(WSH[:, :], WSR[:, :], ACT.Copy).then_inc(ws_split, 1)

        def split_small_dve(dve):
            dve.wait_ge(ws_split, 1)
            nc.vector.tensor_tensor(WSL[:, :], WSR[:, :], WSH[:, :].bitcast(F32), ALU.subtract).then_inc(ws_split, 1)

        def gdn_dve(dve, own):
            vec = nc.vector
            dve.wait_ge(sig_ready, 1)
            own.mark(vec.tensor_scalar(SG[:, :, :], SG[:, :, :], 0.5, 0.5, ALU.mult, ALU.add))
            dtb = col("dtb", 0, 4).unsqueeze(1).to_broadcast([P, T, GH])
            own.link(vec.tensor_tensor(AA[:, 0, :, :], SM[:, :, 4:8], dtb, ALU.add))
            own.link(vec.tensor_scalar(AA[:, 2, :, :], AA[:, 0, :, :], -1.0, None, ALU.mult))
            vec.tensor_tensor(AA[:, 1, :, :], AA[:, 0, :, :], AA[:, 2, :, :], ALU.max).then_inc(soft, 1)
            dve.wait_ge(soft, 3)
            vec.tensor_scalar(AA[:, 1, :, :], AA[:, 1, :, :], 1.0, None, ALU.add).then_inc(soft, 1)
            dve.wait_ge(soft, 5)
            own.link(vec.scalar_tensor_tensor(AA[:, 0, :, :], AA[:, 0, :, :], 0.0, AA[:, 1, :, :], ALU.max, ALU.add))
            ea = EA[:, :].unsqueeze(1).to_broadcast([P, T, GH])
            vec.scalar_tensor_tensor(G[:, :, :], AA[:, 0, :, :], -1.0, ea, ALU.mult, ALU.mult).then_inc(g_ready, 1)
            dve.wait_ge(l2_root, 1)
            vec.reciprocal(L2[:, :], L2[:, :]).then_inc(l2_rec, 1)
            stage_lo(dve, "z", 0, 0, True)
            dve.wait_ge(gsum_read, 1)
            vec.tensor_copy(flat(GC[:, :, :]), ps[:, 7, 0:16]).then_inc(gc_saved, 1)
            dve.wait_ge(gc_saved, 1)
            own.link(vec.tensor_tensor(BG[:, :, :], SG[:, :, 0:GH], EX[:, 0, :, :], ALU.mult))
            nc.vector.memset(ST[:, :, :, :], 0.0).then_inc(state_ready, 1)
            for n in range(2):
                dve.wait_ge(l2_rows, n + 1)
                x = flat(QKV[:, 4 * n:4 * n + 4, :])
                vec.scalar_tensor_tensor(x, x, float(P) ** -0.5 if n == 0 else 1.0, flat(ps[:, 4 * n:4 * n + 4, :]),
                                         ALU.mult, ALU.mult).then_inc(l2_done, 1)
            for t in range(T):
                o = 4 * (t % 2)
                dve.wait_ge(rows_done, t + 1)
                for h in range(GH):
                    ins = vec.scalar_tensor_tensor(Tm[:, t, h, :], ps[:, o, h * P:(h + 1) * P], GC[:, t, h:h + 1],
                                                   CS[:, CON["seen"]:CON["seen"] + P], ALU.subtract, ALU.min)
                ins.then_inc(dec_pre, 1)
                dve.wait_ge(dec_exp, t + 1)
                own.mark(vec.tensor_tensor(flat(QK[:, t, :, :]), ps[:, o + 3, :], flat(Tm[:, t, :, :]), ALU.mult))
                own.link(vec.tensor_tensor(flat(AT[:, t, :, :]), ps[:, o + 2, :], flat(Tm[:, t, :, :]), ALU.mult))
                vec.tensor_tensor(flat(AT[:, t, :, :]), flat(AT[:, t, :, :]), ps[:, o + 1, :], ALU.mult).then_inc(at_ready, 1)
            level = [CS[:, CON["level"] + n * P:CON["level"] + (n + 1) * P].unsqueeze(1).to_broadcast([P, GH, P])
                     for n in range(6)]
            eye = ident[:, :].unsqueeze(1).to_broadcast([P, GH, P])
            for t in range(T):
                dve.wait_ge(at_ready, t + 1)
                own.link(vec.tensor_tensor(TT[:, t, :, :], AT[:, t, :, :], level[0], ALU.mult))
                vec.scalar_tensor_tensor(TT[:, t, :, :], TT[:, t, :, :], -1.0, eye, ALU.mult, ALU.add).then_inc(tt_ready, 1)
            for lev in range(1, 6):
                for t in range(T):
                    n = 4 * lev + t
                    if lev < 5:
                        dve.wait_ge(d_ps, n - 3)
                        vec.tensor_tensor(flat(Tm[:, t, :, :]), flat(Tm[:, t, :, :]), ps[:, 4 + t, :],
                                          ALU.subtract).then_inc(t_ready, 1)
                    dve.wait_ge(dt_ps, n - 3)
                    vec.tensor_tensor(flat(TT[:, t, :, :]), flat(TT[:, t, :, :]), ps[:, t, :],
                                      ALU.subtract).then_inc(tt_ready, 1)
            for t in range(T):
                tok = slice(t * P, (t + 1) * P)
                wide = lambda x: x.unsqueeze(2).to_broadcast([P, GH, P])
                heads = lambda x: x.rearrange("p (h n) -> p h n", h=GH)
                dve.wait_ge(kv_ps, t + 1)
                vec.tensor_tensor(OFF[:, t, :, :], heads(ps[:, t, :]), wide(BG[:, t, :]), ALU.mult)
                vec.tensor_tensor(AT[:, t, :, :], heads(ps[:, 4 + t, :]), wide(SG[:, t, 0:GH]), ALU.mult)
                vec.tensor_tensor(QKV[:, 8:12, tok], heads(ps[:, t, :]), wide(EX[:, 1, t, :]), ALU.mult).then_inc(kv_sb, 1)
            for c in range(S // C):
                t, rows = c // 2, slice(C * (c % 2), C * (c % 2) + C)
                dve.wait_ge(ws_ps, c + 1)
                u = flat(Y1[rows, t, :, :])
                vec.tensor_tensor(u, u, ps[rows, 0, :], ALU.subtract).then_inc(u_ready, 1)
                dve.wait_ge(ds_ps, c + 1)
                if c:
                    dve.wait_ge(o_ps, c)
                for h in range(GH):
                    ins = vec.scalar_tensor_tensor(ST[:, (c + 1) % 2, h, :], ST[:, c % 2, h, :], EX[:, 2 + c % 2, t, h:h + 1],
                                                   ps[:, 1 + c % 2, h * P:(h + 1) * P], ALU.mult, ALU.add)
                ins.then_inc(state_ready, 1)
                if c % 2 and c > 1:
                    dve.wait_ge(o_sq, t)
                    vec.tensor_reduce(RO[:, t - 1, :], OFF[:, t - 1, :, :], AX, ALU.add)
            dve.wait_ge(o_sq, T)
            own.link(vec.tensor_reduce(RO[:, T - 1, :], OFF[:, T - 1, :, :], AX, ALU.add))
            vec.tensor_scalar(RO[:, :, :], RO[:, :, :], 1.0 / P, EPS, ALU.mult, ALU.add).then_inc(o_ms, 1)
            dve.wait_ge(o_root, 1)
            own.link(vec.reciprocal(RO[:, :, :], RO[:, :, :]))
            for t in range(T):
                vec.tensor_tensor(AT[:, t, :, :], AT[:, t, :, :], RO[:, t, :].unsqueeze(2).to_broadcast([P, GH, P]),
                                  ALU.mult).then_inc(on_ready, 1)
            stage_lo(dve, "z", 0, 1, True)
            bank_read(dve, "z", 3)
            for t in range(T):
                tok = slice(t * P, (t + 1) * P)
                dve.wait_ge(ot_ps, t + 1)
                tmp = TMP[:, t % 2, :].rearrange("p (h n) -> p h n", h=GH)
                if t >= 2:
                    dve.wait_ge(yt_lo, t - 1)
                vec.scalar_tensor_tensor(tmp, ps[:, 4 + t % 2, :].rearrange("p (h n) -> p h n", h=GH), col("gdn"),
                                         ZS[:, :, tok], ALU.mult, ALU.mult).then_inc(yt_ready, 1)
                dve.wait_ge(yt_hi, t + 1)
                vec.tensor_tensor(YAL[:, :, tok], tmp, YAH[:, :, tok].bitcast(F32), ALU.subtract).then_inc(yt_lo, 1)

        def gdn_pool(pool):
            for t in range(T):
                qd = QKV[:, 0:GH, t * P:(t + 1) * P]
                pool.wait_ge(row_exp, t + 1)
                nc.gpsimd.tensor_tensor(qd, qd, Y1[:, t, :, :], ALU.mult).then_inc(qd_ready, 1)
            for lev in range(1, 6):
                m = CS[:, CON["level"] + lev * P:CON["level"] + (lev + 1) * P].unsqueeze(1).to_broadcast([P, GH, P])
                for t in range(T):
                    pool.wait_ge(at_ready, T)
                    if lev > 1:
                        pool.wait_ge(y_ps, 4 * (lev - 1) + t + 1)
                    nc.gpsimd.tensor_tensor(OFF[:, t, :, :], AT[:, t, :, :], m, ALU.mult).then_inc(off_ready, 1)

        hid_ps, hid_ready, kv_c_ps, kv_c_sb = (sem(n) for n in (
            "hid_ps", "hid_ready", "kv_c_ps", "kv_c_sb"))
        cs_ps, cs_max, cs_exp, cs_pr, cp_ps, cp_sb, co_ps, co_done = (sem(n) for n in (
            "cs_ps", "cs_max", "cs_exp", "cs_pr", "cp_ps", "cp_sb", "co_ps", "co_done"))
        s_ps, s_max, p_ready, pt_ps, o2_ps, o2_done = (sem(n) for n in (
            "s_ps", "s_max", "p_ready", "pt_ps", "o2_ps", "o2_done"))
        pt_sb = [sem(f"pt_sb{b}") for b in range(2)]
        yb_ps, yb_hi, yb_lo, mb_ready = (sem(n) for n in ("yb_ps", "yb_hi", "yb_lo", "mb_ready"))
        gate_ready, mix_sum, mix_hi, mix_lo = (sem(n) for n in (
            "gate_ready", "mix_sum", "mix_hi", "mix_lo"))
        UNITS = [(qt, h, x) for qt in reversed(range(T)) for h in range(NH) for x in range(2)]

        def nsa_proj_pe(pe):
            for c in (2, 3):
                one_chunk(pe, "nq", c)
            for b in range(2):
                weights_ready(pe, "ncmp", 0, b)
                bank_ready(pe, "ncmp", b)
                product(ps[:, ring("ncmp", b), :], b, 0, DC, AH, AL).then_inc(seg_done, 1)
            weights_ready(pe, "nk", 0, 0)
            for s in range(2):
                bank_ready(pe, "nk", s)
                product(ps[:, ring("nk", s), :], 0, 8 * s, DC, AH, AL).then_inc(seg_done, 1)

        def nv_pe(pe, c):
            pe.wait_ge(w_lo_done, PIECE0["nv"] + 1)
            bank_ready(pe, "nv", c)
            for t in (2 * c, 2 * c + 1):
                tok = slice(t * P, (t + 1) * P)
                o = ps[:, ring("nv", c), (t % 2) * 256:(t % 2) * 256 + 256]
                for k in range(DC):
                    w = slice(k * 256, (k + 1) * 256)
                    nc.tensor.matmul(o, AH[:, k, tok], WH[1][:, w], start=k == 0, stop=False)
                    nc.tensor.matmul(o, AL[:, k, tok], WH[1][:, w], start=False, stop=False)
                    last = nc.tensor.matmul(o, AH[:, k, tok], WL[1][:, w], start=False, stop=k == DC - 1)
            last.then_inc(seg_done, 1)

        def nsa_proj_act(act):
            for b in range(2):
                stage_hi(act, "nq", 0, b, True)
            for b in range(2):
                stage2_hi(act, "ncmp", b)
            stage2_hi(act, "nk", 0)

        def nsa_proj_dve(dve):
            for m in range(4):
                seg_ready(dve, "nq", m)
                for s in range(2):
                    ins = nc.vector.tensor_scalar(QT[0:DK, 2 * m + s, :], ps[s * DK:(s + 1) * DK, ring("nq", m), :],
                                                  DK ** -0.5, None, ALU.mult)
                ins.then_inc(bank_free, 1)
                if m % 2:
                    stage_lo(dve, "nq", 0, m // 2, True)
            dve.wait_ge(cols_landed, 16)
            for x in range(2):
                dve.wait_ge(seg_done, SEG0["ncmp"] + x + 1)
                pos = cols[:, COLS["posk" if x == 0 else "posv"]:][:, 0:16]
                for g in range(NG):
                    src = ps[g * DK:(g + 1) * DK, ring("ncmp", x), :].rearrange("p (n k j) -> p j k n", k=8, j=2)
                    for par in range(2):
                        half = slice(par * DK, (par + 1) * DK)
                        for late in range(2):
                            ins = nc.vector.tensor_tensor(
                                Z[x][half, 8 * late:8 * late + 8, g * NC:(g + 1) * NC],
                                src[:, par, :, late:late + NC],
                                pos[half, 8 * late:8 * late + 8].unsqueeze(2).to_broadcast([DK, 8, NC]), ALU.add)
                ins.then_inc(bank_free, 1)
                stage2_lo(dve, "ncmp", x)
            for x in range(2):
                seg_ready(dve, "nk", x)
                for g in range(NG):
                    ins = nc.vector.tensor_copy(KT[0:DK, x, g, :], ps[g * DK:(g + 1) * DK, ring("nk", x), :])
                ins.then_inc(bank_free, 1)
            stage2_lo(dve, "nk", 0)

        def nv_dve(dve, c):
            seg_ready(dve, "nv", c)
            nc.vector.tensor_copy(flat(V1[:, 2 * c:2 * c + 2, :]), ps[:, ring("nv", c), :]).then_inc(bank_free, 1)

        def stage2_hi(act, ph, b):
            piece = PIECE0[ph] + (b if NPIECE[ph] > 1 else 0)
            n = PIECE_NB[piece + 2] * P
            act.wait_ge(raw_landed[b], 16 * ((piece + 2) // 2 + 1))
            act.wait_ge(seg_done, PIECE_SEG[piece + 1])
            nc.scalar.activation(WH[b][:, 0:n], RAW[b][:, 0:n], ACT.Copy).then_inc(w_hi_done, 1)

        def stage2_lo(dve, ph, b):
            piece = PIECE0[ph] + (b if NPIECE[ph] > 1 else 0)
            n = PIECE_NB[piece + 2] * P
            dve.wait_ge(w_hi_done, piece + 3)
            nc.vector.tensor_tensor(WL[b][:, 0:n], RAW[b][:, 0:n], WH[b][:, 0:n].bitcast(F32),
                                    ALU.subtract).then_inc(w_lo_done, 1)

        def nsa_pe(pe):
            def scores(u):
                qt, h, x = UNITS[u]
                n, bank = (qt + 1) * P, u % 4
                if u >= 4:
                    pe.wait_ge(p_ready, u - 3)
                else:
                    bank_read(pe, "nv", u) if u < 2 else pe.wait_ge(cp_sb, 1)
                nc.tensor.matmul(ps[:, bank, 0:n], QT[0:66, h, qt * P:n], KT[0:66, x, h // R, 0:n], start=True, stop=False)
                nc.tensor.matmul(ps[:, bank, qt * P:n], MB[:, 0, :], MB[:, 1, :], start=False, stop=True).then_inc(s_ps, 1)

            pe.wait_ge(w1_landed, 32)
            bank_read(pe, "ncmp", 1)
            for x in range(2):
                for f in range(2):
                    o = ps[:, 4, (2 * x + f) * 64:(2 * x + f) * 64 + 2 * NC]
                    for k in range(16):
                        last = nc.tensor.matmul(o, W1[x][:, k, f * P:(f + 1) * P], Z[x][:, k, :], start=k == 0, stop=k == 15)
            last.then_inc(hid_ps, 1)
            nv_pe(pe, 0)
            pe.wait_ge(nsa_landed, 16 * N_NSA)
            pe.wait_ge(hid_ready, 1)
            for f in range(2):
                nc.tensor.matmul(ps[0:DK, 5, 0:2 * NC], W2[:, f, :], HID[:, f, :], start=f == 0, stop=f == 1)
            for g in range(NG):
                for r in range(R):
                    for f in range(2):
                        last = nc.tensor.matmul(ps[32 * r:32 * r + NC, 6 + g, 0:DK], HID[:, 2 + f, g * NC:(g + 1) * NC],
                                                W2[:, 2 + f, :], start=f == 0, stop=f == 1)
            last.then_inc(kv_c_ps, 1)
            pe.wait_ge(kv_c_sb, 1)
            for qt in range(T):
                for h in range(NH):
                    last = nc.tensor.matmul(ps[:, 4 + qt // 2, (qt % 2) * 256 + h * 32:(qt % 2) * 256 + h * 32 + 32],
                                            QT[0:66, h, qt * P:(qt + 1) * P], KC[0:66, h // R, :], start=True, stop=True)
            last.then_inc(cs_ps, 1)
            nv_pe(pe, 1)
            bank_read(pe, "nk", 1)
            pe.wait_ge(mb_ready, 2)
            pe.wait_ge(cs_pr, 1)
            for qt in range(T):
                for g in range(NG):
                    j = (qt % 2) * 2 + g
                    last = turned(ps[:, 2 + qt // 2, j * P:(j + 1) * P],
                                               SC[:, qt, g * R:(g + 1) * R, :].rearrange("p a b -> p (a b)"), ident[:, :])
            last.then_inc(cp_ps, 1)
            scores(0)
            scores(1)
            pe.wait_ge(cp_sb, 1)
            for qt in range(T):
                for g in range(NG):
                    j = (qt % 2) * 2 + g
                    last = nc.tensor.matmul(ps[:, 4 + qt, g * 256:(g + 1) * 256], PT[:, qt // 2, j * P:(j + 1) * P],
                                            VB[:, g, :], start=True, stop=True)
            last.then_inc(co_ps, 1)
            def turn(u):
                qt, h, x = UNITS[u]
                pe.wait_ge(p_ready, u + 1)
                pe.wait_ge(pt_sb[u % 2], u // 2) if u >= 2 else pe.wait_ge(co_done, 1)
                for kt in range(qt + 1):
                    last = turned(ps[:, 4 + u % 2, kt * P:(kt + 1) * P], PR[:, u % 4, kt * P:(kt + 1) * P], ident[:, :])
                last.then_inc(pt_ps, 1)

            def values(u):
                qt, h, x = UNITS[u]
                g, pair = h // R, u // 2
                pe.wait_ge(pt_sb[u % 2], u // 2 + 1)
                if u == 0:
                    pe.wait_ge(co_done, 2)
                if pair >= 2 and x == 0:
                    pe.wait_ge(o2_done, pair - 1)
                for kt in range(qt + 1):
                    last = nc.tensor.matmul(ps[:, 6 + pair % 2, x * DK:(x + 1) * DK], PT[:, u % 4, kt * P:(kt + 1) * P],
                                            V1[:, kt, x * P + g * DK:x * P + (g + 1) * DK], start=kt == 0, stop=kt == qt)
                last.then_inc(o2_ps, 1)

            n = len(UNITS)
            for u in range(n + 1):
                if u + 2 < n:
                    scores(u + 2)
                if u < n:
                    turn(u)
                if u:
                    values(u - 1)
            pe.wait_ge(o2_done, n // 2)
            for qt in range(T):
                for c in range(4):
                    last = turned(ps[:, qt, c * P:(c + 1) * P], Y[:, qt, c * P:(c + 1) * P], ident[:, :])
                last.then_inc(yb_ps, 1)

        def save_probs(eng, copy, u):
            n = (UNITS[u][0] + 1) * P
            eng.wait_ge(pt_ps, u + 1)
            if u >= 4:
                eng.wait_ge(o2_ps, u - 3)
            copy(PT[:, u % 4, 0:n], ps[:, 4 + u % 2, 0:n]).then_inc(pt_sb[u % 2], 1)

        def nsa_act(act):
            act.wait_ge(hid_ps, 1)
            nc.scalar.activation(HID[:, :, :], ps[:, 4, 0:256].rearrange("p (a n) -> p a n", a=4)[:, :, 0:2 * NC],
                                 ACT.Gelu_apprx_tanh).then_inc(hid_ready, 1)
            act.wait_ge(cs_max, 1)
            nc.scalar.activation(SC[:, :, :, :], SC[:, :, :, :], ACT.Exp).then_inc(cs_exp, 1)
            stage2_hi(act, "nv", 1)
            for u, (qt, h, x) in enumerate(UNITS + [(0, 0, 0)]):
                n, pair = (qt + 1) * P, u // 2
                if u == len(UNITS):
                    save_probs(act, nc.scalar.copy, u - 1)
                    break
                act.wait_ge(s_max, u + 1)
                if u >= 4:
                    act.wait_ge(pt_ps, u - 3)
                if pair >= 4 and x == 0:
                    act.wait_ge(o2_done, pair - 3)
                nc.scalar.activation(PR[:, u % 4, 0:n], ps[:, u % 4, 0:n], ACT.Exp, bias=NM[:, u % 4, :],
                                     accum_out=LS[:, pair % 4, x:x + 1]).then_inc(p_ready, 1)
                if u and u % 2 == 0:
                    save_probs(act, nc.scalar.copy, u - 1)
            for qt in range(T):
                act.wait_ge(yb_ps, qt + 1)
                nc.scalar.activation(YBH[:, :, qt * P:(qt + 1) * P], ps[:, qt, :].rearrange("p (c n) -> p c n", c=4),
                                     ACT.Copy).then_inc(yb_hi, 1)

        def nsa_dve(dve, own):
            vec = nc.vector
            dve.wait_ge(nsa_landed, 16 * N_NSA)
            own.mark(vec.memset(KC[0:DK, :, :], 0.0))
            own.link(vec.memset(VB[:, :, :], 0.0))
            nv_dve(dve, 0)
            dve.wait_ge(kv_c_ps, 1)
            for g in range(NG):
                vec.tensor_copy(KC[0:DK, g, 0:NC], ps[0:DK, 5, g * NC:(g + 1) * NC])
                for r in range(R):
                    ins = vec.tensor_copy(VB[32 * r:32 * r + NC, g, r * DK:(r + 1) * DK], ps[32 * r:32 * r + NC, 6 + g, 0:DK])
            ins.then_inc(kv_c_sb, 1)
            dve.wait_ge(cs_ps, 1)
            rows = SC[:, :, :, :].rearrange("p t h n -> p (t h) n")
            for b in range(2):
                cn = CN[:, 2 * b:2 * b + 2, :].unsqueeze(2).to_broadcast([P, 2, NH, 32])
                ins = vec.tensor_tensor(SC[:, 2 * b:2 * b + 2, :, :], ps[:, 4 + b, :].rearrange("p (t h n) -> p t h n", t=2, h=NH),
                                        cn, ALU.add)
                own.mark(ins)
            own.wait()
            mx, l = (SX[:, n, :, :].rearrange("p t h -> p (t h)") for n in range(2))
            own.link(vec.tensor_reduce(mx, rows, AX, ALU.max))
            vec.tensor_tensor(rows, rows, mx.unsqueeze(2).to_broadcast([P, T * NH, 32]), ALU.subtract).then_inc(cs_max, 1)
            dve.wait_ge(cs_exp, 1)
            c01 = C01[:, :, :].unsqueeze(2).to_broadcast([P, T, NH, 32])
            vec.tensor_tensor(SC[:, :, :, :], SC[:, :, :, :], c01, ALU.mult).then_inc(cs_pr, 1)
            nv_dve(dve, 1)
            dve.wait_ge(cs_pr, 1)
            own.link(vec.tensor_reduce(l, rows, AX, ALU.add))
            own.link(vec.tensor_scalar(l, l, 1e-30, None, ALU.max))
            own.link(vec.reciprocal(l, l))
            own.link(vec.tensor_tensor(SX[:, 2, :, :], SX[:, 1, :, :],
                                       SG[:, :, 8:32].rearrange("p t (h j) -> p t h j", j=3)[:, :, :, 0], ALU.mult))
            dve.wait_ge(cp_ps, 1)
            vec.tensor_copy(PT[:, 0:2, :], ps[:, 2:4, :]).then_inc(cp_sb, 1)
            def top(u):
                qt, h, x = UNITS[u]
                dve.wait_ge(s_ps, u + 1)
                vec.tensor_reduce(NM[:, u % 4, :], ps[:, u % 4, 0:(qt + 1) * P], AX, ALU.max, negate=True).then_inc(s_max, 1)

            top(0)
            top(1)
            dve.wait_ge(co_ps, 1)
            for qt in range(T):
                ins = vec.tensor_tensor(Y[:, qt, :].rearrange("p (h d) -> p h d", h=NH),
                                        ps[:, 4 + qt, :].rearrange("p (h d) -> p h d", h=NH),
                                        SX[:, 2, qt, :].unsqueeze(2).to_broadcast([P, NH, DK]), ALU.mult)
                if qt % 2:
                    ins.then_inc(co_done, 1)
            dve.wait_ge(co_done, 2)

            def add(pair):
                qt, h, _ = UNITS[2 * pair]
                b = pair % 2
                dve.wait_ge(o2_ps, 2 * pair + 2)
                own.link(vec.reciprocal(RL[:, b, :], LS[:, pair % 4, :]))
                own.link(vec.tensor_tensor(RL[:, b, :], RL[:, b, :], SG[:, qt, 9 + 3 * h:11 + 3 * h], ALU.mult))
                y = Y[:, qt, h * DK:(h + 1) * DK]
                own.link(vec.scalar_tensor_tensor(y, ps[:, 6 + b, 0:DK], RL[:, b, 0:1], y, ALU.mult, ALU.add))
                vec.scalar_tensor_tensor(y, ps[:, 6 + b, DK:2 * DK], RL[:, b, 1:2], y, ALU.mult, ALU.add).then_inc(o2_done, 1)

            n = len(UNITS)
            for u in range(n + 1):
                if u == 4:
                    stage2_lo(dve, "nv", 1)
                if u + 2 < n:
                    top(u + 2)
                if u < n and u % 2 == 0:
                    save_probs(dve, vec.tensor_copy, u)
                if u and u % 2 == 0:
                    add(u // 2 - 1)
            for qt in range(T):
                tok = slice(qt * P, (qt + 1) * P)
                dve.wait_ge(yb_hi, qt + 1)
                vec.tensor_tensor(YBL[:, :, tok], ps[:, qt, :].rearrange("p (c n) -> p c n", c=4),
                                  YBH[:, :, tok].bitcast(F32), ALU.subtract).then_inc(yb_lo, 1)

        def mix_pe(pe):
            pe.wait_ge(yb_lo, T)
            pe.wait_ge(yt_lo, T)
            def body(i, last):
                for b in range(2):
                    weights_ready(pe, "mix", i, b)
                    y_h, y_l = (YAH, YAL) if b == 0 else (YBH, YBL)
                    bank_ready(pe, "mix", 2 * b, i)
                    product(ps[:, ring("mix", 2 * b), :], b, 0, DC, AH, AL).then_inc(seg_done, 1)
                    bank_ready(pe, "mix", 2 * b + 1, i)
                    product(ps[:, ring("mix", 2 * b + 1), :], b, DC, 4, y_h, y_l).then_inc(seg_done, 1)
            pairs(pe, "mix", body)

        def at(x, m):
            return x[:, m:m + 1, :] if isinstance(m, int) else x[:, bass.ds(m, 1), :]

        def mix_act(act):
            def body(i, last):
                for b in range(2):
                    seg_ready(act, "mix", 2 * b, i)
                    nc.scalar.activation(SQ[:, b, :], ps[:, ring("mix", 2 * b), :], ACT.Tanh, scale=0.5).then_inc(gate_ready, 1)
                    stage_hi(act, "mix", i, b, last)
                act.wait_ge(mix_sum, i + 1)
                nc.scalar.activation(at(GHI, i), TMP[:, 0:1, :], ACT.Copy, scale=0.5).then_inc(mix_hi, 1)
            pairs(act, "mix", body)

        def mix_dve(dve):
            def body(i, last):
                for b in range(2):
                    dve.wait_ge(gate_ready, b + 1 + i * 2)
                    seg_ready(dve, "mix", 2 * b + 1, i)
                    nc.vector.scalar_tensor_tensor(TMP[:, b, :], SQ[:, b, :], 1.0, ps[:, ring("mix", 2 * b + 1), :],
                                                   ALU.add, ALU.mult).then_inc(bank_free, 2)
                    stage_lo(dve, "mix", i, b, last)
                bank_read(dve, "mix", 3, i)
                nc.vector.tensor_tensor(TMP[:, 0, :], TMP[:, 0, :], TMP[:, 1, :], ALU.add).then_inc(mix_sum, 1)
                dve.wait_ge(mix_hi, i + 1)
                nc.vector.scalar_tensor_tensor(at(GLO, i), TMP[:, 0:1, :], 0.5, at(GHI, i).bitcast(F32),
                                               ALU.mult, ALU.subtract).then_inc(mix_lo, 1)
                dve.wait_ge(mix_lo, i + 1)
            pairs(dve, "mix", body)

        def wo_pe(pe):
            weights_ready(pe, "wo", 0, 0)
            for k in range(DC):
                pe.wait_ge(mix_lo, k + 1)
                for m in range(2):
                    ins = product(ps[:, WO_BANK[m], :], 0, 8 * m + k, 1, GHI[:, k:k + 1, :], GLO[:, k:k + 1, :],
                                  start=k == 0, stop=k == DC - 1)
                    if k == DC - 1:
                        ins.then_inc(seg_done, 1)
            pe.wait_ge(bank_free, 4 + RING0["up"])
            for m in range(2, DC):
                if m % 2 == 0:
                    weights_ready(pe, "wo", m // 4, m // 2 % 2)
                if m == 7:
                    pe.wait_ge(y0_saved, 1)
                product(ps[:, WO_BANK[m], :], m // 2 % 2, 8 * (m % 2), DC, GHI, GLO).then_inc(seg_done, 1)
            add_gathered(pe, 1)

        def down_pe(pe, ph, k, freed, count):
            def chunk(m, bank, ready=None):
                for b in range(2):
                    weights_ready(pe, ph, m, b)
                    product(bank, b, 0, FC // 2, HH[:, b * 11:b * 11 + 11, :], HL[:, b * 11:b * 11 + 11, :],
                            start=b == 0, stop=b == 1, ready=ready if b else None).then_inc(seg_done, 1)
            hidden = FC * (ph == "down2")
            pe.wait_ge(hid_lo, hidden + FC - 2)
            pe.wait_ge(bank_free, 4 + RING0["up" if ph == "down" else "up2"] + 2 * FC)
            chunk(0, ps[:, 0:1, :], ready=lambda k: pe.wait_ge(hid_lo, hidden + FC // 2 + k + 1))
            with pe.Fori(1, 7) as m:
                chunk(m, ps[:, bass.ds(m, 1), :])
            pe.wait_ge(freed, count)
            chunk(7, ps[:, 0:1, :])
            add_gathered(pe, k)

        def wo_act(act):
            for m in range(DC):
                seg_ready(act, "wo", m)
                square_in(act, 1, m, m % 2, ps[:, WO_BANK[m]:WO_BANK[m] + 1, :])
                if m % 2 and m < DC - 1:
                    stage_hi(act, "wo", m // 4, m // 2 % 2, m >= 4)

        def wo_dve(dve):
            dve.wait_ge(sq_ready, 8 + 1)
            nc.vector.tensor_copy(YX[:, :], ps[:, WO_BANK[0], :]).then_inc(y0_saved, 1)
            for p in range(4):
                for m in (2 * p, 2 * p + 1):
                    if m:
                        gather(dve, 1, m, m % 2)
                if p < 3:
                    stage_lo(dve, "wo", p // 2, p % 2, p >= 2)

        up_conv = sem("up_conv")
        up_base, up_step, up_gelu, up_prod, hid_hi, hid_lo = (sem(n) for n in (
            "up_base", "up_step", "up_gelu", "up_prod", "hid_hi", "hid_lo"))

        def up_act(act):
            def body(i, last, early=False):
                for b in range(2):
                    if early:
                        stage_hi(act, "up", i, b, last)
                    for s, (y, buf) in enumerate(((SQ, CG), (TMP, CV))):
                        bank_read(act, "up", 2 * b + s, i)
                        nc.scalar.activation(buf[:, b, :], y[:, b, :], ACT.Identity,
                                             bias=col("cffnb", (2 * b + s) + i * 4),
                                             scale=col("cffn", (6 * b + 3 * s + 2) + i * 12)).then_inc(up_base, 1)
                    if not early:
                        stage_hi(act, "up", i, b, last)
                    act.wait_ge(up_conv, 2 * b + 1 + i * 4)
                    nc.scalar.activation(CG[:, b, :], CG[:, b, :], ACT.Gelu_apprx_tanh).then_inc(up_gelu, 1)
                    act.wait_ge(up_prod, b + 1 + i * 2)
                    nc.scalar.activation(at(HH, i * 2 + b), CG[:, b:b + 1, :], ACT.Copy).then_inc(hid_hi, 1)
            body(0, False, early=True)
            pairs(act, "up", body, 1)

        def up_dve(dve):
            def body(i, last, early=False):
                for b in range(2):
                    if early:
                        stage_lo(dve, "up", i, b, last)
                    for s, y in enumerate((SQ, TMP)):
                        seg_ready(dve, "up", 2 * b + s, i)
                        nc.vector.tensor_tensor(y[:, b, :], ps[:, ring("up", 2 * b + s), :], RR[:, :],
                                                ALU.mult).then_inc(bank_free, 1)
                    bank_read(dve, "up", 2 * b + 1, i)
                    for s, (y, buf) in enumerate(((SQ, CG), (TMP, CV))):
                        dve.wait_ge(up_base, 2 * b + s + 1 + i * 4)
                        for j in (1, 2):
                            if j == 2:
                                dve.wait_ge(up_step, 2 * b + s + 1 + i * 4)
                            nc.vector.scalar_tensor_tensor(
                                buf[:, b, j:S], y[:, b, 0:S - j],
                                col("cffn", (6 * b + 3 * s + 2 - j) + i * 12), buf[:, b, j:S], ALU.mult,
                                ALU.add).then_inc(up_step if j == 1 else up_conv, 1)
                    if not early:
                        stage_lo(dve, "up", i, b, last)
                    dve.wait_ge(up_conv, 2 * b + 2 + i * 4)
                    dve.wait_ge(up_gelu, b + 1 + i * 2)
                    nc.vector.tensor_tensor(CG[:, b, :], CG[:, b, :], CV[:, b, :], ALU.mult).then_inc(up_prod, 1)
                    dve.wait_ge(hid_hi, b + 1 + i * 2)
                    nc.vector.tensor_tensor(at(HL, i * 2 + b), CG[:, b:b + 1, :], at(HH, i * 2 + b).bitcast(F32),
                                            ALU.subtract).then_inc(hid_lo, 1)
            body(0, False, early=True)
            pairs(dve, "up", body, 1)

        def up2_act(act):
            def body(i, last):
                for b in range(2):
                    stage_hi(act, "up2", i, b, last)
                    bank_read(act, "up2", 2 * b, i)
                    nc.scalar.activation(CG[:, b, :], CG[:, b, :], ACT.Silu).then_inc(up_gelu, 1)
                    act.wait_ge(up_prod, FC + b + 1 + i * 2)
                    nc.scalar.activation(at(HH, i * 2 + b), CG[:, b:b + 1, :], ACT.Copy).then_inc(hid_hi, 1)
            pairs(act, "up2", body)

        def up2_dve(dve):
            def body(i, last):
                for b in range(2):
                    stage_lo(dve, "up2", i, b, last)
                    for s, y in enumerate((CG, CV)):
                        seg_ready(dve, "up2", 2 * b + s, i)
                        nc.vector.tensor_tensor(y[:, b, :], ps[:, ring("up2", 2 * b + s), :], RR[:, :],
                                                ALU.mult).then_inc(bank_free, 1)
                    bank_read(dve, "up2", 2 * b + 1, i)
                    dve.wait_ge(up_gelu, FC + b + 1 + i * 2)
                    nc.vector.tensor_tensor(CG[:, b, :], CG[:, b, :], CV[:, b, :], ALU.mult).then_inc(up_prod, 1)
                    dve.wait_ge(hid_hi, FC + b + 1 + i * 2)
                    nc.vector.tensor_tensor(at(HL, i * 2 + b), CG[:, b:b + 1, :], at(HH, i * 2 + b).bitcast(F32),
                                            ALU.subtract).then_inc(hid_lo, 1)
            pairs(dve, "up2", body)

        def down_chunks(eng, chunk):
            chunk(0, 0, False)
            with eng.Fori(0, 3) as i:
                chunk(i * 2 + 1, 1, False)
                chunk(i * 2 + 2, 0, False)
            chunk(7, 1, True)

        def down_seg(eng, ph, m):
            eng.wait_ge(seg_done, m * 2 + (SEG0[ph] + 2))

        def down_act(act):
            def chunk(m, par, last):
                stage_hi(act, "down", m, 0, last)
                down_seg(act, "down", m)
                square_in(act, 3, m, par, ps[:, 0:1, :] if last else at(ps, m))
                if last:
                    rms_root(act, 3)
                stage_hi(act, "down", m, 1, last)
            down_chunks(act, chunk)

        def down_dve(dve):
            def chunk(m, par, last):
                stage_lo(dve, "down", m, 0, last)
                if isinstance(m, int) and m == 0:
                    dve.wait_ge(sq_ready, 8 * 3 + 1)
                    nc.vector.tensor_copy(YX[:, :], ps[:, 0, :]).then_inc(y0_saved, 1)
                if not last:
                    stage_lo(dve, "down", m, 1, last)
                if not isinstance(m, int) or m:
                    gather(dve, 3, m, par)
            down_chunks(dve, chunk)

        ph_ready, pl_ready, e_gate = (sem(n) for n in ("ph_ready", "pl_ready", "e_gate"))

        def ple_pe(pe):
            for m in range(DC):
                b, i = m % 2, m // 2
                weights_ready(pe, "ple", i, b)
                bank_ready(pe, "ple", 2 * b + 1, i)
                if m == 0:
                    pe.wait_ge(h_ready, 8 + 2)
                    for n, k in enumerate(ORDER[2]):
                        pe.wait_ge(in_lo, 8 * 2 + n + 1)
                        ins = product(ps[:, ring("ple", 1), :], 0, 2 + k, 1, AH[:, k:k + 1, :], AL[:, k:k + 1, :],
                                      start=n == 0, stop=n == DC - 1)
                    ins.then_inc(seg_done, 1)
                    pe.wait_ge(pl_ready, 1)
                else:
                    product(ps[:, ring("ple", 2 * b + 1), :], b, 2, DC, AH, AL).then_inc(seg_done, 1)
                product(ps[:, ring("ple", 2 * b), :], b, 0, 2, PH, PL).then_inc(seg_done, 1)
            add_gathered(pe, 4)

        def ple_act(act):
            act.wait_ge(p_landed, 16)
            nc.scalar.activation(PH[:, :, :], PX[:, :, :], ACT.Copy).then_inc(ph_ready, 1)
            for n, m in enumerate(ORDER[2]):
                act.wait_ge(h_ready, 8 + n + 1)
                nc.scalar.activation(AH[:, m, :], hT[:, m, :], ACT.Copy).then_inc(in_hi, 1)
            for m in range(DC):
                b, i = m % 2, m // 2
                seg_ready(act, "ple", 2 * b + 1, i)
                if m >= 2:
                    bank_read(act, "ple", 2 * b + 1, i - 1)
                nc.scalar.activation(GP[:, b, :], ps[:, ring("ple", 2 * b + 1), :], ACT.Tanh, scale=0.5).then_inc(e_gate, 1)
                if m < DC - 1:
                    stage_hi(act, "ple", i, b, m >= 6)
                act.wait_ge(bank_free, 4 + RING0["ple"] + 2 * m + 2)
                square_in(act, 4, m, b, E[:, m:m + 1, :])

        def ple_input(dve):
            for n in range(DC + 1):
                if n < DC:
                    m = ORDER[2][n]
                    post_chunk(dve, 1, n, m, "ffn_post", YX[:, :] if m == 0 else y_bank(m))
                if n == 3:
                    stage_lo(dve, "down", 7, 1, True)
                if n == DC:
                    dve.wait_ge(ph_ready, 1)
                    nc.vector.tensor_tensor(PL[:, :, :], PX[:, :, :], PH[:, :, :].bitcast(F32), ALU.subtract).then_inc(pl_ready, 1)
                if n:
                    m = ORDER[2][n - 1]
                    dve.wait_ge(in_hi, 8 * 2 + n)
                    nc.vector.tensor_tensor(AL[:, m, :], hT[:, m, :], AH[:, m, :].bitcast(F32), ALU.subtract).then_inc(in_lo, 1)

        def ple_dve(dve):
            for m in range(DC):
                b, i = m % 2, m // 2
                dve.wait_ge(e_gate, m + 1)
                nc.vector.scalar_tensor_tensor(E[:, m, :], GP[:, b, :], 1.0, ps[:, ring("ple", 2 * b), :], ALU.add,
                                               ALU.mult).then_inc(bank_free, 2)
                if m < DC - 1:
                    stage_lo(dve, "ple", i, b, m >= 6)
                if m:
                    gather(dve, 4, m, b)

        glu_gate, b_added, s2_ps, s2_max, p2_ready = (sem(n) for n in (
            "glu_gate", "b_added", "s2_ps", "s2_max", "p2_ready"))
        pt2_ps, pt2_sb, o3_ps, o3_done, y2_ps, y2_hi, y2_lo = (sem(n) for n in (
            "pt2_ps", "pt2_sb", "o3_ps", "o3_done", "y2_ps", "y2_hi", "y2_lo"))
        ug_ready, prod_ready = sem("ug_ready"), sem("prod_ready")
        taps_begun, tap_done, last_tap_done, mu_ps, mu_ready, centred, csq_ready = (sem(n) for n in (
            "taps_begun", "tap_done", "last_tap_done", "mu_ps", "mu_ready", "centred", "csq_ready"))
        var_ps, var_ready, var_root, var_rec, var_rows, normed, cu_ready, cu_hi, cu_lo = (sem(n) for n in (
            "var_ps", "var_ready", "var_root", "var_rec", "var_rows", "normed", "cu_ready", "cu_hi", "cu_lo"))
        UNITS2 = [(qt, h) for qt in reversed(range(T)) for h in range(NH)]
        DVE_CC = CC // 2
        SPLIT, EARLY = 13, 8
        TAPS = [(j, c) for c in range(DVE_CC) for j in range(EARLY)]
        TAPS += [(j, c) for j in range(EARLY, CT) for c in range(DVE_CC)] + [(j, DVE_CC) for j in range(SPLIT, CT)]
        LATE_TAPS = [(j, c) for j in range(CT) for c in range(DVE_CC, CC) if c > DVE_CC or j < SPLIT]
        U_MEAN, U_SQUARE, U_VAR, U_STAGE, U_ROWS = 12, 17, 22, 25, 28

        def y2_bank(qt):
            return (0, 1, 2, 4)[qt]

        def blk2_pe(pe):
            feature_major(pe, "glu", AH, AL, new=3, norm=5)
            feature_major(pe, "qk2", AH, AL)
            for b in range(2):
                weights_ready(pe, "v2", 0, b)
                for t in range(T):
                    tok = slice(t * P, (t + 1) * P)
                    if b == 0:
                        bank_ready(pe, "v2", t)
                    for k in range(4):
                        w = slice(k * 512, (k + 1) * 512)
                        o, kk = ps[:, ring("v2", t), :], 4 * b + k
                        nc.tensor.matmul(o, AH[:, kk, tok], WH[b][:, w], start=kk == 0, stop=False)
                        nc.tensor.matmul(o, AL[:, kk, tok], WH[b][:, w], start=False, stop=False)
                        last = nc.tensor.matmul(o, AH[:, kk, tok], WL[b][:, w], start=False, stop=kk == DC - 1)
                    if t % 2:
                        last.then_inc(seg_done, 1)

            def scores(u):
                qt, h = UNITS2[u]
                n, r = (qt + 1) * P, slice((h % 2) * DK, (h % 2 + 1) * DK)
                if u >= 3:
                    pe.wait_ge(p2_ready, u - 2)
                else:
                    bank_read(pe, "v2", (u - RING0["v2"]) % 4)
                nc.tensor.matmul(ps[:, u % 3, 0:n], QT2[r, h // 2, qt * P:n], KT2[r, h // 2, 0:n], start=True,
                                 stop=True).then_inc(s2_ps, 1)

            def turn(u):
                qt, h = UNITS2[u]
                pe.wait_ge(p2_ready, u + 1)
                if u >= 2:
                    pe.wait_ge(pt2_sb, u - 1)
                for kt in range(qt + 1):
                    last = turned(ps[:, 4 + u % 2, kt * P:(kt + 1) * P], PR2[:, u % 4, kt * P:(kt + 1) * P], ident[:, :])
                last.then_inc(pt2_ps, 1)

            def values(u):
                qt, h = UNITS2[u]
                pe.wait_ge(pt2_sb, u + 1)
                if u >= 4 and h % 2 == 0:
                    pe.wait_ge(o3_done, u // 2 - 1)
                for kt in range(qt + 1):
                    last = nc.tensor.matmul(ps[:, 6 + u // 2 % 2, (h % 2) * DK:(h % 2 + 1) * DK], PT2[:, u % 4, kt * P:(kt + 1) * P],
                                            V2[:, kt, h * DK:(h + 1) * DK], start=kt == 0, stop=kt == qt)
                last.then_inc(o3_ps, 1)

            def norm_mean():
                pe.wait_ge(tap_done, len(TAPS))
                pe.wait_ge(last_tap_done, len(LATE_TAPS))
                for c in range(CC):
                    last = nc.tensor.matmul(ps[:, 3, :], ones[:, :], CU[:, c, :], start=c == 0, stop=c == CC - 1)
                last.then_inc(mu_ps, 1)

            def norm_var():
                pe.wait_ge(csq_ready, CC)
                for c in range(CC):
                    for t in range(T):
                        last = nc.tensor.matmul(ps[:, 3, t:t + 1], UG[:, c, t * P:(t + 1) * P], ones[:, 0:1],
                                                start=c == 0 and t == 0, stop=c == CC - 1 and t == T - 1)
                last.then_inc(var_ps, 1)

            n = len(UNITS2)
            scores(0)
            scores(1)
            for u in range(n + 1):
                if u + 2 < n:
                    scores(u + 2)
                if u < n:
                    turn(u)
                if u:
                    values(u - 1)
                if u == U_MEAN:
                    norm_mean()
                if u == U_VAR:
                    norm_var()
                if u == U_ROWS:
                    pe.wait_ge(var_rec, 1)
                    for t in range(T):
                        last = nc.tensor.matmul(ps[:, 3, t * P:(t + 1) * P], VC[:, t:t + 1].to_broadcast([P, P]),
                                                ident[:, :], start=True, stop=True)
                    last.then_inc(var_rows, 1)
            pe.wait_ge(o3_done, n // 2)
            for qt in range(T):
                for c in range(4):
                    last = turned(ps[:, y2_bank(qt), c * P:(c + 1) * P], Y2[:, qt, c * P:(c + 1) * P], ident[:, :])
                last.then_inc(y2_ps, 1)
            pe.wait_ge(y2_lo, T)
            weights_ready(pe, "wo2", 0, 0)
            for k in range(DC):
                if k >= 4:
                    pe.wait_ge(cu_lo, k - 3)
                for m in range(2):
                    ins = product(y_bank(m), 0, 8 * m + k, 1, AH[:, k:k + 1, :], AL[:, k:k + 1, :], start=k == 0,
                                  stop=k == DC - 1)
                    if k == DC - 1:
                        ins.then_inc(seg_done, 1)
            for m in range(2, DC):
                if m % 2 == 0:
                    weights_ready(pe, "wo2", m // 4, m // 2 % 2)
                if m == 7:
                    pe.wait_ge(h_ready, 25)
                product(y_bank(m), m // 2 % 2, 8 * (m % 2), DC, AH, AL).then_inc(seg_done, 1)

        def blk2_act(act):
            for c in range(CC):
                i, b = c // 2, c % 2
                bank_read(act, "glu", 2 * b + 1, i)
                nc.scalar.activation(SQ[:, b, :], SQ[:, b, :], ACT.Tanh, scale=0.5).then_inc(glu_gate, 1)
                stage_hi(act, "glu", i, b, i == 1)
            act.wait_ge(taps_begun, 1)
            act.wait_ge(ug_ready, CC)
            left = list(enumerate(LATE_TAPS))

            def products(n):
                for k, (j, c) in left[:n]:
                    src, w = UG[:, c, j:j + S], col("cw2", c * CT + j)
                    if j == 0:
                        ins = nc.scalar.activation(CU[:, c, :], src, ACT.Identity, bias=B2[:, c:c + 1], scale=w)
                    else:
                        act.wait_ge(last_tap_done, k - 1)
                        ins = nc.scalar.mul(SQ[:, k % 2, :], src, w)
                    ins.then_inc(prod_ready, 1)
                del left[:n]

            for p in range(NPIECE["qk2"]):
                products(7)
                stage_hi(act, "qk2", p // 2, p % 2, p >= 2)
            products(len(LATE_TAPS))
            def save(u):
                n = (UNITS2[u][0] + 1) * P
                act.wait_ge(pt2_ps, u + 1)
                if u >= 4:
                    act.wait_ge(o3_ps, u - 3)
                nc.scalar.copy(PT2[:, u % 4, 0:n], ps[:, 4 + u % 2, 0:n]).then_inc(pt2_sb, 1)

            for u, (qt, h) in enumerate(UNITS2):
                n, pair = (qt + 1) * P, u // 2
                act.wait_ge(s2_max, u + 1)
                if u >= 4:
                    act.wait_ge(pt2_ps, u - 3)
                if pair >= 4 and h % 2 == 0:
                    act.wait_ge(o3_done, pair - 3)
                nc.scalar.activation(PR2[:, u % 4, 0:n], ps[:, u % 3, 0:n], ACT.Exp, bias=NM2[:, u % 4, :],
                                     accum_out=LS2[:, pair % 4, h % 2:h % 2 + 1]).then_inc(p2_ready, 1)
                if u:
                    save(u - 1)
                if U_SQUARE <= u < U_SQUARE + CC:
                    c = u - U_SQUARE
                    act.wait_ge(centred, c + 1)
                    nc.scalar.activation(UG[:, c, 0:S], CU[:, c, :], ACT.Square).then_inc(csq_ready, 1)
                if u in (U_STAGE, U_STAGE + 2):
                    stage_hi(act, "v2", 0, (u - U_STAGE) // 2, True)
                if u == U_VAR + 2:
                    act.wait_ge(var_ready, 1)
                    nc.scalar.activation(VC[:, :], VC[:, :], ACT.Sqrt).then_inc(var_root, 1)
            save(len(UNITS2) - 1)
            for qt in range(T):
                act.wait_ge(y2_ps, qt + 1)
                nc.scalar.activation(AH[:, 0:4, qt * P:(qt + 1) * P], ps[:, y2_bank(qt), :].rearrange("p (c n) -> p c n", c=4),
                                     ACT.Copy).then_inc(y2_hi, 1)
            for c in range(CC):
                act.wait_ge(normed, c + 1)
                nc.scalar.activation(CU[:, c, :], CU[:, c, :], ACT.Silu, bias=col("lnb", c), scale=col("lng", c)).then_inc(cu_ready, 1)
                act.wait_ge(cu_ready, c + 1)
                nc.scalar.activation(AH[:, 4 + c, :], CU[:, c, :], ACT.Copy).then_inc(cu_hi, 1)
            for m in range(DC):
                act.wait_ge(h_ready, 25 + m)
                square_in(act, 6, m, m % 2, hT[:, m:m + 1, :])
                if m % 2 and m < DC - 1:
                    stage_hi(act, "wo2", m // 4, m // 2 % 2, m >= 4)

        def blk2_dve(dve, own):
            vec = nc.vector
            left = list(enumerate(TAPS))

            def taps(n):
                for k, (j, c) in left[:n]:
                    src, w = UG[:, c, j:j + S], col("cw2", c * CT + j)
                    if j == 0:
                        ins = vec.tensor_scalar(CU[:, c, :], src, w, B2[:, c:c + 1], ALU.mult, ALU.add)
                    else:
                        if (j - 1, c) in TAPS:
                            dve.wait_ge(tap_done, TAPS.index((j - 1, c)) + 1)
                        else:
                            dve.wait_ge(last_tap_done, LATE_TAPS.index((j - 1, c)) + 1)
                        ins = vec.scalar_tensor_tensor(CU[:, c, :], src, w, CU[:, c, :], ALU.mult, ALU.add)
                    ins.then_inc(tap_done, 1)
                del left[:n]

            own.mark(vec.tensor_scalar(B2[:, :], col("cb2", 0, CC), 2.0, None, ALU.mult))
            vec.memset(UG[:, :, 0:CT - 1], 0.0).then_inc(taps_begun, 1)
            own.wait()
            dve.wait_ge(taps_begun, 1)
            for c in range(CC):
                i, b = c // 2, c % 2
                if c >= 2:
                    dve.wait_ge(ug_ready, c - 1)
                for s, y in enumerate((TMP, SQ)):
                    seg_ready(dve, "glu", 2 * b + s, i)
                    vec.tensor_tensor(y[:, b, :], ps[:, ring("glu", 2 * b + s), :], RR[:, :], ALU.mult).then_inc(bank_free, 1)
                bank_read(dve, "glu", 2 * b + 1, i)
                dve.wait_ge(glu_gate, c + 1)
                vec.scalar_tensor_tensor(UG[:, c, CT - 1:], SQ[:, b, :], 1.0, TMP[:, b, :], ALU.add,
                                         ALU.mult).then_inc(ug_ready, 1)
                stage_lo(dve, "glu", i, b, i == 1)
                if c < 3:
                    dve.wait_ge(ug_ready, c + 1)
                    taps(EARLY)
            dve.wait_ge(ug_ready, CC)
            for p in range(NPIECE["qk2"]):
                i, b = p // 2, p % 2
                for s in range(2):
                    c = 2 * b + s
                    seg_ready(dve, "qk2", c, i)
                    if i == 0:
                        ins = vec.scalar_tensor_tensor(QT2[:, c, :], ps[:, ring("qk2", c), :], DK ** -0.5, RR[:, :],
                                                       ALU.mult, ALU.mult)
                    else:
                        ins = vec.tensor_tensor(KT2[:, c, :], ps[:, ring("qk2", c), :], RR[:, :], ALU.mult)
                    ins.then_inc(bank_free, 1)
                    taps(4)
                stage_lo(dve, "qk2", i, b, i == 1)
                taps(5)
            dve.wait_ge(blk2_landed, 32)
            own.link(vec.tensor_tensor(BT[:, :, :], BT[:, :, :], col("far", 0, 8).unsqueeze(2).to_broadcast([P, NH, 256]), ALU.subtract))
            own.link(vec.tensor_tensor(BT[:, :, P:], BT[:, :, P:], MB2[:, :].unsqueeze(1).to_broadcast([P, NH, P]), ALU.add))
            taps(len(left) - 10)
            for t in range(T):
                if t % 2 == 0:
                    seg_ready(dve, "v2", 2 + t // 2)
                vec.tensor_scalar(V2[:, t, :], ps[:, ring("v2", t), :], RC[:, t:t + 1], None, ALU.mult).then_inc(bank_free, 1)

            def top(u):
                qt, h = UNITS2[u]
                n, w = (qt + 1) * P, min((qt + 1) * P, 256)
                dve.wait_ge(s2_ps, u + 1)
                vec.tensor_tensor(ps[:, u % 3, n - w:n], ps[:, u % 3, n - w:n], BT[:, h, 256 - w:256], ALU.add).then_inc(b_added, 1)
                dve.wait_ge(b_added, u + 1)
                vec.tensor_reduce(NM2[:, u % 4, :], ps[:, u % 3, 0:n], AX, ALU.max, negate=True).then_inc(s2_max, 1)

            def add(pair):
                qt, h = UNITS2[2 * pair]
                b = pair % 2
                dve.wait_ge(o3_ps, 2 * pair + 2)
                own.link(vec.reciprocal(RL2[:, b, :], LS2[:, pair % 4, :]))
                y = Y2[:, qt, h * DK:(h + 2) * DK].rearrange("p (x d) -> p x d", x=2)
                vec.tensor_tensor(y, ps[:, 6 + b, 0:2 * DK].rearrange("p (x d) -> p x d", x=2),
                                  RL2[:, b, :].unsqueeze(2).to_broadcast([P, 2, DK]), ALU.mult).then_inc(o3_done, 1)

            n = len(UNITS2)
            top(0)
            top(1)
            for u in range(n + 1):
                if u + 2 < n:
                    top(u + 2)
                if u and u % 2 == 0:
                    add(u // 2 - 1)
                taps(1)
                if u == U_MEAN + 1:
                    dve.wait_ge(mu_ps, 1)
                    vec.tensor_scalar(TMP[:, 0, :], ps[:, 3, :], 1.0 / 512, None, ALU.mult).then_inc(mu_ready, 1)
                if u == U_VAR + 1:
                    dve.wait_ge(var_ps, 1)
                    vec.tensor_scalar(VC[:, :], ps[:, 3, 0:T], 1.0 / 512, 4 * LN_EPS, ALU.mult, ALU.add).then_inc(var_ready, 1)
                if u == U_ROWS - 1:
                    dve.wait_ge(var_root, 1)
                    vec.reciprocal(VC[:, :], VC[:, :]).then_inc(var_rec, 1)
                if u in (U_STAGE + 1, U_STAGE + 3):
                    stage_lo(dve, "v2", 0, (u - U_STAGE - 1) // 2, True)
            dve.wait_ge(var_rows, 1)
            for c in range(CC):
                vec.tensor_tensor(CU[:, c, :], CU[:, c, :], ps[:, 3, :], ALU.mult).then_inc(normed, 1)
            for qt in range(T):
                tok = slice(qt * P, (qt + 1) * P)
                dve.wait_ge(y2_hi, qt + 1)
                vec.tensor_tensor(AL[:, 0:4, tok], ps[:, y2_bank(qt), :].rearrange("p (c n) -> p c n", c=4),
                                  AH[:, 0:4, tok].bitcast(F32), ALU.subtract).then_inc(y2_lo, 1)
            for c in range(CC):
                dve.wait_ge(cu_hi, c + 1)
                vec.tensor_tensor(AL[:, 4 + c, :], CU[:, c, :], AH[:, 4 + c, :].bitcast(F32), ALU.subtract).then_inc(cu_lo, 1)
            for m in range(DC):
                seg_ready(dve, "wo2", m)
                vec.tensor_tensor(hT[:, m, :], hT[:, m, :], y_bank(m), ALU.add).then_inc(h_ready, 1)
                if m >= 2:
                    gather(dve, 6, m - 1, (m - 1) % 2)
                if m % 2 and m < DC - 1:
                    stage_lo(dve, "wo2", m // 4, m // 2 % 2, m >= 4)

        def conv_pool(pool):
            for k, (j, c) in enumerate(LATE_TAPS):
                pool.wait_ge(prod_ready, k + 1)
                if j:
                    pool.wait_ge(last_tap_done, k - 1 if j < SPLIT else k)
                    nc.gpsimd.tensor_tensor(CU[:, c, :], CU[:, c, :], SQ[:, k % 2, :], ALU.add).then_inc(last_tap_done, 1)
                else:
                    nc.gpsimd.memset(B2[:, c:c + 1], 0.0).then_inc(last_tap_done, 1)
            pool.wait_ge(mu_ready, 1)
            for c in range(CC):
                nc.gpsimd.tensor_tensor(CU[:, c, :], CU[:, c, :], TMP[:, 0, :], ALU.subtract).then_inc(centred, 1)

        def down2_act(act):
            def chunk(m, par, last):
                stage_hi(act, "down2", m, 0, last)
                act.wait_ge(h_ready, m + 33)
                square_in(act, 7, m, par, at(hT, m))
                stage_hi(act, "down2", m, 1, last)
            down_chunks(act, chunk)

        def down2_dve(dve):
            def chunk(m, par, last):
                stage_lo(dve, "down2", m, 0, last)
                down_seg(dve, "down2", m)
                nc.vector.tensor_tensor(at(hT, m), at(hT, m), ps[:, 0:1, :] if last else at(ps, m), ALU.add).then_inc(h_ready, 1)
                stage_lo(dve, "down2", m, 1, last)
                if not isinstance(m, int) or m:
                    gather(dve, 7, m, par)
            down_chunks(dve, chunk)

        def out_dve(dve):
            for m in range(DC):
                nc.vector.scalar_tensor_tensor(hT[:, m, :], hT[:, m, :], col("final", m), RR[:, :], ALU.mult,
                                               ALU.mult).then_inc(out_ready, 1)

        def first_hi(act, b):
            act.wait_ge(raw_landed[b], 16)
            nc.scalar.activation(WH[b][:, :], RAW[b][:, :], ACT.Copy).then_inc(w_hi_done, 1)

        def first_lo(dve, b):
            dve.wait_ge(w_hi_done, b + 1)
            nc.vector.tensor_tensor(WL[b][:, :], RAW[b][:, :], WH[b][:, :].bitcast(F32), ALU.subtract).then_inc(w_lo_done, 1)

        block = ctx.enter_context(nc.Block())

        @block.sync
        def _(sp):
            xv = xT.rearrange("(c p) s -> p c s", p=P)
            for q in range(4):
                sp.dma_start(hT[:, 2 * q:2 * q + 2, :], xv[:, 2 * q:2 * q + 2, :]).then_inc(x_landed[q], 16)

            def load(name, b, piece):
                n = NB[name] * P
                sp.dma_start(RAW[b][:, 0:n], wstream[piece, :, 0:n] if isinstance(piece, int) else
                             wstream[bass.ds(piece, 1), :, 0:n].rearrange("a p n -> p (a n)")).then_inc(raw_landed[b], 16)

            for name, n, nb, _ in PHASES:
                first = 0
                if PIECE0[name] == 0:
                    load(name, 0, 0)
                    load(name, 1, 1)
                    first = 1
                if n == 1:
                    sp.wait_ge(w_lo_done, PIECE0[name] - 1)
                    load(name, PIECE0[name] % 2, PIECE0[name])
                elif n // 2 - first > 1:
                    with sp.Fori(first, n // 2) as i:
                        for b in range(2):
                            sp.wait_ge(w_lo_done, PIECE0[name] + b - 1 + i * 2)
                            load(name, b, i * 2 + (PIECE0[name] + b))
                else:
                    for i in range(first, n // 2):
                        for b in range(2):
                            sp.wait_ge(w_lo_done, PIECE0[name] + b - 1 + i * 2)
                            load(name, b, i * 2 + (PIECE0[name] + b))
            ov = out.rearrange("(c p) s -> p c s", p=P)
            for m in range(0, DC, 2):
                sp.wait_ge(out_ready, m + 1)
                sp.dma_start(ov[:, m, :], hT[:, m, :]).then_inc(out_stored[0], 16)
            sp.wait_ge(out_stored[0], 16 * DC // 2)

        @block.gpsimd
        def _(pool):
            pool.memset(ones[:, :], 1.0).then_inc(set_up, 1)
            gdn_pool(pool)
            pool.wait_ge(yt_lo, T)
            nc.gpsimd.tensor_copy(MB[:, 0, :], ident[:, :]).then_inc(mb_ready, 1)
            nc.gpsimd.tensor_copy(MB[:, 1, :], NG_T[:, :]).then_inc(mb_ready, 1)
            pool.dma_start(QT[64:66, :, :], alibi_d).then_inc(nsa_landed, 16)
            pool.dma_start(KT[64:66, :, :, :], krow_d).then_inc(nsa_landed, 16)
            pool.dma_start(KC[64:66, :, :], crow_d).then_inc(nsa_landed, 16)
            pool.dma_start(W2[:, :, :], w2_d).then_inc(nsa_landed, 16)
            pool.dma_start(CN[:, :, :], cneg_d).then_inc(nsa_landed, 16)
            pool.dma_start(C01[:, :, :], c01_d).then_inc(nsa_landed, 16)
            pool.dma_start(W1[0][:, :, :], w1k_d).then_inc(w1_landed, 16)
            pool.dma_start(W1[1][:, :, :], w1v_d).then_inc(w1_landed, 16)
            pool_gather(pool, 2)
            pool.wait_ge(seg_done, SEG0["ple"])
            pool.dma_start(PX[:, :, :], pT.rearrange("(c p) s -> p c s", p=P)).then_inc(p_landed, 16)
            pool_gather(pool, 5)
            pool.wait_ge(h_ready, 24)
            pool.dma_start(BT[:, :, :], bias2_d).then_inc(blk2_landed, 16)
            pool.dma_start(MB2[:, :], causal_d).then_inc(blk2_landed, 16)
            conv_pool(pool)

        @block.scalar
        def _(act):
            act.dma_start(cols[:, :], cols_d).then_inc(cols_landed, 16)
            act.dma_start(ident[:, :], ident_d).then_inc(ident_landed, 16)
            for dst, src in ((NG_T[:, :], causal_d), (CS[:, :], consts_d), (WSR[:, :], wsm_d)):
                act.dma_start(dst, src).then_inc(con_landed, 16)
            for m in range(DC):
                if m % 2 == 0:
                    act.wait_ge(x_landed[m // 2], 16)
                square(act, 0, m, hT[:, m, :])
            first_hi(act, 0)
            rms_root(act, 0)
            pre_hi(act, 0)
            first_hi(act, 1)
            split_small_act(act)
            qkv_act(act)
            gdn_act(act)
            nsa_proj_act(act)
            nsa_act(act)
            mix_act(act)
            wo_act(act)
            rms_root(act, 1)
            normed_input_act(act, 1, 2, "ffn_pre", 0)
            stage_hi(act, "wo", 1, 1, True)
            rms_root(act, 2)
            up_act(act)
            down_act(act)
            ple_act(act)
            rms_root(act, 4)
            stage_hi(act, "ple", 3, 1, True)
            normed_input_act(act, 3, 5, "mix2", 16)
            rms_root(act, 5)
            blk2_act(act)
            act.wait_ge(seg_done, SEG0["up2"])
            for m in range(DC):
                scaled_hi(act, 4, m, "ffn2")
            stage_hi(act, "wo2", 1, 1, True)
            rms_root(act, 6)
            up2_act(act)
            down2_act(act)
            rms_root(act, 7)
            ov = out.rearrange("(c p) s -> p c s", p=P)
            for m in range(1, DC, 2):
                act.wait_ge(out_ready, m + 1)
                act.dma_start(ov[:, m, :], hT[:, m, :]).then_inc(out_stored[1], 16)
            act.wait_ge(out_stored[1], 16 * DC // 2)

        @block.vector
        def _(dve):
            own = Own(dve, dve_own)
            dve.memset(YX[:, 0:1], 0.0).then_inc(bank_free, 4)
            dve.wait_ge(cols_landed, 16)
            first_lo(dve, 0)
            rms_rest(dve, 0)
            pre_rest(dve, 0, "mix_pre")
            first_lo(dve, 1)
            split_small_dve(dve)
            qkv_dve(dve)
            gdn_dve(dve, own)
            nsa_proj_dve(dve)
            nsa_dve(dve, own)
            mix_dve(dve)
            wo_dve(dve)
            rms_rest(dve, 1)
            normed_input_dve(dve, 1, "ffn_pre",
                             lambda n, m: post_chunk(dve, 0, n, m, "mix_post",
                                                     YX[:, :] if m == 0 else ps[:, WO_BANK[m], :]))
            stage_lo(dve, "wo", 1, 1, True)
            rms_rest(dve, 2)
            up_dve(dve)
            down_dve(dve)
            rms_rest(dve, 3)
            ple_input(dve)
            ple_dve(dve)
            rms_rest(dve, 4, eps=4 * EPS)
            normed_input_dve(dve, 3, "mix2", lambda n, m: post_chunk(dve, 2, n, m, "ple_post", E[:, m, :]))
            stage_lo(dve, "ple", 3, 1, True)
            rms_rest(dve, 5)
            blk2_dve(dve, own)
            for m in range(DC):
                scaled_lo(dve, 4, m, "ffn2", m)
                if m == 1:
                    gather(dve, 6, DC - 1, 1)
            stage_lo(dve, "wo2", 1, 1, True)
            rms_rest(dve, 6)
            up2_dve(dve)
            down2_dve(dve)
            rms_rest(dve, 7)
            out_dve(dve)

        @block.tensor
        def _(pe):
            pe.wait_ge(set_up, 1)
            for m in range(DC):
                add_squares(pe, 0, m)
            pe.wait_ge(ident_landed, 16)
            spread_rms(pe, 0)
            feature_major(pe, "qkv", AH, AL, new=0)
            gdn_pe(pe)
            nsa_proj_pe(pe)
            nsa_pe(pe)
            mix_pe(pe)
            wo_pe(pe)
            spread_rms(pe, 1)
            pe.wait_ge(h_ready, 2)
            feature_major(pe, "up", AH, AL, new=1, norm=2)
            down_pe(pe, "down", 3, y0_saved, 2)
            spread_rms(pe, 3)
            ple_pe(pe)
            spread_rms(pe, 4)
            blk2_pe(pe)
            feature_major(pe, "up2", AH, AL, new=4, norm=6)
            down_pe(pe, "down2", 7, h_ready, 33)
            spread_rms(pe, 7)


def shape_tables():
    i = np.arange(P)
    same = lambda w: i[:, None] // w == i[None, :] // w
    parts = [(i[:, None] <= i[None, :]) & same(C), (i[:, None] > i[None, :]) & same(C),
             i[:, None] < C, i[:, None] >= C]
    parts.append(np.where(parts[0], 0.0, NEG))
    for w in (1, 2, 4, 8, 16, 32):
        parts.append(same(2 * w) & (i[:, None] // w % 2 == 0) & (i[None, :] // w % 2 == 1))
    consts = np.concatenate([x.astype(np.float32) for x in parts], axis=1)
    ident = np.eye(P, dtype=np.float32)
    causal = np.where(i[None, :] > i[:, None], np.float32(NEG), np.float32(0))
    t = (np.arange(T)[:, None, None] * P + i[None, :, None])
    ends = np.arange(32)[None, None, :] * CMP_STRIDE + CMP_LEN - 1
    seen = ((t >= ends) & (np.arange(32) < NC)).transpose(1, 0, 2)
    cneg = np.where(seen, np.float32(0), np.float32(NEG))
    c01 = seen.astype(np.float32)
    slope = 2.0 ** (-8.0 * np.arange(1, NH + 1) / NH)
    alibi = np.stack([np.repeat(slope[:, None], S, 1), -slope[:, None] * np.arange(S)]).astype(np.float32)
    krow = np.stack([np.broadcast_to(np.arange(S), (2, NG, S)), np.ones((2, NG, S))]).astype(np.float32)
    crow = np.stack([np.broadcast_to(ends[0, 0], (NG, 32)), np.ones((NG, 32))]).astype(np.float32)
    return consts, ident, causal, cneg, c01, alibi, krow, crow


def t5_bucket(dist):
    d = np.maximum(dist, 1).astype(np.float32)
    large = 16 + (np.log(d / np.float32(16)) / np.float32(np.log(128 / 16)) * np.float32(16)).astype(np.int32)
    return np.where(dist < 16, dist, np.minimum(large, 31))


def blocks(w, k0, k1, c0, c1):
    return w[k0:k1, c0:c1].reshape((k1 - k0) // P, P, c1 - c0).transpose(1, 0, 2)


def weight_stream(a):
    w = a["w_in"][0]
    ks, fm = [], lambda w_, cols_: [np.concatenate([blocks(w_, 0, w_.shape[0], c, c + P).reshape(P, -1) for c in cs], 1) for cs in cols_]
    two = lambda c0, n: [[c0 + 2 * P * j, c0 + 2 * P * j + P] for j in range(n)]
    ks += fm(w, two(0, 6)) + fm(w, two(1536, 2))
    ks += fm(w, two(2056, 2)) + fm(w, [[2568], [2696]]) + fm(w, [[2824, 3080]])
    ks += [np.concatenate([blocks(w, 0, D, 2952, 3080), blocks(w, 0, D, 3208, 3336)], 2).reshape(P, -1)]
    for j in range(DC):
        for g0, y in ((3360, a["w_a2d"][0]), (3360 + D, a["w_b2d"][0])):
            ks.append(np.concatenate([blocks(w, 0, D, g0 + j * P, g0 + j * P + P).reshape(P, -1),
                                      blocks(y, 0, 512, j * P, j * P + P).reshape(P, -1)], 1))
    ks += fm(a["w_o"][0], two(0, 4))
    ks += fm(a["w_up"][0], [[j * P, FF + j * P] for j in range(FC)])

    def down(w_):
        return [blocks(w_, x * 11 * P, (x + 1) * 11 * P, j * P, j * P + P).reshape(P, -1) for j in range(DC) for x in range(2)]
    ks += down(a["w_down"][0])
    ks += [np.concatenate([blocks(a["w_ple"][0], 0, PLE, j * P, j * P + P).reshape(P, -1),
                           blocks(a["w_ple_gate"][0], 0, D, j * P, j * P + P).reshape(P, -1)], 1) for j in range(DC)]
    w2 = a["w_in_2"][0]
    ks += fm(w2, [[1536 + j * P, 2048 + j * P] for j in range(CC)]) + fm(w2, two(0, 4))
    ks += [blocks(w2, x * 512, (x + 1) * 512, 1024, 1536).reshape(P, -1) for x in range(2)]
    ks += fm(a["w_out_2"][0], two(0, 4))
    ks += [np.concatenate([blocks(a["w_gate_2"][0], 0, D, j * P, j * P + P).reshape(P, -1),
                           blocks(a["w_up_2"][0], 0, D, j * P, j * P + P).reshape(P, -1)], 1) for j in range(FC)]
    ks += down(a["w_down_2"][0])
    assert [x.shape[1] // P for x in ks] == PIECE_NB[:PIECES]
    stream = np.zeros((PIECES, P, BLK * P), np.float32)
    for j, x in enumerate(ks):
        stream[j, :, :x.shape[1]] = x
    return stream


def lay_out(a):
    a = {k: np.asarray(v) for k, v in a.items()}
    consts, ident, causal, cneg, c01, alibi, krow, crow = shape_tables()
    cols = np.zeros((P, NCOLS), np.float32)

    def put(name, x):
        cols[:, COLS[name]:COLS[name] + x.shape[1]] = x

    vec = lambda x: x.reshape(-1, P).T
    for name, key in (("mix_pre", "norm_mix_pre"), ("mix_post", "norm_mix_post"), ("ffn_pre", "norm_ffn_pre"),
                      ("ffn_post", "norm_ffn_post"), ("ple_post", "norm_ple_post"), ("mix2", "mix_norm_g_2"),
                      ("ffn2", "ffn_norm_g_2"), ("final", "final_norm_g_2"), ("gdn", "gdn_norm"),
                      ("cb2", "conv_b_2"), ("lng", "conv_ln_g_2"), ("lnb", "conv_ln_b_2")):
        put(name, vec(a[key]))
    put("cqkv", a["conv_qkv"][0].reshape(4, 12, P).transpose(2, 1, 0).reshape(P, -1))
    put("cffn", a["conv_ffn"][0].reshape(3, 2, FC, P).transpose(3, 2, 1, 0).reshape(P, -1))
    put("cffnb", a["conv_ffn_b"][0].reshape(2, FC, P).transpose(2, 1, 0).reshape(P, -1))
    put("cw2", a["conv_w_2"][0].reshape(CT, CC, P).transpose(2, 1, 0).reshape(P, -1))
    put("alog", np.broadcast_to(a["a_log"], (P, GH)))
    put("dtb", np.broadcast_to(a["dt_bias"], (P, GH)))
    put("far", np.broadcast_to(a["rel_bias_2"][31], (P, NH)))
    put("posk", a["cmp_pos_k"][0].reshape(16, P).T)
    put("posv", a["cmp_pos_v"][0].reshape(16, P).T)
    put("eps", np.full((P, 1), EPS, np.float32))
    w = a["w_in"][0]
    wsm = np.concatenate([blocks(w, 0, D, 2048, 2056), blocks(w, 0, D, 3336, 3360)], 2).reshape(P, -1)
    q, kk = np.arange(P)[:, None], np.arange(256)[None, :]
    bias = a["rel_bias_2"][t5_bucket(np.maximum(q + P - kk, 0))].transpose(0, 2, 1)
    w2 = np.concatenate([blocks(a["cmp_w2_k"][0], 0, CMP_HID, 0, DK), blocks(a["cmp_w2_v"][0], 0, CMP_HID, 0, DK)], 1)
    return {
        "wstream": weight_stream(a), "xT": a["x"][0].T, "pT": a["p"][0, 0].T, "cols_d": cols, "ident_d": ident,
        "causal_d": causal, "consts_d": consts, "cneg_d": cneg, "c01_d": c01, "alibi_d": alibi, "krow_d": krow,
        "crow_d": crow, "wsm_d": wsm, "w1k_d": blocks(a["cmp_w1_k"][0], 0, 2048, 0, CMP_HID),
        "w1v_d": blocks(a["cmp_w1_v"][0], 0, 2048, 0, CMP_HID), "w2_d": w2, "bias2_d": bias,
    }


def kernel(**inputs):
    import concourse.bacc as bacc
    from concourse.bass_utils import run_bass_kernel_spmd

    nc = bacc.Bacc("TRN2", target_bir_lowering=False, num_devices=1)
    arrays, args = {}, {}
    for name, x in lay_out(inputs).items():
        arrays[name] = np.ascontiguousarray(x)
        args[name] = nc.dram_tensor(name, x.shape, mybir.dt.from_np(x.dtype), kind="ExternalInput").ap()
    args["out"] = nc.dram_tensor("out", (D, S), F32, kind="ExternalOutput").ap()
    build(nc, **args)
    r = run_bass_kernel_spmd(nc, [arrays], core_ids=[0])
    return np.ascontiguousarray(r.results[0]["out"].T).reshape(1, S, D)
```
